# Optimizing a Trainium2 kernel written in Bass

```python
import math
import numpy as np
import jax
import jax.numpy as jnp
from jax import lax

D_MODEL = 1024
BATCH = 1
SEQ = 512
DEPTH = 2

HEAD_DIM = 64
N_HEADS = D_MODEL // HEAD_DIM
HEADS_PER_MIXER = N_HEADS // 4
GROUP_W = HEADS_PER_MIXER * HEAD_DIM
D_MIX = 4 * GROUP_W
D_FF = 2816
Q_BLOCK = 128
ROPE_THETA = 10000.0
LN_EPS = 1e-5
NORM_EPS = 1e-6
NEG = -1e30
DIFF_QK_DIM = HEAD_DIM // 2
GDN_CONV = 4
GDN_CHUNK = 64
CMP_BLOCK = 32
CMP_STRIDE = 16
CMP_HIDDEN = 256
SLC_BLOCK = 64
SLC_TOPN = 16
WINDOW = 512
FORCE = 1e4
PROJ_SIZES = ((HEADS_PER_MIXER * DIFF_QK_DIM,) * 4 + (GROUP_W,)
              + (GROUP_W,) * 4 + (HEADS_PER_MIXER,) * 2
              + (GROUP_W,) + (HEAD_DIM,) * 6 + (3 * HEADS_PER_MIXER,)
              + (GROUP_W,) * 3)
P_TOTAL = sum(PROJ_SIZES)

kernel_name = 'hybrid_parallel_head_groups_block'

def _layer_norm(x, g, b):
    x32 = x.astype(jnp.float32)
    mu = jnp.mean(x32, axis=-1, keepdims=True)
    var = jnp.mean(jnp.square(x32 - mu), axis=-1, keepdims=True)
    return ((x32 - mu) * lax.rsqrt(var + LN_EPS) * g + b).astype(x.dtype)

def _rms_norm(x, g):
    x32 = x.astype(jnp.float32)
    y = x32 * lax.rsqrt(jnp.mean(jnp.square(x32), axis=-1, keepdims=True) + NORM_EPS) * g
    return y.astype(x.dtype)

def _l2norm(x):
    return x * lax.rsqrt(jnp.sum(x * x, axis=-1, keepdims=True) + NORM_EPS)

def _swiglu(x, w_gu, w_down):
    g, u = jnp.split(x @ w_gu, 2, axis=-1)
    return (jax.nn.silu(g) * u) @ w_down

def _to_heads(t, n):
    B, S, _ = t.shape
    return t.reshape(B, S, n, -1).transpose(0, 2, 1, 3)

def _from_heads(t):
    B, H, S, d = t.shape
    return t.transpose(0, 2, 1, 3).reshape(B, S, H * d)

def _unblock(o):
    n, B, H, Q, d = o.shape
    return o.transpose(1, 2, 0, 3, 4).reshape(B, H, n * Q, d)

def _rope_tables(seq, dim):
    inv = ROPE_THETA ** (-jnp.arange(0, dim, 2, dtype=jnp.float32) / dim)
    ang = jnp.arange(seq, dtype=jnp.float32)[:, None] * inv[None, :]
    return jnp.cos(ang), jnp.sin(ang)

def _rope(t, cs):
    cos, sin = cs[0].astype(t.dtype), cs[1].astype(t.dtype)
    t1, t2 = jnp.split(t, 2, axis=-1)
    return jnp.concatenate([t1 * cos - t2 * sin, t2 * cos + t1 * sin], axis=-1)

def _causal_dwconv(x, w):
    K = w.shape[0]
    return lax.conv_general_dilated(x, w[:, None, :], window_strides=(1,), padding=((K - 1, 0),),
                                    dimension_numbers=('NWC', 'WIO', 'NWC'),
                                    feature_group_count=x.shape[-1])

def diff_attention(q1, q2, k1, k2, v, lam_q1, lam_k1, lam_q2, lam_k2, subln_g, lam_init):
    f32 = jnp.float32
    B, H, S, dq = q1.shape
    scale = dq ** -0.5
    lam = (jnp.exp(jnp.sum(lam_q1.astype(f32) * lam_k1.astype(f32)))
           - jnp.exp(jnp.sum(lam_q2.astype(f32) * lam_k2.astype(f32))) + lam_init)
    kpos = jnp.arange(S)

    def block(i):
        start = i * Q_BLOCK
        qpos = start + jnp.arange(Q_BLOCK)
        causal = kpos[None, :] <= qpos[:, None]

        def probs(q, k):
            qb = lax.dynamic_slice_in_dim(q, start, Q_BLOCK, axis=2)
            s = jnp.einsum('bhqd,bhkd->bhqk', qb, k).astype(f32) * scale
            return jax.nn.softmax(jnp.where(causal, s, NEG), axis=-1)

        w = probs(q1, k1) - lam * probs(q2, k2)
        return jnp.einsum('bhqk,bhkd->bhqd', w.astype(v.dtype), v)

    o = _unblock(lax.map(block, jnp.arange(S // Q_BLOCK)))
    return _from_heads(_rms_norm(o, subln_g) * (1.0 - lam_init))

def gated_delta_net(q, k, v, z, a, b, conv_w, a_log, dt_bias, norm_g):
    f32 = jnp.float32
    B, S, _ = q.shape
    H, d, C = HEADS_PER_MIXER, HEAD_DIM, GDN_CHUNK
    N = S // C
    qkv = jax.nn.silu(_causal_dwconv(jnp.concatenate([q, k, v], axis=-1), conv_w))
    q, k, v = [_to_heads(t, H).astype(f32) for t in jnp.split(qkv, 3, axis=-1)]
    q = _l2norm(q) * d ** -0.5
    k = _l2norm(k)
    beta = jax.nn.sigmoid(b.astype(f32)).transpose(0, 2, 1)
    g = (-jnp.exp(a_log.astype(f32))[None, :, None]
         * jax.nn.softplus(a.astype(f32).transpose(0, 2, 1) + dt_bias.astype(f32)[None, :, None]))

    def chunk(t):
        return t.reshape((B, H, N, C) + t.shape[3:])

    q, k, v, beta, g = chunk(q), chunk(k), chunk(v), chunk(beta), chunk(g)
    G = jnp.cumsum(g, axis=-1)
    tri = jnp.tril(jnp.ones((C, C), bool))
    strict = jnp.tril(jnp.ones((C, C), bool), -1)
    decay = jnp.exp(jnp.where(tri, G[..., :, None] - G[..., None, :], -jnp.inf))
    kb = k * beta[..., None]
    A = jnp.where(strict, jnp.einsum('bhncd,bhnsd->bhncs', kb, k) * decay, 0.0)
    lhs = A + jnp.eye(C, dtype=f32)
    rhs = jnp.concatenate([v * beta[..., None], kb * jnp.exp(G)[..., None]], axis=-1)
    sol = lax.linalg.triangular_solve(lhs, rhs, left_side=True, lower=True, unit_diagonal=True)
    u, w = jnp.split(sol, 2, axis=-1)
    intra = jnp.einsum('bhncd,bhnsd->bhncs', q, k) * decay
    q_dec = q * jnp.exp(G)[..., None]
    k_dec = k * jnp.exp(G[..., -1:] - G)[..., None]
    g_last = jnp.exp(G[..., -1])

    def step(state, inp):
        u_n, w_n, qd_n, kd_n, in_n, gl_n = inp
        v_new = u_n - jnp.einsum('bhcd,bhde->bhce', w_n, state)
        o_n = (jnp.einsum('bhcd,bhde->bhce', qd_n, state)
               + jnp.einsum('bhcs,bhse->bhce', in_n, v_new))
        state = state * gl_n[..., None, None] + jnp.einsum('bhcd,bhce->bhde', kd_n, v_new)
        return state, o_n

    xs = tuple(jnp.moveaxis(t, 2, 0) for t in (u, w, q_dec, k_dec, intra, g_last))
    _, o = lax.scan(step, jnp.zeros((B, H, d, d), f32), xs)
    o = _rms_norm(_unblock(o), norm_g) * jax.nn.silu(_to_heads(z, H).astype(f32))
    return _from_heads(o).astype(z.dtype)

def native_sparse_attention(q, kc, vc, ks, vs, kw, vw, gate, pe_k, pe_v,
                            ck_w1, ck_w2, cv_w1, cv_w2, rope_n):
    f32 = jnp.float32
    B, S, _ = q.shape
    H, d = HEADS_PER_MIXER, HEAD_DIM
    scale = d ** -0.5
    q = _rope(_to_heads(q, H), rope_n)
    kc, ks, kw = _rope(kc, rope_n), _rope(ks, rope_n), _rope(kw, rope_n)
    tpos = jnp.arange(S)

    n_cmp = (S - CMP_BLOCK) // CMP_STRIDE + 1
    cidx = np.arange(n_cmp)[:, None] * CMP_STRIDE + np.arange(CMP_BLOCK)[None, :]

    def compress(t, pe, w1, w2):
        blk = (t[:, cidx, :] + pe).reshape(B, n_cmp, CMP_BLOCK * d)
        return jax.nn.silu(blk @ w1) @ w2

    k_cmp = compress(kc, pe_k, ck_w1, ck_w2)
    v_cmp = compress(vc, pe_v, cv_w1, cv_w2)
    cmask = jnp.asarray(cidx[:, -1])[None, :] <= tpos[:, None]
    s_cmp = jnp.einsum('bhtd,bcd->bhtc', q, k_cmp).astype(f32) * scale
    p_cmp = jax.nn.softmax(jnp.where(cmask, s_cmp, NEG), axis=-1) * cmask
    o_cmp = jnp.einsum('bhtc,bcd->bhtd', p_cmp.astype(v_cmp.dtype), v_cmp)

    n_slc = S // SLC_BLOCK
    sstart = np.arange(n_slc) * SLC_BLOCK
    overlap = (cidx[:, :1] < sstart[None, :] + SLC_BLOCK) & (cidx[:, -1:] >= sstart[None, :])
    imp = jnp.einsum('btc,cj->btj', p_cmp.sum(axis=1), jnp.asarray(overlap, f32))
    blk = jnp.arange(n_slc)[None, :]
    cur = (tpos // SLC_BLOCK)[:, None]
    valid = blk <= cur
    forced = valid & ((blk == 0) | (blk == cur) | (blk == cur - 1))
    imp = jnp.where(forced, FORCE, jnp.where(valid, imp, -FORCE))
    _, sel = lax.top_k(imp, min(SLC_TOPN, n_slc))

    ks_blk = ks.reshape(B, n_slc, SLC_BLOCK, d)
    vs_blk = vs.reshape(B, n_slc, SLC_BLOCK, d)
    kw_pad = jnp.pad(kw, ((0, 0), (WINDOW, 0), (0, 0)))
    vw_pad = jnp.pad(vw, ((0, 0), (WINDOW, 0), (0, 0)))
    gather = jax.vmap(lambda tb, ib: tb[ib])

    def block(i):
        start = i * Q_BLOCK
        qb = lax.dynamic_slice_in_dim(q, start, Q_BLOCK, axis=2)
        qpos = start + jnp.arange(Q_BLOCK)
        sel_b = lax.dynamic_slice_in_dim(sel, start, Q_BLOCK, axis=1)
        kg = gather(ks_blk, sel_b).reshape(B, Q_BLOCK, -1, d)
        vg = gather(vs_blk, sel_b).reshape(B, Q_BLOCK, -1, d)
        kpos = (sel_b[..., None] * SLC_BLOCK + jnp.arange(SLC_BLOCK)).reshape(B, Q_BLOCK, -1)
        smask = (kpos <= qpos[None, :, None])[:, None]
        ss = jnp.einsum('bhqd,bqkd->bhqk', qb, kg).astype(f32) * scale
        ps = jax.nn.softmax(jnp.where(smask, ss, NEG), axis=-1)
        o_s = jnp.einsum('bhqk,bqkd->bhqd', ps.astype(vg.dtype), vg)
        kwin = lax.dynamic_slice_in_dim(kw_pad, start, Q_BLOCK + WINDOW, axis=1)
        vwin = lax.dynamic_slice_in_dim(vw_pad, start, Q_BLOCK + WINDOW, axis=1)
        wpos = start - WINDOW + jnp.arange(Q_BLOCK + WINDOW)
        rel = qpos[:, None] - wpos[None, :]
        wmask = (rel >= 0) & (rel < WINDOW) & (wpos[None, :] >= 0)
        sw = jnp.einsum('bhqd,bkd->bhqk', qb, kwin).astype(f32) * scale
        pw = jax.nn.softmax(jnp.where(wmask, sw, NEG), axis=-1)
        o_w = jnp.einsum('bhqk,bkd->bhqd', pw.astype(vwin.dtype), vwin)
        return o_s, o_w

    o_sel, o_win = lax.map(block, jnp.arange(S // Q_BLOCK))
    o_sel, o_win = _unblock(o_sel), _unblock(o_win)
    gts = jax.nn.sigmoid(gate).reshape(B, S, H, 3).transpose(0, 2, 1, 3)
    o = gts[..., 0:1] * o_cmp + gts[..., 1:2] * o_sel + gts[..., 2:3] * o_win
    return _from_heads(o)

def stick_breaking(q, k, v):
    f32 = jnp.float32
    H = HEADS_PER_MIXER
    q, k, v = _to_heads(q, H), _to_heads(k, H), _to_heads(v, H)
    B, _, S, d = q.shape
    scale = d ** -0.5
    kpos = jnp.arange(S)

    def block(i):
        start = i * Q_BLOCK
        qb = lax.dynamic_slice_in_dim(q, start, Q_BLOCK, axis=2)
        qpos = start + jnp.arange(Q_BLOCK)
        before = kpos[None, :] < qpos[:, None]
        z = jnp.einsum('bhqd,bhkd->bhqk', qb, k).astype(f32) * scale
        log_keep = jnp.where(before, jax.nn.log_sigmoid(-z), 0.0)
        between = lax.cumsum(log_keep, axis=3, reverse=True) - log_keep
        att = jnp.where(before, jnp.exp(jax.nn.log_sigmoid(z) + between), 0.0)
        return jnp.einsum('bhqk,bhkd->bhqd', att.astype(v.dtype), v)

    return _from_heads(_unblock(lax.map(block, jnp.arange(S // Q_BLOCK))))

def hybrid_mixer(x, w_in, w_out, lam_q1, lam_k1, lam_q2, lam_k2, subln_g,
                 conv_w, a_log, dt_bias, gdn_g, pe_k, pe_v, ck_w1, ck_w2, cv_w1, cv_w2,
                 lam_init, rope_d, rope_n):
    H = HEADS_PER_MIXER
    (dq1, dq2, dk1, dk2, dv, gq, gk, gv, gz, ga, gb,
     nq, nkc, nvc, nks, nvs, nkw, nvw, ngate, sq, sk, sv) = jnp.split(
        x @ w_in, np.cumsum(PROJ_SIZES)[:-1].tolist(), axis=-1)
    o_diff = diff_attention(_rope(_to_heads(dq1, H), rope_d), _rope(_to_heads(dq2, H), rope_d),
                            _rope(_to_heads(dk1, H), rope_d), _rope(_to_heads(dk2, H), rope_d),
                            _to_heads(dv, H), lam_q1, lam_k1, lam_q2, lam_k2, subln_g, lam_init)
    o_gdn = gated_delta_net(gq, gk, gv, gz, ga, gb, conv_w, a_log, dt_bias, gdn_g)
    o_nsa = native_sparse_attention(nq, nkc, nvc, nks, nvs, nkw, nvw, ngate, pe_k, pe_v,
                                    ck_w1, ck_w2, cv_w1, cv_w2, rope_n)
    o_sb = stick_breaking(sq, sk, sv)
    return jnp.concatenate([o_diff, o_gdn, o_nsa, o_sb], axis=-1) @ w_out

def setup_inputs(seed: int = 0) -> dict:
    key = jax.random.key(seed)
    ks = iter(jax.random.split(key, 48))
    L, H = DEPTH, HEADS_PER_MIXER
    beta_dn = (8 * DEPTH) ** -0.25

    def nrm(shape, scale):
        return jax.random.normal(next(ks), shape, jnp.float32) * scale

    def gain(shape):
        return 1.0 + nrm(shape, 0.02)

    x = nrm((BATCH, SEQ, D_MODEL), 1.0)
    w_in = nrm((L, D_MODEL, P_TOTAL), D_MODEL ** -0.5)
    w_out = nrm((L, D_MIX, D_MODEL), beta_dn * D_MIX ** -0.5)
    ffn1_w_gu = nrm((L, D_MODEL, 2 * D_FF), D_MODEL ** -0.5)
    ffn1_w_down = nrm((L, D_FF, D_MODEL), beta_dn * D_FF ** -0.5)
    ffn2_w_gu = nrm((L, D_MODEL, 2 * D_FF), D_MODEL ** -0.5)
    ffn2_w_down = nrm((L, D_FF, D_MODEL), beta_dn * D_FF ** -0.5)
    ln1_g, ln1_b = gain((L, D_MODEL)), nrm((L, D_MODEL), 0.02)
    ln2_g, ln2_b = gain((L, D_MODEL)), nrm((L, D_MODEL), 0.02)
    ln3_g, ln3_b = gain((L, D_MODEL)), nrm((L, D_MODEL), 0.02)
    diff_lam_q1 = nrm((L, DIFF_QK_DIM), 0.1)
    diff_lam_k1 = nrm((L, DIFF_QK_DIM), 0.1)
    diff_lam_q2 = nrm((L, DIFF_QK_DIM), 0.1)
    diff_lam_k2 = nrm((L, DIFF_QK_DIM), 0.1)
    diff_subln_g = gain((L, HEAD_DIM))
    gdn_conv_w = nrm((L, GDN_CONV, 3 * GROUP_W), GDN_CONV ** -0.5)
    gdn_a_log = jnp.log(jax.random.uniform(next(ks), (L, H), jnp.float32, 1.0, 16.0))
    dt = jnp.exp(jax.random.uniform(next(ks), (L, H), jnp.float32, math.log(1e-3), math.log(1e-1)))
    gdn_dt_bias = dt + jnp.log(-jnp.expm1(-dt))
    gdn_norm_g = gain((L, HEAD_DIM))
    nsa_pe_k = nrm((L, CMP_BLOCK, HEAD_DIM), 0.02)
    nsa_pe_v = nrm((L, CMP_BLOCK, HEAD_DIM), 0.02)
    nsa_cmp_k_w1 = nrm((L, CMP_BLOCK * HEAD_DIM, CMP_HIDDEN), (CMP_BLOCK * HEAD_DIM) ** -0.5)
    nsa_cmp_k_w2 = nrm((L, CMP_HIDDEN, HEAD_DIM), CMP_HIDDEN ** -0.5)
    nsa_cmp_v_w1 = nrm((L, CMP_BLOCK * HEAD_DIM, CMP_HIDDEN), (CMP_BLOCK * HEAD_DIM) ** -0.5)
    nsa_cmp_v_w2 = nrm((L, CMP_HIDDEN, HEAD_DIM), CMP_HIDDEN ** -0.5)
    return {'x': x, 'w_in': w_in, 'w_out': w_out,
            'ffn1_w_gu': ffn1_w_gu, 'ffn1_w_down': ffn1_w_down,
            'ffn2_w_gu': ffn2_w_gu, 'ffn2_w_down': ffn2_w_down,
            'ln1_g': ln1_g, 'ln1_b': ln1_b, 'ln2_g': ln2_g, 'ln2_b': ln2_b,
            'ln3_g': ln3_g, 'ln3_b': ln3_b,
            'diff_lam_q1': diff_lam_q1, 'diff_lam_k1': diff_lam_k1,
            'diff_lam_q2': diff_lam_q2, 'diff_lam_k2': diff_lam_k2, 'diff_subln_g': diff_subln_g,
            'gdn_conv_w': gdn_conv_w, 'gdn_a_log': gdn_a_log, 'gdn_dt_bias': gdn_dt_bias,
            'gdn_norm_g': gdn_norm_g,
            'nsa_pe_k': nsa_pe_k, 'nsa_pe_v': nsa_pe_v,
            'nsa_cmp_k_w1': nsa_cmp_k_w1, 'nsa_cmp_k_w2': nsa_cmp_k_w2,
            'nsa_cmp_v_w1': nsa_cmp_v_w1, 'nsa_cmp_v_w2': nsa_cmp_v_w2}

def reference(x, w_in, w_out, ffn1_w_gu, ffn1_w_down, ffn2_w_gu, ffn2_w_down,
              ln1_g, ln1_b, ln2_g, ln2_b, ln3_g, ln3_b,
              diff_lam_q1, diff_lam_k1, diff_lam_q2, diff_lam_k2, diff_subln_g,
              gdn_conv_w, gdn_a_log, gdn_dt_bias, gdn_norm_g,
              nsa_pe_k, nsa_pe_v, nsa_cmp_k_w1, nsa_cmp_k_w2, nsa_cmp_v_w1, nsa_cmp_v_w2):
    S = x.shape[1]
    alpha = (2 * DEPTH) ** 0.25
    rope_d = _rope_tables(S, DIFF_QK_DIM)
    rope_n = _rope_tables(S, HEAD_DIM)
    for l in range(DEPTH):
        lam_init = 0.8 - 0.6 * math.exp(-0.3 * l)
        x = _layer_norm(alpha * x + 0.5 * _swiglu(x, ffn1_w_gu[l], ffn1_w_down[l]), ln1_g[l], ln1_b[l])
        mix = hybrid_mixer(x, w_in[l], w_out[l], diff_lam_q1[l], diff_lam_k1[l], diff_lam_q2[l],
                           diff_lam_k2[l], diff_subln_g[l], gdn_conv_w[l], gdn_a_log[l],
                           gdn_dt_bias[l], gdn_norm_g[l], nsa_pe_k[l], nsa_pe_v[l],
                           nsa_cmp_k_w1[l], nsa_cmp_k_w2[l], nsa_cmp_v_w1[l], nsa_cmp_v_w2[l],
                           lam_init, rope_d, rope_n)
        x = _layer_norm(alpha * x + mix, ln2_g[l], ln2_b[l])
        x = _layer_norm(alpha * x + 0.5 * _swiglu(x, ffn2_w_gu[l], ffn2_w_down[l]), ln3_g[l], ln3_b[l])
    return x


_drawn_inputs = setup_inputs


def setup_inputs(seed=0):
    import zlib

    import numpy as np

    out = dict(_drawn_inputs(seed))
    spreads = {}
    factors = {'diff_lam_q1': 7.52,
     'diff_lam_k1': 8.0,
     'diff_lam_q2': 7.946,
     'diff_lam_k2': 6.827,
     'diff_subln_g': 8.0,
     'gdn_norm_g': 28.42,
     'nsa_pe_k': 34.427,
     'nsa_pe_v': 41.278,
     'nsa_cmp_k_w1': 5.194,
     'nsa_cmp_k_w2': 5.151}
    for name, (base, spread) in spreads.items():
        noise = np.random.default_rng([zlib.crc32(name.encode()), seed]).standard_normal(out[name].shape)
        drawn = base * np.exp(spread * noise) if base else spread * noise
        out[name] = jnp.asarray(drawn.astype(out[name].dtype))
    for name, factor in factors.items():
        out[name] = (out[name] * factor).astype(out[name].dtype)
    return out
```

```python
import math
from contextlib import ExitStack

import numpy as np
import concourse.bass as bass
from concourse import mybir

F32 = mybir.dt.float32
BF16 = mybir.dt.bfloat16
ALU = mybir.AluOpType
ACT = mybir.ActivationFunctionType
AX = mybir.AxisListType

P = 128
SEQ, DM, DEPTH, DFF = 512, 1024, 2, 2816
T = SEQ // P
KD = DM // P
FC = DFF // P
H, HD, DQK = 4, 64, 32
CH = 64
NCMP = 31
ALPHA = (2 * DEPTH) ** 0.25
LN_EPS, NORM_EPS, NEG = 1e-5, 1e-6, -1e30

C_DQ1, C_DQ2, C_DK1, C_DK2, C_DV = 0, 128, 256, 384, 512
C_GQ, C_GZ, C_GA, C_GB, C_NQ = 768, 1536, 1792, 1796, 1800
C_NKC, C_NVC, C_NVS, C_NVW, C_GATE = 2056, 2120, 2248, 2376, 2440
C_SQ, C_SK, C_SV, C_END = 2452, 2708, 2964, 3220
GDN_W = 3 * H * HD
TW = 421
HW = C_END - GDN_W

GU_W = 256
GU_LOADS = DFF // GU_W
DOWN_LOADS = [(0, 0, 8), (0, 8, 16), (0, 16, 22), (1, 0, 6), (1, 6, 12), (1, 12, 17), (1, 17, 22)]
PROJ_LOADS = [(768, 1152), (1152, 1536)] + [(C_GZ + TW * g, C_GZ + TW * (g + 1)) for g in range(4)] \
    + [(0, 384), (384, 768)]
RING = 3
SLOT = KD * 2 * GU_W
FFN_LOADS = GU_LOADS + len(DOWN_LOADS)
MIX_LOADS = len(PROJ_LOADS) + 4
LAYER_LOADS = 2 * FFN_LOADS + MIX_LOADS
assert FFN_LOADS % RING == 0 and MIX_LOADS % RING == 0
FIRST_LOAD = (0, FFN_LOADS, FFN_LOADS + MIX_LOADS)

PARAM_DMAS = 14
ACT_STEPS, DVE_STEPS, POOL_STEPS = 35, 202, 15

NSA_U = [("sel", h) if b == 0 else ("win", h) for h in range(H) for b in range(2)]
UNITS = 2 * H + 2 * H
LEVELS = 6
PARAM_ROWS = 24 + 16 + 16


def mixer_items():
    q = [(("par",), "dve")]
    q += [(("proj", m), ("act", "dve")[m % 2]) for m in range(30)]
    q += [(("trn", s), "act") for s in range(6)]
    q += [(("dup", s), "act") for s in range(2)]
    q += [(("hid", s), "act") for s in range(2)] + [(("kcmp",), "dve"), (("vcmp",), "dve"), (("cs",), "dve")]
    q += [(("cpT", i), "act") for i in range(T)] + [(("co", i), "dve") for i in range(T)]
    for n in range(UNITS * T + 2):
        u = n // T
        if n < UNITS * T:
            q.append((("sc", u, n % T), "act"))
            if n % T == 1 and 2 * H <= u + 1 < UNITS:
                q += [(("trq", u + 1), "act"), (("trk", u + 1), "act")]
        if n >= 2:
            v, i = (n - 2) // T, (n - 2) % T
            q.append((("tp", v, i), ("act", "act", "dve", "dve")[i]))
            if i == T - 1:
                q.append((("pv", v), "dve"))
    for m in range(H * T + 2):
        if m < H * T:
            if m % T == 0:
                q += [(("trq", UNITS + m // T), "act"), (("trk", UNITS + m // T), "act")]
            q.append((("z", m // T, T - 1 - m % T), "dve"))
        if m >= 2:
            h, j = (m - 2) // T, T - 1 - (m - 2) % T
            q.append((("c", h, j), "act"))
            if j == 0:
                q.append((("sbo", h), "act"))
    q += [(("gtok", i, f), "act") for i in range(T) for f in range(2)]
    q.append((("G",), "dve"))
    for i in range(T):
        q += [(("kT", i), "act"), (("kbT", i), "dve"), (("qT", i), "act"), (("qdT", i), "act"),
              (("D", i), "act"), (("KK", i), "dve"), (("KQ", i), "dve")]
    for m in range(LEVELS * T + 1):
        if m < LEVELS * T:
            lev, i = divmod(m, T)
            q.append((("X0", i), "dve") if lev == 0 else (("T1", lev, i), "act"))
        if m - 1 >= T:
            lev, i = divmod(m - 1, T)
            if lev < LEVELS - 1:
                q.append((("X", lev, i), "dve"))
            q.append((("XT", lev, i), "dve"))
    for i in range(T):
        q += [(("wT", i), "act"), (("u", i), "act")]
    for n in range(2 * T):
        if n:
            q.append((("ws", n), "dve"))
        if n < 2 * T - 1:
            q.append((("S", n), "dve"))
        if n % 2:
            q.append((("o", n // 2), "act"))
    q += [(("mt", i, f), "act") for i in range(T) for f in range(2)]
    q += [(("wo", f, i), "dve") for f in range(2) for i in range(T)]
    return q


def const_columns():
    widths = [("ident", 128), ("upto", 128), ("chunk", 128), ("negtri", 128), ("negone", 128),
              ("sb01", 128), ("c01", T * 32), ("cneg", T * 32),
              ("cq", T * 32), ("sq", T * 64), ("ck", T * 32), ("sk", T * 64),
              ("dcq", T * 16), ("dsq", T * 32), ("dck", T * 16), ("dsk", T * 32)]
    at, n = {}, 0
    for name, w in widths:
        at[name] = (n, n + w)
        n += w
    return at, n


MASKS = ["ident", "causal", "sbneg", "gdnneg"] + [f"lev{m}" for m in range(LEVELS)]


def constants():
    at, n = const_columns()
    c = np.zeros((P, n), np.float32)

    def put(name, a):
        c[:, at[name][0]:at[name][1]] = np.asarray(a, np.float32).reshape(P, -1)

    r = np.arange(P)[:, None]
    k = np.arange(P)[None, :]
    same = (r // CH) == (k // CH)
    put("ident", r == k)
    put("upto", (r <= k) & same)
    put("chunk", same)
    put("negtri", -(r >= k).astype(np.float32))
    put("negone", -np.ones((P, P)))
    put("sb01", r < k)
    tok = np.arange(T)[None, :, None] * P + np.arange(P)[:, None, None]
    blk = np.arange(32)[None, None, :]
    seen = (blk < NCMP) & (blk * 16 + 31 <= tok)
    put("c01", seen)
    put("cneg", np.where(seen, 0, NEG))

    def rope(dim, scale):
        inv = (np.float32(10000.0) ** (-np.arange(0, dim, 2, dtype=np.float32) / dim)).astype(np.float32)
        ang = tok.astype(np.float32) * inv[None, None, :]
        cos, sin = np.cos(ang) * scale, np.sin(ang) * scale
        return cos, np.stack([-sin, sin], 2)

    for pre, dim in (("", HD), ("d", DQK)):
        for kind, scale in (("q", np.float32(dim ** -0.5)), ("k", np.float32(1))):
            cos, sin = rope(dim, scale)
            put(pre + "c" + kind, cos)
            put(pre + "s" + kind, sin)
    masks = [r == k, np.where(k > r, NEG, 0), np.where(r < k, 0, NEG),
             np.where((k >= r) & same, 0, NEG)]
    for lev in range(LEVELS):
        b = 2 ** lev
        masks.append(-(((k // b) % 2 == 1) & ((r // b) == (k // b) - 1)).astype(np.float32))
    masks = np.stack([np.asarray(m, np.float32) for m in masks], 1).reshape(P, -1)
    lam = np.zeros((DEPTH, 2), np.float32)
    for layer in range(DEPTH):
        init = 0.8 - 0.6 * math.exp(-0.3 * layer)
        lam[layer] = (init, 1 - init)
    return c, masks, lam


class Signal:

    def __init__(self, sem, per_layer, start=0):
        self.sem, self.per_layer, self.start = sem, per_layer, start

    def at(self, layer, n):
        return self.sem, layer * self.per_layer + (n + self.start)


def trunk_program(nc, a, out):
    items = mixer_items()
    number = {key: n for n, (key, _) in enumerate(items)}
    drainer = {key: who for key, who in items}
    rank, seen = {}, {"act": 0, "dve": 0}
    for key, who in items:
        seen[who] += 1
        rank[key] = seen[who]

    ctx = ExitStack()
    with ctx:
        def sb(name, shape, dt=F32):
            return ctx.enter_context(nc.sbuf_tensor(name, shape, dt))

        def sem(name, per_layer, start=0):
            return Signal(ctx.enter_context(nc.semaphore(name)), per_layer, start)

        cat, cw = const_columns()
        consts = sb("consts", [P, cw])
        masks = sb("masks", [P, len(MASKS) * P], BF16)
        x_tok = sb("x_tok", [P, T, DM])
        xT = sb("xT", [P, KD, SEQ])
        ring = sb("ring", [P, RING, SLOT])
        small = sb("small", [P, 640])
        prm = sb("prm", [P, 272])
        w2 = sb("w2", [P, 2, 2, HD])
        stage = sb("stage", [P, P])
        parT = sb("parT", [P, PARAM_ROWS])
        ptmp = sb("ptmp", [P, 2, 256])
        epses = sb("epses", [P, 2])
        lnst = sb("lnst", [P, T, 16])
        ARENA = 24656
        arena = sb("arena", [P, ARENA])
        PS = ctx.enter_context(nc.psum_tensor("banks", [P, 8, 512], F32))

        def const(name):
            return consts[:, cat[name][0]:cat[name][1]]

        def mask(name):
            n = MASKS.index(name)
            return masks[:, n * P:(n + 1) * P]

        ident, identb = const("ident"), mask("ident")

        used = [0]

        def cols(n):
            used[0] += n
            assert used[0] <= 640
            return small[:, used[0] - n:used[0]]

        nmax, rsum = cols(64), cols(64)
        rinv = cols(16)
        cmx = cols(16)
        gate = cols(T * 12)
        ab_x, ab_abs, ab_e, ab_ln = cols(16), cols(16), cols(16), cols(16)
        ea = cols(4)
        beta, gdec = cols(16), cols(16)
        gcol = cols(64)
        negG = cols(16)
        expG, expKd, gl, betaG = cols(16), cols(16), cols(32), cols(16)
        lamdot, lamexp, neglam = cols(2), cols(2), cols(1)
        ssq = cols(32)
        rstd = cols(32)

        hT = arena[:, 0:FC * SEQ].rearrange("p (f t) -> p f t", f=FC)
        sil = arena[:, FC * SEQ:FC * SEQ + 2 * SEQ].rearrange("p (b t) -> p b t", b=2)
        lnp = arena[:, 14336:14336 + 2 * DM].rearrange("p (b c) -> p b c", b=2)
        off = {}

        def area(name, start, n):
            off[name] = start + n
            return arena[:, start:start + n]

        mix = area("mix", 0, T * DM).rearrange("p (t c) -> p t c", t=T)
        h_tok = area("h", off["mix"], T * HW).rearrange("p (t c) -> p t c", t=T)
        nsaT = area("nsaT", off["h"], 6 * SEQ).rearrange("p (s t) -> p s t", s=6)
        pair0 = off["nsaT"]
        pairT = area("pairT", pair0, 4 * SEQ).rearrange("p (s t) -> p s t", s=4)
        prob = area("prob", off["pairT"], 3 * SEQ).rearrange("p (s t) -> p s t", s=3)
        raw = arena[:, pair0:pair0 + 6 * 515].rearrange("p (j t) -> p j t", j=6)
        conv = area("conv", off["prob"], 6 * SEQ).rearrange("p (j t) -> p j t", j=6)
        siluz = area("siluz", off["conv"], T * 256).rearrange("p (t c) -> p t c", t=T)
        assert off["siluz"] <= ARENA
        scratch = xT[:, :, :].rearrange("p k t -> p (k t)")
        dupT = scratch[:, 0:1024].rearrange("p (s t) -> p s t", s=2)
        blk = scratch[:, 1024:1024 + 992].rearrange("p (s j c) -> p s j c", s=2, j=16)
        cpTs = scratch[:, 2048:4096].rearrange("p (t c) -> p t c", t=T)
        csb = prob[:, 0, :].rearrange("p (n c) -> p n c", c=32)
        hid = pairT[:, 3, 0:128].rearrange("p (s f c) -> p s f c", s=2, f=2)
        kcmpT = pairT[:, 3, 128:160]
        vcmp = pairT[:, 3, 160:224]
        dup = pairT[:, 0:2, :].rearrange("p s (t c) -> p s t c", c=P)
        probT = scratch[:, 0:2560].rearrange("p (b n q) -> p b n q", b=2, n=10)
        tmpo = scratch[:, 2560:2560 + 256].rearrange("p (t c) -> p t c", t=T)
        tmpl = scratch[:, 2816:2816 + 1024].rearrange("p (t c) -> p t c", t=T)
        soft = probT.rearrange("p b n q -> p b (n q)")
        attT = arena[:, off["h"]:off["h"] + 2560].rearrange("p (b c) -> p b c", b=2)
        g0 = off["mix"]

        def garea(n):
            nonlocal g0
            g0 += n
            return arena[:, g0 - n:g0]

        states = arena[:, g0:g0 + 2048].rearrange("p (n c) -> p n c", n=8)
        qtok = garea(1024).rearrange("p (t c) -> p t c", t=T)
        ktok = garea(1024).rearrange("p (t c) -> p t c", t=T)
        vtok = garea(1024).rearrange("p (t c) -> p t c", t=T)
        kb = garea(1024).rearrange("p (t c) -> p t c", t=T)
        u_new = kb
        kbG = garea(1024).rearrange("p (t c) -> p t c", t=T)
        qd = garea(1024).rearrange("p (t c) -> p t c", t=T)
        kd = garea(1024).rearrange("p (t c) -> p t c", t=T)
        kTb, kbTb, qTb = garea(512), garea(512), garea(512)
        sg = kTb[:, 0:256]
        qdT = garea(2048).rearrange("p (t c) -> p t c", t=T)
        intraT = garea(2048).rearrange("p (t c) -> p t c", t=T)
        wT = garea(2048).rearrange("p (t c) -> p t c", t=T)
        Dm = garea(512)
        T1 = garea(1024).rearrange("p (b c) -> p b c", b=2)
        NL = garea(1024).rearrange("p (b c) -> p b c", b=2)
        X = garea(2048).rearrange("p (t c) -> p t c", t=T)
        assert g0 <= off["conv"]
        XT = scratch[:, 0:2048].rearrange("p (t c) -> p t c", t=T)
        AT = scratch[:, 2048:4096].rearrange("p (t c) -> p t c", t=T)

        consts_loaded = sem("consts_loaded", 0)
        x_loaded = sem("x_loaded", 0)
        slot_loaded = [sem(f"slot{s}_loaded", 32 * LAYER_LOADS // RING) for s in range(RING)]
        lnp_loaded = sem("lnp_loaded", 3 * 32)
        params_loaded = sem("params_loaded", PARAM_DMAS * 16)
        out_stored = sem("out_stored", 0)
        down_used = sem("down_used", 10, 10)
        ln_turned = sem("ln_turned", 3 * 8)
        gu_ready = sem("gu_ready", 2 * FC)
        down_ready = sem("down_ready", 2 * 8, 2 * 8)
        bank_filled = sem("bank_filled", len(items))
        act_done = sem("act_done", ACT_STEPS)
        xT_ready = sem("xT_ready", 3 * 8)
        silu_ready = sem("silu_ready", 2 * FC)
        ln_std = sem("ln_std", 3 * T)
        drained_act = sem("drained_act", seen["act"])
        conv_silu = sem("conv_silu", 1)
        gates_exp = sem("gates_exp", 1)
        cmp_exp = sem("cmp_exp", 1)
        soft_ln = sem("soft_ln", H * T)
        norm_std = sem("norm_std", 3)
        decays_exp = sem("decays_exp", 1)
        dve_done = sem("dve_done", DVE_STEPS)
        consts_cast = sem("consts_cast", 0)
        x_ready = sem("x_ready", 3 * T, T)
        h_ready = sem("h_ready", 2 * FC, 2)
        ln_var = sem("ln_var", 3 * T)
        drained_dve = sem("drained_dve", seen["dve"])
        conv_done = sem("conv_done", 6)
        gates_in = sem("gates_in", 1)
        nsa_rotated = sem("nsa_rotated", 1)
        blocks_ready = sem("blocks_ready", 2)
        cmp_shifted = sem("cmp_shifted", 1)
        cmp_probs = sem("cmp_probs", 1)
        row_max = sem("row_max", UNITS * T)
        soft_ready = sem("soft_ready", H * T)
        norm_sum = sem("norm_sum", 3)
        dup_ready = sem("dup_ready", 1)
        gates_ready = sem("gates_ready", 1)
        decays_in = sem("decays_in", 1)
        gdn_ready = sem("gdn_ready", 1)
        xt0_ready = sem("xt0_ready", T)
        states_clear = sem("states_clear", 1)
        mix_ready = sem("mix_ready", 2)
        waits_taken = sem("waits_taken", 0)
        diff_rotated = sem("diff_rotated", 1)
        pool_done = sem("pool_done", POOL_STEPS)
        level_ready = sem("level_ready", LEVELS * T)

        def filled(layer, key):
            return bank_filled.at(layer, number[key] + 1)

        def drained(layer, key):
            s = drained_act if drainer[key] == "act" else drained_dve
            return s.at(layer, rank[key])

        def bank(key):
            return PS[:, number[key] % 8, :]

        block = ctx.enter_context(nc.Block())

        def slot_at(n):
            return ring[:, n % RING, :]

        def load_arrived(layer, n):
            return slot_loaded[n % RING].at(layer, 32 * (n // RING + 1))

        def down_col(w, idx):
            return 5 * w + (idx + 1 if idx < 2 else idx)

        @block.sync
        def _(sp):
            sp.dma_start(consts[:, :], a["consts"]).then_inc(consts_loaded.sem, 16)
            sp.dma_start(arena[:, 0:len(MASKS) * P], a["masks"]).then_inc(consts_loaded.sem, 16)
            sp.dma_start(x_tok[:, :, :], a["x"].rearrange("b (t p) d -> p (b t) d", p=P)).then_inc(x_loaded.sem, 16)

            def wait_slot_free(l, n):
                o = n - RING
                if o < 0:
                    l, o = l - 1, o + LAYER_LOADS
                if FIRST_LOAD[1] <= o < FIRST_LOAD[2]:
                    m = o - FIRST_LOAD[1]
                    last = [("proj", 2), ("proj", 5)] + [("proj", 9 + 4 * g) for g in range(6)] \
                        + [("hid", 0), ("hid", 1), ("wo", 0, T - 1), ("wo", 1, T - 1)]
                    sp.wait_ge(*filled(l, last[m]))
                    sp.sem_inc(waits_taken.sem, 1)
                    return
                w = int(o >= FIRST_LOAD[2])
                idx = o - FIRST_LOAD[2 * w] - GU_LOADS
                if idx < 0:
                    sp.wait_ge(*gu_ready.at(l, w * FC + 2 * (idx + GU_LOADS) + 2))
                elif idx in (2, 6):
                    sp.wait_ge(*down_ready.at(l, 8 * w + 4 * (idx // 4) + 4))
                else:
                    sp.wait_ge(*down_used.at(l, down_col(w, idx)))

            def load_gate_up(l, w, g, s):
                gu = a["gu"][w][l].rearrange("(k p) c -> p k c", p=P)
                dst = ring[:, s, :].rearrange("p (k c) -> p k c", k=KD)
                for half in range(2):
                    sp.dma_start(dst[:, :, half * GU_W:(half + 1) * GU_W],
                                 gu[:, :, bass.ds(g * GU_W + half * DFF, GU_W)]).then_inc(slot_loaded[s].sem, 16)

            def ffn_loads(l, w):
                first = FIRST_LOAD[2 * w]
                for g in range(RING):
                    wait_slot_free(l, first + g)
                    load_gate_up(l, w, g, g)
                with sp.Fori(0, 2) as it:
                    for s in range(RING):
                        sp.wait_ge(*gu_ready.at(l, w * FC + 2 * s + 2 + it * (2 * RING)))
                        load_gate_up(l, w, it * RING + (RING + s), s)
                for g in range(3 * RING, GU_LOADS):
                    wait_slot_free(l, first + g)
                    load_gate_up(l, w, g, g % RING)
                for idx, (half, f0, f1) in enumerate(DOWN_LOADS):
                    n = first + GU_LOADS + idx
                    wait_slot_free(l, n)
                    dst = ring[:, n % RING, 0:(f1 - f0) * 512].rearrange("p (f c) -> p f c", c=512)
                    src = a["down"][w][l].rearrange("(f p) c -> p f c", p=P)[:, f0:f1, half * 512:half * 512 + 512]
                    sp.dma_start(dst, src).then_inc(slot_loaded[n % RING].sem, 32)

            def mixer_loads(l):
                n = FIRST_LOAD[1]
                for c0, c1 in PROJ_LOADS:
                    wait_slot_free(l, n)
                    dst = ring[:, n % RING, 0:KD * (c1 - c0)].rearrange("p (k c) -> p k c", k=KD)
                    sp.dma_start(dst, a["w_in"][l].rearrange("(k p) c -> p k c", p=P)[:, :, c0:c1]) \
                        .then_inc(slot_loaded[n % RING].sem, 32)
                    n += 1
                for w1 in (a["cmp_k_w1"], a["cmp_v_w1"]):
                    wait_slot_free(l, n)
                    sp.dma_start(ring[:, n % RING, :].rearrange("p (k c) -> p k c", k=16),
                                 w1[l].rearrange("(k p) c -> p k c", p=P)).then_inc(slot_loaded[n % RING].sem, 32)
                    n += 1
                for half in range(2):
                    wait_slot_free(l, n)
                    sp.dma_start(ring[:, n % RING, :].rearrange("p (k c) -> p k c", k=KD),
                                 a["w_out"][l].rearrange("(k p) c -> p k c", p=P)[:, :, half * 512:half * 512 + 512]) \
                        .then_inc(slot_loaded[n % RING].sem, 32)
                    n += 1

            with sp.Fori(0, DEPTH) as l:
                ffn_loads(l, 0)
                mixer_loads(l)
                ffn_loads(l, 1)
            for i in range(T):
                sp.wait_ge(*x_ready.at(DEPTH - 1, 2 * T + i + 1))
                sp.dma_start(out.rearrange("b (t p) d -> p (b t) d", p=P)[:, i, :], x_tok[:, i, :]) \
                    .then_inc(out_stored.sem, 16)
            sp.wait_ge(out_stored.sem, 16 * T)

        @block.tensor
        def _(pe):
            mm, tr = nc.tensor.matmul, nc.tensor.transpose
            pe.sem_inc(down_used.sem, down_used.start)
            pe.sem_inc(down_ready.sem, down_ready.start)
            pe.wait_ge(consts_loaded.sem, 32)
            pe.wait_ge(consts_cast.sem, 1)

            def turn_x(l, j):
                for i in range(T):
                    pe.wait_ge(*x_ready.at(l, T * (j - 1) + i + 1))
                    for f in range(2):
                        e = 2 * i + f
                        if e >= 4:
                            pe.wait_ge(*xT_ready.at(l, 8 * j + e - 3))
                        for c in range(4):
                            k = 4 * f + c
                            ins = tr(PS[:, 4 + e % 4, c * P:(c + 1) * P], x_tok[:, i, k * P:(k + 1) * P], ident)
                        ins.then_inc(ln_turned.sem, 1)
                pe.wait_ge(*xT_ready.at(l, 8 * j + 8))
                pe.sem_inc(waits_taken.sem, 1)

            def ffn(l, w):
                turn_x(l, 2 * w)
                first = FIRST_LOAD[2 * w]

                def gate_up(f, par, s, sub, arrived):
                    if sub == 0:
                        pe.wait_ge(*arrived)
                    pe.wait_ge(*h_ready.at(l, w * FC - 1 + f))
                    wv = ring[:, s, :].rearrange("p (k c) -> p k c", k=KD)
                    for kind in range(2):
                        for k in range(KD):
                            c0 = kind * GU_W + sub * P
                            ins = mm(PS[:, 2 * kind + par, :], lhsT=wv[:, k, c0:c0 + P], rhs=xT[:, k, :],
                                     start=k == 0, stop=k == KD - 1)
                    ins.then_inc(gu_ready.sem, 1)

                with pe.Fori(0, 3) as it:
                    for s in range(RING):
                        for sub in range(2):
                            gate_up(it * (2 * RING) + (2 * s + sub), sub, s, sub,
                                    slot_loaded[s].at(l, it * 32 + 32 * (first // RING + 1)))
                for f in range(6 * RING, FC):
                    n = first + f // 2
                    gate_up(f, f % 2, n % RING, f % 2, load_arrived(l, n))
                for idx, (half, f0, f1) in enumerate(DOWN_LOADS):
                    n = first + GU_LOADS + idx
                    wv = slot_at(n).rearrange("p (f c) -> p f c", c=512)
                    pe.wait_ge(*load_arrived(l, n))
                    if half == 0:
                        pe.wait_ge(*h_ready.at(l, w * FC + f1))
                    for i in range(T):
                        b = i if half else 4 + i
                        for f in range(f0, f1):
                            ins = mm(PS[:, b, :], lhsT=hT[:, f, i * P:(i + 1) * P], rhs=wv[:, f - f0, :],
                                     start=f == 0, stop=f == FC - 1)
                        if f1 == FC:
                            ins.then_inc(down_ready.sem, 1)
                    if f1 != FC:
                        ins.then_inc(down_used.sem, 1)

            def mixer(l):
                turn_x(l, 1)
                nxt = [0]

                def fill(*key, narrow=False):
                    q = number[key]
                    assert q == nxt[0], (key, items[nxt[0]])
                    nxt[0] += 1
                    if narrow:
                        pe.sem_inc(waits_taken.sem, 1)
                    if q >= 8:
                        pe.wait_ge(*drained(l, items[q - 8][0]))
                    if narrow:
                        pe.sem_inc(waits_taken.sem, 1)
                    return PS[:, q % 8, :]

                def done(ins):
                    ins.then_inc(bank_filled.sem, 1)

                pe.wait_ge(*params_loaded.at(l, 16 * PARAM_DMAS))
                b = fill("par", narrow=True)
                done(tr(b[:, 0:PARAM_ROWS], stage[0:PARAM_ROWS, :], ident[0:PARAM_ROWS, 0:PARAM_ROWS]))
                for m in range(30):
                    g = m // 3 if m < 6 else 2 + (m - 6) // 4
                    n = FIRST_LOAD[1] + g
                    w = PROJ_LOADS[g][1] - PROJ_LOADS[g][0]
                    wv = slot_at(n)[:, 0:KD * w].rearrange("p (k c) -> p k c", k=KD)
                    if (m < 6 and m % 3 == 0) or (m >= 6 and (m - 6) % 4 == 0):
                        pe.wait_ge(*load_arrived(l, n))
                    b = fill("proj", m)
                    for k in range(KD):
                        if m < 6:
                            c = m % 3
                            ins = mm(b, lhsT=wv[:, k, c * P:(c + 1) * P], rhs=xT[:, k, :],
                                     start=k == 0, stop=k == KD - 1)
                        else:
                            i = (m - 6) % 4
                            ins = mm(b[:, 0:w], lhsT=xT[:, k, i * P:(i + 1) * P], rhs=wv[:, k, :],
                                     start=k == 0, stop=k == KD - 1)
                    done(ins)

                def turn_heads(b, src, width):
                    for i in range(T):
                        ins = tr(b[0:width, i * P:(i + 1) * P], src(i), ident)
                    return ins

                pe.wait_ge(*nsa_rotated.at(l, 1))
                for s in range(6):
                    c = (C_NQ + HD * s if s < 4 else C_NKC + 128 * (s - 3)) - GDN_W
                    b = fill("trn", s, narrow=True)
                    done(turn_heads(b, lambda i: h_tok[:, i, c:c + HD], HD))
                pe.wait_ge(*dup_ready.at(l, 1))
                for s in range(2):
                    b = fill("dup", s)
                    done(turn_heads(b, lambda i: dup[:, s, i, :], P))
                for s in range(2):
                    n = FIRST_LOAD[1] + len(PROJ_LOADS) + s
                    pe.wait_ge(*load_arrived(l, n))
                    pe.wait_ge(*blocks_ready.at(l, s + 1))
                    b = fill("hid", s)
                    wv = slot_at(n).rearrange("p (k c) -> p k c", k=16)
                    for f in range(2):
                        for k in range(16):
                            ins = mm(b[:, f * 32:f * 32 + NCMP], lhsT=wv[:, k, f * P:(f + 1) * P],
                                     rhs=blk[:, s, k, :], start=k == 0, stop=k == 15)
                    done(ins)
                pe.wait_ge(*drained(l, ("hid", 1)))
                b = fill("kcmp", narrow=True)
                for f in range(2):
                    ins = mm(b[0:HD, 0:NCMP], lhsT=w2[:, 0, f, :], rhs=hid[:, 0, f, 0:NCMP], start=f == 0, stop=f == 1)
                done(ins)
                b = fill("vcmp", narrow=True)
                for f in range(2):
                    ins = mm(b[0:NCMP, 0:HD], lhsT=hid[:, 1, f, 0:NCMP], rhs=w2[:, 1, f, :], start=f == 0, stop=f == 1)
                done(ins)
                pe.wait_ge(*drained(l, ("kcmp",)))
                b = fill("cs")
                for i in range(T):
                    for h in range(H):
                        c = (i * H + h) * 32
                        ins = mm(b[:, c:c + NCMP], lhsT=nsaT[0:HD, h, i * P:(i + 1) * P],
                                 rhs=kcmpT[0:HD, 0:NCMP], start=True, stop=True)
                done(ins)
                pe.wait_ge(*cmp_probs.at(l, 1))
                for i in range(T):
                    b = fill("cpT", i, narrow=True)
                    for h in range(H):
                        ins = tr(b[0:NCMP, h * P:(h + 1) * P], csb[:, i * H + h, 0:NCMP], ident)
                    done(ins)
                for i in range(T):
                    pe.wait_ge(*drained(l, ("cpT", i)))
                    b = fill("co", i)
                    for h in range(H):
                        ins = mm(b[:, h * HD:(h + 1) * HD], lhsT=cpTs[0:NCMP, i, h * P:(h + 1) * P],
                                 rhs=vcmp[0:NCMP, :], start=True, stop=True)
                    done(ins)

                def v_col(u):
                    if u < 2 * H:
                        return (C_NVS, C_NVW)[u % 2] - GDN_W
                    return C_DV + (u - 2 * H) // 2 * HD

                def turn_pair(u):
                    if u < UNITS:
                        h, br = divmod(u - 2 * H, 2)
                        cq, ck, w = (C_DQ1, C_DQ2)[br] + DQK * h, (C_DK1, C_DK2)[br] + DQK * h, DQK
                        s = 2 * (u % 2)
                    else:
                        h = u - UNITS
                        cq, ck, w = C_SQ + HD * h - GDN_W, C_SK + HD * h - GDN_W, HD
                    for name, c in (("trq", cq), ("trk", ck)):
                        b = fill(name, u, narrow=True)
                        done(turn_heads(b, lambda i: h_tok[:, i, c:c + w], w))

                def scores(u, i):
                    w = (i + 1) * P
                    if u < 2 * H:
                        h, br = divmod(u, 2)
                        qT, kT = nsaT[0:HD, h, :], nsaT[0:HD, 4 + br, :]
                    else:
                        s = 2 * (u % 2)
                        qT, kT = pairT[0:DQK, s, :], pairT[0:DQK, s + 1, :]
                        if i == 0:
                            pe.wait_ge(*drained(l, ("trk", u)))
                    b = fill("sc", u, i)
                    mm(b[:, 0:w], lhsT=qT[:, i * P:w], rhs=kT[:, 0:w], start=True, stop=False)
                    done(mm(b[:, i * P:w], lhsT=identb, rhs=mask("causal"), start=False, stop=True))

                def turn_probs(u, i):
                    pe.wait_ge(*drained(l, ("sc", u, i)))
                    b = fill("tp", u, i)
                    for k in range(i + 1):
                        ins = tr(b[:, k * P:(k + 1) * P], prob[:, (T * u + i) % 3, k * P:(k + 1) * P], ident)
                    done(ins)

                def attend(u):
                    pe.wait_ge(*drained(l, ("tp", u, 1)))
                    pe.wait_ge(*drained(l, ("tp", u, 3)))
                    b = fill("pv", u)
                    c = v_col(u)
                    for i in range(T):
                        for k in range(i + 1):
                            ins = mm(b[:, i * HD:(i + 1) * HD], lhsT=probT[:, u % 2, i * (i + 1) // 2 + k, :],
                                     rhs=h_tok[:, k, c:c + HD], start=k == 0, stop=k == i)
                    done(ins)

                for n in range(UNITS * T + 2):
                    u = n // T
                    if n < UNITS * T:
                        scores(u, n % T)
                        if n % T == 1 and 2 * H <= u + 1 < UNITS:
                            if u + 1 == 2 * H:
                                pe.wait_ge(*diff_rotated.at(l, 1))
                            turn_pair(u + 1)
                    if n >= 2:
                        turn_probs(*divmod(n - 2, T))
                        if (n - 2) % T == T - 1:
                            attend((n - 2) // T)

                first = [0, 512, 896, 1152]

                def log_odds(b, h, j, stop):
                    s = 2 * (h % 2)
                    w = SEQ - j * P
                    return mm(b[:, 0:w], lhsT=pairT[0:HD, s + 1, j * P:(j + 1) * P], rhs=pairT[0:HD, s, j * P:SEQ],
                              start=True, stop=stop)

                for m in range(H * T + 2):
                    if m < H * T:
                        h, j = m // T, T - 1 - m % T
                        if m % T == 0:
                            turn_pair(UNITS + h)
                            pe.wait_ge(*drained(l, ("trk", UNITS + h)))
                        b = fill("z", h, j)
                        done(log_odds(b, h, j, True))
                    if m >= 2:
                        h, j = (m - 2) // T, T - 1 - (m - 2) % T
                        w = SEQ - j * P
                        pe.wait_ge(*soft_ready.at(l, m - 1))
                        b = fill("c", h, j)
                        log_odds(b, h, j, False)
                        mm(b[:, 0:w], lhsT=const("negtri"), rhs=soft[:, h % 2, first[j]:first[j] + w],
                           start=False, stop=False)
                        for k in range(j + 1, T):
                            mm(b[:, (k - j) * P:w], lhsT=const("negone"),
                               rhs=soft[:, h % 2, first[k]:first[k] + SEQ - k * P], start=False, stop=False)
                        done(mm(b[:, 0:P], lhsT=identb, rhs=mask("sbneg"), start=False, stop=True))
                        if j == 0:
                            pe.wait_ge(*drained(l, ("c", h, 0)))
                            b = fill("sbo", h)
                            for i in range(T):
                                for k in range(i + 1):
                                    c = first[k] + (i - k) * P
                                    cv = C_SV + HD * h - GDN_W
                                    ins = mm(b[:, i * HD:(i + 1) * HD], lhsT=attT[:, h % 2, c:c + P],
                                             rhs=h_tok[:, k, cv:cv + HD], start=k == 0, stop=k == i)
                            done(ins)

                pe.wait_ge(*conv_silu.at(l, 1))
                for i in range(T):
                    for f in range(2):
                        b = fill("gtok", i, f)
                        for c in range(3):
                            ins = tr(b[:, c * P:(c + 1) * P], conv[:, 3 * f + c, i * P:(i + 1) * P], ident)
                        done(ins)
                pe.wait_ge(*gates_ready.at(l, 1))
                b = fill("G", narrow=True)
                mm(b[:, 0:16], lhsT=const("upto"), rhs=gdec, start=True, stop=True)
                mm(b[:, 16:32], lhsT=const("chunk"), rhs=gdec, start=True, stop=True)
                mm(b[0:64, 32:48], lhsT=const("chunk")[:, 0:64], rhs=gdec, start=True, stop=True)
                done(mm(b[0:64, 48:64], lhsT=const("chunk")[:, 64:128], rhs=gdec, start=True, stop=True))
                pe.wait_ge(*gdn_ready.at(l, 1))
                for i in range(T):
                    for name, src in (("kT", ktok), ("kbT", kb), ("qT", qtok), ("qdT", qd)):
                        b = fill(name, i, narrow=True)
                        for h in range(H):
                            ins = tr(b[0:HD, h * P:(h + 1) * P], src[:, i, h * HD:(h + 1) * HD], ident)
                        done(ins)
                    b = fill("D", i)
                    for h in range(H):
                        n = i * H + h
                        mm(b[:, h * P:(h + 1) * P], lhsT=gdec[:, n:n + 1].to_broadcast([P, P]), rhs=const("upto"),
                           start=True, stop=False)
                        ins = mm(b[:, h * P:(h + 1) * P], lhsT=identb, rhs=mask("gdnneg"), start=False, stop=True)
                    done(ins)
                    for name, other, need in (("KK", kbTb, "kbT"), ("KQ", qTb, "qT")):
                        pe.wait_ge(*drained(l, (need, i)))
                        pe.wait_ge(*drained(l, ("kT", i)))
                        b = fill(name, i)
                        for h in range(H):
                            ins = mm(b[:, h * P:(h + 1) * P], lhsT=kTb[0:HD, h * P:(h + 1) * P],
                                     rhs=other[0:HD, h * P:(h + 1) * P], start=True, stop=True)
                        done(ins)

                def heads(b, lhs, rhs):
                    for h in range(H):
                        s = slice(h * P, (h + 1) * P)
                        ins = mm(b[:, s], lhsT=lhs[:, s], rhs=rhs(h), start=True, stop=True)
                    return ins

                for m in range(LEVELS * T + 1):
                    if m < LEVELS * T:
                        lev, i = divmod(m, T)
                        pe.wait_ge(*level_ready.at(l, m + 1))
                        if lev == 0:
                            b = fill("X0", i)
                            done(heads(b, NL[:, m % 2, :], lambda h: ident))
                        else:
                            pe.wait_ge(*drained(l, ("X0", i) if lev == 1 else ("X", lev - 1, i)))
                            b = fill("T1", lev, i)
                            done(heads(b, NL[:, m % 2, :], lambda h: X[:, i, h * P:(h + 1) * P]))
                    if m - 1 >= T:
                        lev, i = divmod(m - 1, T)
                        t1 = T1[:, (m - 1) % 2, :]
                        pe.wait_ge(*(xt0_ready.at(l, i + 1) if lev == 1 else drained(l, ("XT", lev - 1, i))))
                        pe.wait_ge(*drained(l, ("T1", lev, i)))
                        if lev < LEVELS - 1:
                            b = fill("X", lev, i)
                            done(heads(b, XT[:, i, :], lambda h: t1[:, h * P:(h + 1) * P]))
                        b = fill("XT", lev, i)
                        done(heads(b, t1, lambda h: XT[:, i, h * P:(h + 1) * P]))
                for i in range(T):
                    pe.wait_ge(*drained(l, ("XT", LEVELS - 1, i)))
                    b = fill("wT", i, narrow=True)
                    for h in range(H):
                        ins = mm(b[0:HD, h * P:(h + 1) * P], lhsT=kbG[:, i, h * HD:(h + 1) * HD],
                                 rhs=XT[:, i, h * P:(h + 1) * P], start=True, stop=True)
                    done(ins)
                    b = fill("u", i)
                    for h in range(H):
                        ins = mm(b[:, h * HD:(h + 1) * HD], lhsT=XT[:, i, h * P:(h + 1) * P],
                                 rhs=vtok[:, i, h * HD:(h + 1) * HD], start=True, stop=True)
                    done(ins)
                pe.wait_ge(*drained(l, ("u", T - 1)))
                for n in range(2 * T):
                    i, p = divmod(n, 2)
                    rows = slice(p * CH, (p + 1) * CH)
                    if n:
                        pe.wait_ge(*drained(l, ("S", n - 1)))
                        b = fill("ws", n, narrow=True)
                        for h in range(H):
                            c = h * P + p * CH
                            ins = mm(b[rows, h * HD:(h + 1) * HD], lhsT=wT[0:HD, i, c:c + CH],
                                     rhs=states[0:HD, n, h * HD:(h + 1) * HD], start=True, stop=True)
                        done(ins)
                        pe.wait_ge(*drained(l, ("ws", n)))
                    if n < 2 * T - 1:
                        b = fill("S", n, narrow=True)
                        for h in range(H):
                            ins = mm(b[0:HD, h * HD:(h + 1) * HD], lhsT=kd[rows, i, h * HD:(h + 1) * HD],
                                     rhs=u_new[rows, i, h * HD:(h + 1) * HD], start=True, stop=True)
                        done(ins)
                    if p:
                        if n == 1:
                            pe.wait_ge(*states_clear.at(l, 1))
                        b = fill("o", i, narrow=True)
                        for h in range(H):
                            s = slice(h * HD, (h + 1) * HD)
                            for par in range(2):
                                c = h * P + par * CH
                                mm(b[par * CH:(par + 1) * CH, s], lhsT=qdT[0:HD, i, c:c + CH],
                                   rhs=states[0:HD, 2 * i + par, s], start=h == 0, stop=False, skip_group_check=True)
                            ins = mm(b[:, s], lhsT=intraT[:, i, h * P:(h + 1) * P], rhs=u_new[:, i, s],
                                     start=False, stop=h == H - 1, skip_group_check=True)
                        done(ins)
                pe.wait_ge(*mix_ready.at(l, 2))
                for i in range(T):
                    for f in range(2):
                        b = fill("mt", i, f)
                        for c in range(4):
                            k = 4 * f + c
                            ins = tr(b[:, c * P:(c + 1) * P], mix[:, i, k * P:(k + 1) * P], ident)
                        done(ins)
                pe.wait_ge(*drained(l, ("mt", T - 1, 1)))
                for f in range(2):
                    n = FIRST_LOAD[1] + len(PROJ_LOADS) + 2 + f
                    pe.wait_ge(*load_arrived(l, n))
                    wv = slot_at(n).rearrange("p (k c) -> p k c", k=KD)
                    for i in range(T):
                        b = fill("wo", f, i)
                        for k in range(KD):
                            ins = mm(b, lhsT=xT[:, k, i * P:(i + 1) * P], rhs=wv[:, k, :],
                                     start=k == 0, stop=k == KD - 1)
                        done(ins)
                assert nxt[0] == len(items)

            with pe.Fori(0, DEPTH) as l:
                ffn(l, 0)
                mixer(l)
                ffn(l, 1)

        @block.scalar
        def _(act):
            f_ = nc.scalar.activation
            steps = [0]
            act.wait_ge(consts_cast.sem, 1)

            def turn_x(l, j):
                for i in range(T):
                    for f in range(2):
                        e = 2 * i + f
                        act.wait_ge(*ln_turned.at(l, 8 * j + e + 1))
                        nc.scalar.copy(xT[:, 4 * f:4 * f + 4, i * P:(i + 1) * P],
                                       PS[:, 4 + e % 4, :].rearrange("p (k t) -> p k t", k=4)).then_inc(xT_ready.sem, 1)

            def norm_stds(l, j):
                for i in range(T):
                    act.wait_ge(*ln_var.at(l, T * j + i + 1))
                    f_(lnst[:, i, 14:15], lnst[:, i, 13:14], ACT.Sqrt, bias=epses[:, 0:1]).then_inc(ln_std.sem, 1)

            def ffn(l, w):
                turn_x(l, 2 * w)

                def gate(f, par):
                    act.wait_ge(*h_ready.at(l, w * FC - 1 + f))
                    act.wait_ge(*gu_ready.at(l, w * FC + 1 + f))
                    f_(sil[:, par, :], PS[:, par, :], ACT.Silu).then_inc(silu_ready.sem, 1)

                with act.Fori(0, FC // 2) as it:
                    for par in range(2):
                        gate(it * 2 + par, par)
                norm_stds(l, 2 * w)

            def mixer(l):
                turn_x(l, 1)
                steps[0] = 0

                def link(ins):
                    steps[0] += 1
                    ins.then_inc(act_done.sem, 1)
                    act.wait_ge(*act_done.at(l, steps[0]))

                def bank_of(*key):
                    act.wait_ge(*filled(l, key))
                    return bank(key)

                def drain_heads(dst, *key, **kw):
                    b = bank_of(*key)
                    f_(dst, b[0:dst.shape[0], 0:dst.shape[1]], ACT.Copy, **kw).then_inc(drained_act.sem, 1)

                act.wait_ge(*drained(l, ("par",)))
                for m in range(0, 30, 2):
                    b = bank_of("proj", m)
                    if m < 6:
                        nc.scalar.copy(raw[:, m, 3:515], b).then_inc(drained_act.sem, 1)
                    else:
                        g, i = 2 + (m - 6) // 4, (m - 6) % 4
                        c0, c1 = PROJ_LOADS[g]
                        d = c0 - (GDN_W if c0 >= C_GZ else 0)
                        nc.scalar.copy(h_tok[:, i, d:d + c1 - c0], b[:, 0:c1 - c0]).then_inc(drained_act.sem, 1)
                act.wait_ge(*conv_done.at(l, 6))
                f_(conv[:, :, :], conv[:, :, :], ACT.Silu).then_inc(conv_silu.sem, 1)
                act.wait_ge(*gates_in.at(l, 1))
                z = C_GZ - GDN_W
                link(f_(siluz[:, :, :], h_tok[:, :, z:z + 256], ACT.Silu))
                link(f_(ab_e, ab_abs, ACT.Exp, scale=-1.0))
                link(f_(ab_ln, ab_e, ACT.Ln, bias=1.0))
                f_(ea, prm[:, 256:260], ACT.Exp)
                f_(lamexp, lamdot, ACT.Exp)
                cb, cg = C_GB - GDN_W, C_GATE - GDN_W
                f_(beta.rearrange("p (t h) -> p t h", t=T), h_tok[:, :, cb:cb + H], ACT.Exp, scale=-1.0)
                f_(gate.rearrange("p (t h) -> p t h", t=T), h_tok[:, :, cg:cg + 12], ACT.Exp,
                   scale=-1.0).then_inc(gates_exp.sem, 1)
                for s in range(6):
                    drain_heads(nsaT[0:HD, s, :], "trn", s)
                for s in range(2):
                    drain_heads(dupT[:, s, :], "dup", s)
                for s in range(2):
                    b = bank_of("hid", s)
                    f_(hid[:, s, :, 0:NCMP], b[:, 0:64].rearrange("p (f c) -> p f c", f=2)[:, :, 0:NCMP],
                       ACT.Silu).then_inc(drained_act.sem, 1)
                act.wait_ge(*cmp_shifted.at(l, 1))
                f_(csb[:, :, 0:NCMP], csb[:, :, 0:NCMP], ACT.Exp).then_inc(cmp_exp.sem, 1)
                for i in range(T):
                    drain_heads(cpTs[0:NCMP, i, :], "cpT", i)
                for n in range(UNITS * T + 2):
                    u, i = divmod(n, T)
                    if n < UNITS * T:
                        w = (i + 1) * P
                        b = bank_of("sc", u, i)
                        act.wait_ge(*row_max.at(l, n + 1))
                        f_(prob[:, n % 3, 0:w], b[:, 0:w], ACT.Exp, bias=nmax[:, n:n + 1],
                           accum_out=rsum[:, n:n + 1]).then_inc(drained_act.sem, 1)
                        if i == 1 and 2 * H <= u + 1 < UNITS:
                            s = 2 * ((u + 1) % 2)
                            drain_heads(pairT[0:DQK, s, :], "trq", u + 1)
                            drain_heads(pairT[0:DQK, s + 1, :], "trk", u + 1)
                    if n >= 2:
                        v, i = divmod(n - 2, T)
                        if i < 2:
                            b = bank_of("tp", v, i)
                            c = i * (i + 1) // 2
                            nc.scalar.copy(probT[:, v % 2, c:c + i + 1, :],
                                           b[:, 0:(i + 1) * P].rearrange("p (n q) -> p n q", q=P)) \
                                .then_inc(drained_act.sem, 1)
                act.wait_ge(*norm_sum.at(l, 1))
                f_(rstd[:, 0:16], ssq[:, 0:16], ACT.Sqrt, bias=epses[:, 1:2], scale=1.0 / HD).then_inc(norm_std.sem, 1)
                first = [0, 512, 896, 1152]
                for m in range(H * T + 2):
                    if m < H * T:
                        h, j = m // T, T - 1 - m % T
                        if m % T == 0:
                            s = 2 * (h % 2)
                            drain_heads(pairT[0:HD, s, :], "trq", UNITS + h, scale=HD ** -0.5)
                            drain_heads(pairT[0:HD, s + 1, :], "trk", UNITS + h)
                        w = SEQ - j * P
                        t = prob[:, m % 3, 0:w]
                        if m >= 3:
                            act.wait_ge(*drained(l, ("z", (m - 3) // T, T - 1 - (m - 3) % T)))
                        b = bank_of("z", h, j)
                        link(f_(t, b[:, 0:w], ACT.Abs))
                        link(f_(t, t, ACT.Exp, scale=-1.0))
                        f_(t, t, ACT.Ln, bias=1.0).then_inc(soft_ln.sem, 1)
                    if m >= 2:
                        h, j = (m - 2) // T, T - 1 - (m - 2) % T
                        w = SEQ - j * P
                        b = bank_of("c", h, j)
                        f_(attT[:, h % 2, first[j]:first[j] + w], b[:, 0:w], ACT.Exp).then_inc(drained_act.sem, 1)
                        if j == 0:
                            b = bank_of("sbo", h)
                            c = 3 * 256 + HD * h
                            nc.scalar.copy(mix[:, :, c:c + HD],
                                           b[:, 0:256].rearrange("p (t c) -> p t c", t=T)).then_inc(drained_act.sem, 1)
                for i in range(T):
                    b = bank_of("gtok", i, 0)
                    nc.scalar.copy(qtok[:, i, :], b[:, 0:256])
                    nc.scalar.copy(ktok[:, i, 0:128], b[:, 256:384]).then_inc(drained_act.sem, 1)
                    b = bank_of("gtok", i, 1)
                    nc.scalar.copy(ktok[:, i, 128:256], b[:, 0:128])
                    nc.scalar.copy(vtok[:, i, :], b[:, 128:384]).then_inc(drained_act.sem, 1)
                act.wait_ge(*norm_sum.at(l, 2))
                f_(rstd, ssq, ACT.Sqrt, bias=epses[:, 1:2]).then_inc(norm_std.sem, 1)
                act.wait_ge(*decays_in.at(l, 1))
                f_(expG, gcol[:, 0:16], ACT.Exp)
                f_(expKd, expKd, ACT.Exp)
                f_(gl[0:64, :], gcol[0:64, 32:64], ACT.Exp).then_inc(decays_exp.sem, 1)
                for i in range(T):
                    drain_heads(kTb[0:HD, :], "kT", i)
                    drain_heads(qTb[0:HD, :], "qT", i)
                    drain_heads(qdT[0:HD, i, :], "qdT", i)
                    b = bank_of("D", i)
                    if i:
                        act.wait_ge(*drained(l, ("KQ", i - 1)))
                    for h in range(H):
                        s = slice(h * P, (h + 1) * P)
                        n = i * H + h
                        ins = f_(Dm[:, s], b[:, s], ACT.Exp, bias=negG[:, n:n + 1])
                    ins.then_inc(drained_act.sem, 1)
                for m in range(T, LEVELS * T):
                    lev, i = divmod(m, T)
                    drain_heads(T1[:, m % 2, :], "T1", lev, i)
                for i in range(T):
                    drain_heads(wT[0:HD, i, :], "wT", i)
                    b = bank_of("u", i)
                    nc.scalar.copy(u_new[:, i, :], b[:, 0:256]).then_inc(drained_act.sem, 1)
                for i in range(T):
                    b = bank_of("o", i)
                    nc.scalar.copy(mix[:, i, 256:512], b[:, 0:256]).then_inc(drained_act.sem, 1)
                act.wait_ge(*norm_sum.at(l, 3))
                f_(rstd[:, 0:16], ssq[:, 0:16], ACT.Sqrt, bias=epses[:, 1:2], scale=1.0 / HD).then_inc(norm_std.sem, 1)
                for i in range(T):
                    for f in range(2):
                        b = bank_of("mt", i, f)
                        nc.scalar.copy(xT[:, 4 * f:4 * f + 4, i * P:(i + 1) * P],
                                       b.rearrange("p (k t) -> p k t", k=4)).then_inc(drained_act.sem, 1)
                norm_stds(l, 1)
                assert steps[0] == ACT_STEPS, ("ACT_STEPS", steps[0])

            with act.Fori(0, DEPTH) as l:
                ffn(l, 0)
                mixer(l)
                ffn(l, 1)

        @block.vector
        def _(dve):
            v = nc.vector
            tt, ts, stt = v.tensor_tensor, v.tensor_scalar, v.scalar_tensor_tensor
            steps = [0]
            dve.wait_ge(consts_loaded.sem, 32)
            v.memset(epses[:, 0:1], LN_EPS)
            v.memset(epses[:, 1:2], NORM_EPS)
            v.tensor_copy(masks[:, :], arena[:, 0:len(MASKS) * P]).then_inc(consts_cast.sem, 1)
            dve.sem_inc(h_ready.sem, h_ready.start)
            dve.wait_ge(x_loaded.sem, 16)
            dve.sem_inc(x_ready.sem, x_ready.start)

            def link(l, ins):
                steps[0] += 1
                ins.then_inc(dve_done.sem, 1)
                dve.wait_ge(*dve_done.at(l, steps[0]))

            def add_and_count(l, i, half, b, sem_=None):
                xs = x_tok[:, i, half * 512:(half + 1) * 512]
                ins = stt(out=xs, in0=xs, scalar=ALPHA, in1=b, op0=ALU.mult, op1=ALU.add)
                if sem_ is None:
                    link(l, ins)
                else:
                    ins.then_inc(sem_.sem, 1)
                    dve.wait_ge(*drained(l, ("wo", half, i)))
                link(l, v.bn_stats(lnst[:, i, 6 * half:6 * half + 6], xs))

            def normalise(l, j, i):
                dve.sem_inc(waits_taken.sem, 1)
                link(l, v.bn_aggr(lnst[:, i, 12:14], lnst[:, i, 0:12]))
                ts(lnst[:, i, 13:14], lnst[:, i, 13:14], 1.0, None, ALU.mult).then_inc(ln_var.sem, 1)
                dve.wait_ge(*ln_std.at(l, T * j + i + 1))
                link(l, v.reciprocal(lnst[:, i, 15:16], lnst[:, i, 14:15]))
                xs = x_tok[:, i, :]
                link(l, ts(xs, xs, lnst[:, i, 12:13], lnst[:, i, 15:16], ALU.subtract, ALU.mult))
                dve.wait_ge(*lnp_loaded.at(l, 32 * (j + 1)))
                link(l, tt(xs, xs, lnp[:, 0, :], ALU.mult))
                tt(xs, xs, lnp[:, 1, :], ALU.add).then_inc(x_ready.sem, 1)

            def ffn(l, w):
                def gated(f, par):
                    dve.wait_ge(*silu_ready.at(l, w * FC + 1 + f))
                    stt(out=hT[:, bass.ds(f, 1), :].rearrange("p f t -> p (f t)"), in0=sil[:, par, :], scalar=0.5,
                        in1=PS[:, 2 + par, :], op0=ALU.mult, op1=ALU.mult).then_inc(h_ready.sem, 1)

                with dve.Fori(0, FC // 2) as it:
                    for par in range(2):
                        gated(it * 2 + par, par)
                for half in range(2):
                    for i in range(T):
                        dve.wait_ge(*down_ready.at(l, 8 * w + 4 * half + i + 1))
                        add_and_count(l, i, half, PS[:, i if half else 4 + i, :])
                        if half:
                            normalise(l, 2 * w, i)

            def mixer(l):
                def bank_of(*key):
                    dve.wait_ge(*filled(l, key))
                    return bank(key)

                def drain(ins):
                    ins.then_inc(drained_dve.sem, 1)

                def tiles(x_):
                    return x_.rearrange("p (t c) -> p t c", t=T)

                def over(col, n):
                    return col.unsqueeze(2).broadcast_to([col.shape[0], col.shape[1], n])

                def head_scale(dst, src, colmn):
                    for i in range(T):
                        c = over(colmn[:, i * H:(i + 1) * H], HD)
                        ins = tt(dst[:, i, :].rearrange("p (h d) -> p h d", h=H),
                                 src[:, i, :].rearrange("p (h d) -> p h d", h=H), c, ALU.mult)
                    return ins

                b = bank_of("par")
                v.memset(raw[:, :, 0:3], 0.0)
                drain(v.tensor_copy(parT[:, :], b[:, 0:PARAM_ROWS]))
                dve.wait_ge(*drained(l, ("par",)))
                for m in range(1, 30, 2):
                    b = bank_of("proj", m)
                    if m < 6:
                        drain(v.tensor_copy(raw[:, m, 3:515], b))
                    else:
                        g, i = 2 + (m - 6) // 4, (m - 6) % 4
                        c0, c1 = PROJ_LOADS[g]
                        d = c0 - (GDN_W if c0 >= C_GZ else 0)
                        drain(v.tensor_copy(h_tok[:, i, d:d + c1 - c0], b[:, 0:c1 - c0]))
                    if 7 <= m < 19:
                        j = (m - 7) // 2
                        dve.wait_ge(*drained(l, ("proj", j)))
                        link(l, ts(conv[:, j, :], raw[:, j, 0:SEQ], parT[:, j:j + 1], None, ALU.mult))
                        for k in range(1, 4):
                            ins = stt(out=conv[:, j, :], in0=raw[:, j, k:k + SEQ], scalar=parT[:, 6 * k + j:6 * k + j + 1],
                                      in1=conv[:, j, :], op0=ALU.mult, op1=ALU.add)
                            if k < 3:
                                link(l, ins)
                        ins.then_inc(conv_done.sem, 1)
                dve.wait_ge(*drained(l, ("proj", 28)))
                dve.wait_ge(*drained(l, ("proj", 29)))
                ca = C_GA - GDN_W
                link(l, tt(tiles(ab_x), h_tok[:, :, ca:ca + H],
                           prm[:, 260:264].unsqueeze(1).broadcast_to([P, T, H]), ALU.add))
                link(l, stt(out=ab_abs, in0=ab_x, scalar=-1.0, in1=ab_x, op0=ALU.mult, op1=ALU.max))
                lam = rinv[:, 0:1]
                prod = prob[:, 2, 0:64]
                link(l, tt(prod, prm[:, 0:64], prm[:, 64:128], ALU.mult))
                v.tensor_reduce(lamdot, prod.rearrange("p (a d) -> p a d", a=2), AX.X, ALU.add).then_inc(gates_in.sem, 1)
                for i in range(T):
                    cq, ck = C_NQ - GDN_W, C_NKC - GDN_W
                    for src, kind, n in ((h_tok[:, i, cq:cq + 256].rearrange("p (n a d) -> p n a d", n=4, a=2), "q", 4),
                                         (h_tok[:, i, ck:ck + 384].rearrange("p (n w) -> p n w", n=3)[:, :, 0:HD]
                                          .rearrange("p n (a d) -> p n a d", a=2), "k", 3)):
                        cos = const("c" + kind)[:, i * 32:(i + 1) * 32].unsqueeze(1).unsqueeze(1)
                        sin = const("s" + kind)[:, i * 64:(i + 1) * 64].rearrange("p (a d) -> p a d", a=2).unsqueeze(1)
                        t0 = prob[:, 0, 0:64 * n].rearrange("p (n a d) -> p n a d", n=n, a=2)
                        t1 = prob[:, 1, 0:64 * n].rearrange("p (n a d) -> p n a d", n=n, a=2)
                        tt(t0, src, cos.broadcast_to([P, n, 2, 32]), ALU.mult)
                        link(l, tt(t1, src[:, :, ::-1, :], sin.broadcast_to([P, n, 2, 32]), ALU.mult))
                        ins = tt(src, t0, t1, ALU.add)
                        if i == T - 1 and kind == "k":
                            ins.then_inc(nsa_rotated.sem, 1)
                        else:
                            link(l, ins)
                dve.wait_ge(*nsa_rotated.at(l, 1))
                for s, c in ((0, C_NKC - GDN_W), (1, C_NVC - GDN_W)):
                    ins = v.tensor_copy(dup[:, s].rearrange("p t (a d) -> p t a d", a=2),
                                        h_tok[:, :, c:c + HD].unsqueeze(2).broadcast_to([P, T, 2, HD]))
                ins.then_inc(dup_ready.sem, 1)
                dve.wait_ge(*gates_exp.at(l, 1))
                for s in (beta, gate):
                    link(l, ts(s, s, 1.0, None, ALU.add))
                    link(l, v.reciprocal(s, s))
                link(l, stt(out=ab_ln, in0=ab_x, scalar=0.0, in1=ab_ln, op0=ALU.max, op1=ALU.add))
                link(l, stt(out=tiles(gdec), in0=tiles(ab_ln), scalar=-1.0,
                            in1=ea.unsqueeze(1).broadcast_to([P, T, H]), op0=ALU.mult, op1=ALU.mult))
                link(l, tt(lam, lamexp[:, 1:2], lamexp[:, 0:1], ALU.subtract))
                tt(neglam, lam, prm[:, 264:265], ALU.subtract).then_inc(gates_ready.sem, 1)
                for s in range(2):
                    dve.wait_ge(*drained(l, ("dup", s)))
                    for r in range(2):
                        rows = slice(HD * r, HD * (r + 1))
                        src = dupT[rows, s, :].rearrange("p (c q) -> p q c", q=16)
                        for e in range(2):
                            pe_ = over(parT[rows, 24 + 16 * s + 8 * e:24 + 16 * s + 8 * e + 8], NCMP)
                            ins = tt(blk[rows, s, 8 * e:8 * e + 8, :], src[:, r::2, e:e + NCMP], pe_, ALU.add)
                            if r == 0 or e == 0:
                                link(l, ins)
                    ins.then_inc(blocks_ready.sem, 1)
                b = bank_of("kcmp")
                drain(v.tensor_copy(kcmpT[0:HD, 0:NCMP], b[0:HD, 0:NCMP]))
                b = bank_of("vcmp")
                drain(v.tensor_copy(vcmp[0:NCMP, :], b[0:NCMP, 0:HD]))
                b = bank_of("cs")
                cn = csb[:, :, 0:NCMP]

                def by_tile(x_):
                    return x_.rearrange("p (t h) c -> p t h c", t=T)

                def tile_mask(name):
                    return tiles(const(name)).unsqueeze(2).broadcast_to([P, T, H, 32])[:, :, :, 0:NCMP]

                drain(tt(by_tile(cn), by_tile(b.rearrange("p (n c) -> p n c", c=32)[:, :, 0:NCMP]),
                         tile_mask("cneg"), ALU.add))
                dve.wait_ge(*drained(l, ("cs",)))
                link(l, v.tensor_reduce(cmx, cn, AX.X, ALU.max))
                tt(cn, cn, over(cmx, NCMP), ALU.subtract).then_inc(cmp_shifted.sem, 1)
                dve.wait_ge(*cmp_exp.at(l, 1))
                link(l, v.tensor_reduce(cmx, cn, AX.X, ALU.add))
                link(l, v.reciprocal(cmx, cmx))
                link(l, tt(cn, cn, over(cmx, NCMP), ALU.mult))
                tt(by_tile(cn), by_tile(cn), tile_mask("c01"), ALU.mult).then_inc(cmp_probs.sem, 1)
                gates = tiles(gate).rearrange("p t (h b) -> p t h b", b=3)
                for i in range(T):
                    b = bank_of("co", i)
                    drain(tt(mix[:, i, 512:768].rearrange("p (h d) -> p h d", h=H),
                             b[:, 0:256].rearrange("p (h d) -> p h d", h=H), over(gates[:, i, :, 0], HD), ALU.mult))
                dve.wait_ge(*drained(l, ("co", T - 1)))
                for n in range(UNITS * T + 2):
                    if n < UNITS * T:
                        u, i = divmod(n, T)
                        b = bank_of("sc", u, i)
                        v.tensor_reduce(nmax[:, n:n + 1], b[:, 0:(i + 1) * P], AX.X, ALU.max,
                                        negate=True).then_inc(row_max.sem, 1)
                    if n >= 2:
                        u, i = divmod(n - 2, T)
                        if i >= 2:
                            b = bank_of("tp", u, i)
                            c = i * (i + 1) // 2
                            drain(v.tensor_copy(probT[:, u % 2, c:c + i + 1, :],
                                                b[:, 0:(i + 1) * P].rearrange("p (n q) -> p n q", q=P)))
                        if i == T - 1:
                            b = bank_of("pv", u)
                            pv = tiles(b[:, 0:256])
                            r = rinv[:, 0:T]
                            link(l, v.reciprocal(r, rsum[:, T * u:T * u + T]))
                            if u < 2 * H:
                                h, br = divmod(u, 2)
                                c = 512 + HD * h
                                link(l, tt(r, r, gates[:, :, h, 1 + br], ALU.mult))
                            else:
                                h, br = divmod(u - 2 * H, 2)
                                c = HD * h
                                if br:
                                    link(l, ts(r, r, neglam, None, ALU.mult))
                            dst = mix[:, :, c:c + HD]
                            if u >= 2 * H and br == 0:
                                drain(tt(dst, pv, over(r, HD), ALU.mult))
                                dve.wait_ge(*drained(l, ("pv", u)))
                            else:
                                drain(tt(tmpo, pv, over(r, HD), ALU.mult))
                                dve.wait_ge(*drained(l, ("pv", u)))
                                link(l, tt(dst, dst, tmpo, ALU.add))

                def sums_of_squares(dst, src, tmp, last):
                    for i in range(T):
                        ins = tt(tmp[:, i, :], src[:, i, :], src[:, i, :], ALU.mult)
                    link(l, ins)
                    for i in range(T):
                        ins = v.tensor_reduce(dst[:, i * H:(i + 1) * H], tmp[:, i, :].rearrange("p (h d) -> p h d", h=H),
                                              AX.X, ALU.add)
                    if last:
                        ins.then_inc(norm_sum.sem, 1)
                    else:
                        link(l, ins)

                def gain(dst, g):
                    for i in range(T):
                        d = dst[:, i, :].rearrange("p (h d) -> p h d", h=H)
                        ins = tt(d, d, g.unsqueeze(1).broadcast_to([P, H, HD]), ALU.mult)
                    return ins

                dmix = mix[:, :, 0:256]
                sums_of_squares(ssq[:, 0:16], dmix, tmpl, True)
                link(l, ts(prm[:, 128:192], prm[:, 128:192], prm[:, 265:266], None, ALU.mult))
                dve.wait_ge(*norm_std.at(l, 1))
                link(l, v.reciprocal(rstd[:, 0:16], rstd[:, 0:16]))
                link(l, head_scale(dmix, dmix, rstd[:, 0:16]))
                gain(dmix, prm[:, 128:192]).then_inc(mix_ready.sem, 1)
                first = [0, 512, 896, 1152]
                for m in range(H * T):
                    h, j = m // T, T - 1 - m % T
                    w = SEQ - j * P
                    dve.wait_ge(*soft_ln.at(l, m + 1))
                    b = bank_of("z", h, j)
                    drain(stt(out=soft[:, h % 2, first[j]:first[j] + w], in0=b[:, 0:w], scalar=0.0,
                              in1=prob[:, m % 3, 0:w], op0=ALU.max, op1=ALU.add))
                    dve.wait_ge(*drained(l, ("z", h, j)))
                    d = soft[:, h % 2, first[j]:first[j] + P]
                    tt(d, d, const("sb01"), ALU.mult).then_inc(soft_ready.sem, 1)
                dve.wait_ge(*drained(l, ("gtok", T - 1, 1)))
                sums_of_squares(ssq[:, 0:16], qtok, kb, False)
                sums_of_squares(ssq[:, 16:32], ktok, kd, True)
                b = bank_of("G")
                v.tensor_copy(gcol[:, 0:32], b[:, 0:32])
                drain(v.tensor_copy(gcol[0:64, 32:64], b[0:64, 32:64]))
                dve.wait_ge(*drained(l, ("G",)))
                ts(negG, gcol[:, 0:16], -1.0, None, ALU.mult)
                tt(expKd, gcol[:, 16:32], gcol[:, 0:16], ALU.subtract).then_inc(decays_in.sem, 1)
                dve.wait_ge(*norm_std.at(l, 2))
                link(l, v.reciprocal(rstd, rstd))
                link(l, ts(rstd[:, 0:16], rstd[:, 0:16], HD ** -0.5, None, ALU.mult))
                head_scale(qtok, qtok, rstd[:, 0:16])
                link(l, head_scale(ktok, ktok, rstd[:, 16:32]))
                dve.wait_ge(*decays_exp.at(l, 1))
                link(l, tt(betaG, beta, expG, ALU.mult))
                head_scale(kb, ktok, beta)
                head_scale(kbG, ktok, betaG)
                head_scale(vtok, vtok, beta)
                head_scale(qd, qtok, expG)
                head_scale(kd, ktok, expKd).then_inc(gdn_ready.sem, 1)
                for i in range(T):
                    b = bank_of("kbT", i)
                    drain(v.tensor_copy(kbTb[0:HD, :], b[0:HD, :]))
                    b = bank_of("KK", i)
                    dve.wait_ge(*drained(l, ("D", i)))
                    drain(tt(AT[:, i, :], b, Dm, ALU.mult))
                    b = bank_of("KQ", i)
                    drain(tt(intraT[:, i, :], b, Dm, ALU.mult))
                eye = ident.unsqueeze(1).broadcast_to([P, H, P])

                def by_head(x_):
                    return x_.rearrange("p (h c) -> p h c", h=H)

                for m in range(LEVELS * T + 1):
                    if m < T:
                        b = bank_of("X0", m)
                        drain(tt(by_head(X[:, m, :]), by_head(b), eye, ALU.add))
                        tt(by_head(XT[:, m, :]), by_head(NL[:, m % 2, :]), eye, ALU.add).then_inc(xt0_ready.sem, 1)
                    if m - 1 >= T:
                        lev, i = divmod(m - 1, T)
                        if lev < LEVELS - 1:
                            b = bank_of("X", lev, i)
                            drain(tt(X[:, i, :], X[:, i, :], b, ALU.add))
                        b = bank_of("XT", lev, i)
                        drain(tt(XT[:, i, :], XT[:, i, :], b, ALU.add))
                v.memset(states[0:HD, 0, :], 0.0).then_inc(states_clear.sem, 1)
                for n in range(2 * T):
                    i, p = divmod(n, 2)
                    rows = slice(p * CH, (p + 1) * CH)
                    if n:
                        b = bank_of("ws", n)
                        drain(tt(u_new[rows, i, :], u_new[rows, i, :], b[rows, 0:256], ALU.subtract))
                    if n < 2 * T - 1:
                        b = bank_of("S", n)
                        if n == 0:
                            drain(v.tensor_copy(states[0:HD, 1, :], b[0:HD, 0:256]))
                        else:
                            drain(tt(states[0:HD, n + 1, :], sg[0:HD, :], b[0:HD, 0:256], ALU.add))
                        dve.wait_ge(*drained(l, ("S", n)))
                        if n < 2 * T - 2:
                            i2, p2 = divmod(n + 1, 2)
                            c = p2 * 16 + i2 * H
                            link(l, tt(sg[0:HD, :].rearrange("p (h d) -> p h d", h=H),
                                       states[0:HD, n + 1, :].rearrange("p (h d) -> p h d", h=H),
                                       over(gl[0:HD, c:c + H], HD), ALU.mult))
                gmix = mix[:, :, 256:512]
                dve.wait_ge(*drained(l, ("o", T - 1)))
                sums_of_squares(ssq[:, 0:16], gmix, kbG, True)
                dve.wait_ge(*norm_std.at(l, 3))
                link(l, v.reciprocal(rstd[:, 0:16], rstd[:, 0:16]))
                link(l, head_scale(gmix, gmix, rstd[:, 0:16]))
                link(l, gain(gmix, prm[:, 192:256]))
                tt(gmix, gmix, siluz, ALU.mult).then_inc(mix_ready.sem, 1)
                for f in range(2):
                    for i in range(T):
                        b = bank_of("wo", f, i)
                        add_and_count(l, i, f, b, drained_dve)
                        if f:
                            normalise(l, 1, i)

            with dve.Fori(0, DEPTH) as l:
                steps[0] = 0
                ffn(l, 0)
                mixer(l)
                ffn(l, 1)
                assert steps[0] == DVE_STEPS, ("DVE_STEPS", steps[0])

        @block.gpsimd
        def _(pool):
            g = nc.gpsimd
            steps = [0]
            pool.wait_ge(consts_cast.sem, 1)

            def link(l, ins):
                steps[0] += 1
                ins.then_inc(pool_done.sem, 1)
                pool.wait_ge(*pool_done.at(l, steps[0]))

            def load_norm(l, j):
                pool.sem_inc(waits_taken.sem, 1)
                for n, p_ in enumerate(a["ln"][j]):
                    g.dma_start(lnp[:, n, :], p_[bass.ds(l, 1), :].broadcast_to([P, DM])).then_inc(lnp_loaded.sem, 16)
                pool.wait_ge(*lnp_loaded.at(l, 32 * (j + 1)))

            with pool.Fori(0, DEPTH) as l:
                steps[0] = 0
                pool.wait_ge(*x_ready.at(l, 0))
                at = 0
                for name, w in (("lam_q1", 32), ("lam_q2", 32), ("lam_k1", 32), ("lam_k2", 32), ("subln", 64),
                                ("gdn_g", 64), ("a_log", 4), ("dt", 4), ("lam0", 2)):
                    g.dma_start(prm[:, at:at + w], a[name][bass.ds(l, 1), :].broadcast_to([P, w])) \
                        .then_inc(params_loaded.sem, 16)
                    at += w
                g.dma_start(stage[0:24, :], a["conv_w"][l].rearrange("k (c p) -> (k c) p", p=P)) \
                    .then_inc(params_loaded.sem, 16)
                g.dma_start(stage[24:40, :], a["pe_k"][l].rearrange("(k r) d -> k (r d)", r=2)) \
                    .then_inc(params_loaded.sem, 16)
                g.dma_start(stage[40:56, :], a["pe_v"][l].rearrange("(k r) d -> k (r d)", r=2)) \
                    .then_inc(params_loaded.sem, 16)
                for s, name in enumerate(("cmp_k_w2", "cmp_v_w2")):
                    g.dma_start(w2[:, s], a[name][l].rearrange("(f p) d -> p f d", p=P)) \
                        .then_inc(params_loaded.sem, 16)
                pool.wait_ge(*params_loaded.at(l, 16 * PARAM_DMAS))
                load_norm(l, 0)
                pool.wait_ge(*drained(l, ("proj", 28)))
                pool.wait_ge(*drained(l, ("proj", 29)))
                for i in range(T):
                    for c0, kind in ((C_DQ1, "q"), (C_DK1, "k")):
                        src = h_tok[:, i, c0:c0 + 256].rearrange("p (n a d) -> p n a d", n=8, a=2)
                        cos = const("dc" + kind)[:, i * 16:(i + 1) * 16].unsqueeze(1).unsqueeze(1)
                        sin = const("ds" + kind)[:, i * 32:(i + 1) * 32].rearrange("p (a d) -> p a d", a=2).unsqueeze(1)
                        t0 = ptmp[:, 0, :].rearrange("p (n a d) -> p n a d", n=8, a=2)
                        t1 = ptmp[:, 1, :].rearrange("p (n a d) -> p n a d", n=8, a=2)
                        g.tensor_tensor(t0, src, cos.broadcast_to([P, 8, 2, 16]), ALU.mult)
                        link(l, g.tensor_tensor(t1, src[:, :, ::-1, :], sin.broadcast_to([P, 8, 2, 16]), ALU.mult))
                        ins = g.tensor_tensor(src, t0, t1, ALU.add)
                        if i == T - 1 and kind == "k":
                            ins.then_inc(diff_rotated.sem, 1)
                        else:
                            link(l, ins)
                for m in range(LEVELS * T):
                    lev, i = divmod(m, T)
                    if m < T:
                        pool.wait_ge(*drained(l, ("KK", i)))
                    if m >= 2:
                        plev, pi = divmod(m - 2, T)
                        pool.wait_ge(*filled(l, ("X0", pi) if plev == 0 else ("T1", plev, pi)))
                        if plev == 0:
                            pool.wait_ge(*xt0_ready.at(l, pi + 1))
                    g.tensor_tensor(NL[:, m % 2, :].rearrange("p (h c) -> p h c", h=H),
                                    AT[:, i, :].rearrange("p (h c) -> p h c", h=H),
                                    mask(f"lev{lev}").unsqueeze(1).broadcast_to([P, H, P]), ALU.mult) \
                        .then_inc(level_ready.sem, 1)
                pool.wait_ge(*filled(l, ("mt", T - 1, 1)))
                load_norm(l, 1)
                pool.wait_ge(*x_ready.at(l, 2 * T))
                load_norm(l, 2)
                assert steps[0] == POOL_STEPS, ("POOL_STEPS", steps[0])


_OUT = (1, SEQ, DM)


def kernel(x, w_in, w_out, ffn1_w_gu, ffn1_w_down, ffn2_w_gu, ffn2_w_down,
           ln1_g, ln1_b, ln2_g, ln2_b, ln3_g, ln3_b,
           diff_lam_q1, diff_lam_k1, diff_lam_q2, diff_lam_k2, diff_subln_g,
           gdn_conv_w, gdn_a_log, gdn_dt_bias, gdn_norm_g,
           nsa_pe_k, nsa_pe_v, nsa_cmp_k_w1, nsa_cmp_k_w2, nsa_cmp_v_w1, nsa_cmp_v_w2):
    from concourse import bacc
    from concourse.bass_utils import run_bass_kernel_spmd

    tables, masks_, lam0 = constants()
    given = dict(x=x, w_in=w_in, w_out=w_out, gu1=ffn1_w_gu, down1=ffn1_w_down, gu2=ffn2_w_gu, down2=ffn2_w_down,
                 ln1_g=ln1_g, ln1_b=ln1_b, ln2_g=ln2_g, ln2_b=ln2_b, ln3_g=ln3_g, ln3_b=ln3_b,
                 lam_q1=diff_lam_q1, lam_k1=diff_lam_k1, lam_q2=diff_lam_q2, lam_k2=diff_lam_k2,
                 subln=diff_subln_g, conv_w=gdn_conv_w, a_log=gdn_a_log, dt=gdn_dt_bias, gdn_g=gdn_norm_g,
                 pe_k=nsa_pe_k, pe_v=nsa_pe_v, cmp_k_w1=nsa_cmp_k_w1, cmp_k_w2=nsa_cmp_k_w2,
                 cmp_v_w1=nsa_cmp_v_w1, cmp_v_w2=nsa_cmp_v_w2, consts=tables, masks=masks_, lam0=lam0)
    nc = bacc.Bacc("TRN2", target_bir_lowering=False, num_devices=1)
    arrays, aps = {}, {}
    for name, value in given.items():
        arrays[name + "_in"] = np.ascontiguousarray(value)
        aps[name] = nc.dram_tensor(name + "_in", arrays[name + "_in"].shape, F32, kind="ExternalInput").ap()
    aps["gu"] = (aps["gu1"], aps["gu2"])
    aps["down"] = (aps["down1"], aps["down2"])
    aps["ln"] = [(aps[f"ln{j}_g"], aps[f"ln{j}_b"]) for j in (1, 2, 3)]
    y = nc.dram_tensor("y_out", _OUT, F32, kind="ExternalOutput").ap()
    trunk_program(nc, aps, y)
    got = run_bass_kernel_spmd(nc, [arrays], core_ids=[0])
    return got.results[0]["y_out"]
```

```python
import math
from contextlib import ExitStack

import numpy as np
import concourse.bass as bass
from concourse import mybir

F32 = mybir.dt.float32
F32R = mybir.dt.float32r
BF16 = mybir.dt.bfloat16
ALU = mybir.AluOpType
ACT = mybir.ActivationFunctionType
AX = mybir.AxisListType

P = 128
SEQ, DM, DEPTH, DFF = 512, 1024, 2, 2816
T = SEQ // P
KD = DM // P
FC = DFF // P
H, HD, DQK = 4, 64, 32
CH = 64
NCMP = 31
ALPHA = (2 * DEPTH) ** 0.25
LN_EPS, NORM_EPS, NEG = 1e-5, 1e-6, -1e30

C_DQ1, C_DQ2, C_DK1, C_DK2, C_DV = 0, 128, 256, 384, 512
C_GQ, C_GZ, C_GA, C_GB, C_NQ = 768, 1536, 1792, 1796, 1800
C_NKC, C_NVC, C_NVS, C_NVW, C_GATE = 2056, 2120, 2248, 2376, 2440
C_SQ, C_SK, C_SV, C_END = 2452, 2708, 2964, 3220
GDN_W = 3 * H * HD
HW = C_END - GDN_W

GU_W = 256
GU_LOADS = DFF // GU_W
DOWN_LOADS = [(f, min(f + 4, FC)) for f in range(0, FC, 4)]
PROJ_COLS = [768, 1152, C_GZ, C_GZ + 422, C_GZ + 844, C_GZ + 1264, C_END]
PROJ_LOADS = list(zip(PROJ_COLS, PROJ_COLS[1:])) + [(0, 384), (384, 768)]
RING = 2
SLOT = KD * 2 * GU_W
FFN_LOADS = GU_LOADS + len(DOWN_LOADS)
MIX_LOADS = len(PROJ_LOADS) + 4
LAYER_LOADS = 2 * FFN_LOADS + MIX_LOADS
assert LAYER_LOADS % RING == 0
UNIT = SLOT // 2
DOWN_UNITS = FC // 2
FFN_UNITS = FC + DOWN_UNITS
PROJ_UNITS = 2 * len(PROJ_LOADS)
OUT_UNITS = 4
FIRST_UNIT = (0, FFN_UNITS, FFN_UNITS + PROJ_UNITS, FFN_UNITS + PROJ_UNITS + OUT_UNITS)
LAYER_UNITS = FIRST_UNIT[3] + FFN_UNITS
FIRST_LOAD = (0, FFN_LOADS, FFN_LOADS + MIX_LOADS)

SLAB = 52704
PARAM_DMAS = 14
ACT_STEPS, DVE_STEPS, POOL_STEPS = 35, 202, 15

NSA_U = [("sel", h) if b == 0 else ("win", h) for h in range(H) for b in range(2)]
UNITS = 2 * H + 2 * H
LEVELS = 6
PARAM_ROWS = 24 + 16 + 16


def mixer_items():
    q = [(("par",), "dve")]
    q += [(("proj", m), ("act", "dve")[m % 2]) for m in range(30)]
    q += [(("trn", s), "act") for s in range(6)]
    q += [(("dup", s), "act") for s in range(2)]
    q += [(("hid", s), "act") for s in range(2)] + [(("kcmp",), "dve"), (("vcmp",), "dve"), (("cs",), "dve")]
    q += [(("cpT", i), "act") for i in range(T)] + [(("co", i), "dve") for i in range(T)]
    for n in range(UNITS * T + 2):
        u = n // T
        if n < UNITS * T:
            q.append((("sc", u, n % T), "act"))
            if n % T == 1 and 2 * H <= u + 1 < UNITS:
                q += [(("trq", u + 1), "act"), (("trk", u + 1), "act")]
        if n >= 2:
            v, i = (n - 2) // T, (n - 2) % T
            q.append((("tp", v, i), ("act", "act", "dve", "dve")[i]))
            if i == T - 1:
                q.append((("pv", v), "dve"))
    for m in range(H * T + 2):
        if m < H * T:
            if m % T == 0:
                q += [(("trq", UNITS + m // T), "act"), (("trk", UNITS + m // T), "act")]
            q.append((("z", m // T, T - 1 - m % T), "dve"))
        if m >= 2:
            h, j = (m - 2) // T, T - 1 - (m - 2) % T
            q.append((("c", h, j), "act"))
            if j == 0:
                q.append((("sbo", h), "act"))
    q += [(("gtok", i, f), "act") for i in range(T) for f in range(2)]
    q.append((("G",), "dve"))
    for i in range(T):
        q += [(("kT", i), "act"), (("kbT", i), "dve"), (("qT", i), "act"), (("qdT", i), "act"),
              (("D", i), "act"), (("KK", i), "dve"), (("KQ", i), "dve")]
    for m in range(LEVELS * T + 1):
        if m < LEVELS * T:
            lev, i = divmod(m, T)
            q.append((("X0", i), "dve") if lev == 0 else (("T1", lev, i), "act"))
        if m - 1 >= T:
            lev, i = divmod(m - 1, T)
            if lev < LEVELS - 1:
                q.append((("X", lev, i), "dve"))
            q.append((("XT", lev, i), "dve"))
    for i in range(T):
        q += [(("wT", i), "act"), (("u", i), "act")]
    for n in range(2 * T):
        if n:
            q.append((("ws", n), "dve"))
        if n < 2 * T - 1:
            q.append((("S", n), "dve"))
        if n % 2:
            q.append((("o", n // 2), "act"))
    q += [(("mt", i, f), "dve") for i in range(T) for f in range(2)]
    q += [(("wo", f, i), "dve") for f in range(2) for i in range(T)]
    return q


def const_columns():
    widths = [("ident", 128), ("upto", 128), ("chunk", 128), ("negtri", 128), ("negone", 128),
              ("sb01", 128), ("c01", T * 32), ("cneg", T * 32),
              ("cq", T * 32), ("sq", T * 64), ("ck", T * 32), ("sk", T * 64),
              ("dcq", T * 16), ("dsq", T * 32), ("dck", T * 16), ("dsk", T * 32)]
    at, n = {}, 0
    for name, w in widths:
        at[name] = (n, n + w)
        n += w
    return at, n


MASKS = ["ident", "causal", "sbneg", "gdnneg"] + [f"lev{m}" for m in range(LEVELS)]


def constants():
    at, n = const_columns()
    c = np.zeros((P, n), np.float32)

    def put(name, a):
        c[:, at[name][0]:at[name][1]] = np.asarray(a, np.float32).reshape(P, -1)

    r = np.arange(P)[:, None]
    k = np.arange(P)[None, :]
    same = (r // CH) == (k // CH)
    put("ident", r == k)
    put("upto", (r <= k) & same)
    put("chunk", same)
    put("negtri", -(r >= k).astype(np.float32))
    put("negone", -np.ones((P, P)))
    put("sb01", r < k)
    tok = np.arange(T)[None, :, None] * P + np.arange(P)[:, None, None]
    blk = np.arange(32)[None, None, :]
    seen = (blk < NCMP) & (blk * 16 + 31 <= tok)
    put("c01", seen)
    put("cneg", np.where(seen, 0, NEG))

    def rope(dim, scale):
        inv = (np.float32(10000.0) ** (-np.arange(0, dim, 2, dtype=np.float32) / dim)).astype(np.float32)
        ang = tok.astype(np.float32) * inv[None, None, :]
        cos, sin = np.cos(ang) * scale, np.sin(ang) * scale
        return cos, np.stack([-sin, sin], 2)

    for pre, dim in (("", HD), ("d", DQK)):
        for kind, scale in (("q", np.float32(dim ** -0.5)), ("k", np.float32(1))):
            cos, sin = rope(dim, scale)
            put(pre + "c" + kind, cos)
            put(pre + "s" + kind, sin)
    masks = [r == k, np.where(k > r, NEG, 0), np.where(r < k, 0, NEG),
             np.where((k >= r) & same, 0, NEG)]
    for lev in range(LEVELS):
        b = 2 ** lev
        masks.append(-(((k // b) % 2 == 1) & ((r // b) == (k // b) - 1)).astype(np.float32))
    masks = np.stack([np.asarray(m, np.float32) for m in masks], 1).reshape(P, -1)
    lam = np.zeros((DEPTH, 2), np.float32)
    for layer in range(DEPTH):
        init = 0.8 - 0.6 * math.exp(-0.3 * layer)
        lam[layer] = (init, 1 - init)
    return c, masks, lam


class Signal:

    def __init__(self, sem, per_layer, start=0):
        self.sem, self.per_layer, self.start = sem, per_layer, start

    def at(self, layer, n):
        return self.sem, layer * self.per_layer + (n + self.start)


def trunk_program(nc, a, out):
    items = mixer_items()
    number = {key: n for n, (key, _) in enumerate(items)}
    drainer = {key: who for key, who in items}
    rank, seen = {}, {"act": 0, "dve": 0}
    for key, who in items:
        seen[who] += 1
        rank[key] = seen[who]

    ctx = ExitStack()
    with ctx:
        ctx.enter_context(nc.sbuf_tensor("slab", [P, SLAB], F32))
        slab_at = nc.sbuf_base - 4 * SLAB
        taken = [0]

        def place(name, at, shape, dt):
            return nc.alloc_sbuf_tensor_at(name, [P] + shape, dt, offset=slab_at + 4 * at)

        def sb(name, shape, dt=F32):
            words = int(np.prod(shape[1:])) // (2 if dt == BF16 else 1)
            at = taken[0]
            taken[0] += -(-words // 8) * 8
            assert taken[0] <= SLAB, (name, taken[0])
            return place(name, at, shape[1:], dt)

        def sem(name, per_layer, start=0):
            return Signal(ctx.enter_context(nc.semaphore(name)), per_layer, start)

        cat, cw = const_columns()
        consts = sb("consts", [P, cw])
        masks = sb("masks", [P, len(MASKS) * P], BF16)
        x_tok = sb("x_tok", [P, T, DM])
        xT_at = taken[0]
        xTh = sb("xTh", [P, KD, SEQ], F32R)
        xTl = sb("xTl", [P, KD, SEQ], F32R)
        scratch = place("scratch", xT_at, [2 * KD * SEQ], F32)
        ring = sb("ring", [P, RING, SLOT])
        lnp = sb("lnp", [P, 2, DM])
        small = sb("small", [P, 640])
        prm = sb("prm", [P, 272])
        w2 = sb("w2", [P, 2, 2, HD])
        stage = sb("stage", [P, P])
        parT = sb("parT", [P, PARAM_ROWS])
        ptmp = sb("ptmp", [P, 2, 256])
        epses = sb("epses", [P, 2])
        lnst = sb("lnst", [P, T, 16])
        ARENA = 24656
        arena_at = taken[0]
        arena = sb("arena", [P, ARENA])
        PS = ctx.enter_context(nc.psum_tensor("banks", [P, 8, 512], F32))

        def const(name):
            return consts[:, cat[name][0]:cat[name][1]]

        def mask(name):
            n = MASKS.index(name)
            return masks[:, n * P:(n + 1) * P]

        ident, identb = const("ident"), mask("ident")

        used = [0]

        def cols(n):
            used[0] += n
            assert used[0] <= 640
            return small[:, used[0] - n:used[0]]

        nmax, rsum = cols(64), cols(64)
        rinv = cols(16)
        cmx = cols(16)
        gate = cols(T * 12)
        ab_x, ab_abs, ab_e, ab_ln = cols(16), cols(16), cols(16), cols(16)
        ea = cols(4)
        beta, gdec = cols(16), cols(16)
        gcol = cols(64)
        negG = cols(16)
        expG, expKd, gl, betaG = cols(16), cols(16), cols(32), cols(16)
        lamdot, lamexp, neglam = cols(2), cols(2), cols(1)
        ssq = cols(32)
        rstd = cols(32)

        hT = arena[:, 0:FC * SEQ].rearrange("p (f t) -> p f t", f=FC)
        sil = arena[:, FC * SEQ:FC * SEQ + 2 * SEQ].rearrange("p (b t) -> p b t", b=2)
        hh = place("hh", arena_at + 20480, [4, SEQ], F32R)
        hl = place("hl", arena_at + 20480 + 4 * SEQ, [4, SEQ], F32R)
        ffn_unit = [place(f"ffn_unit{b}", arena_at + 12288 + b * 2 * UNIT, [2, UNIT], F32R) for b in range(2)]
        proj_unit = [place(f"proj_unit{b}", arena_at + b * 8 * 422, [2, 4 * 422], F32R) for b in range(2)]
        out_unit = [place(f"out_unit{n}", arena_at + at, [2, UNIT], F32R)
                    for n, at in enumerate((19456, 4096, 8192, 12288))]
        off = {}

        def area(name, start, n):
            off[name] = start + n
            return arena[:, start:start + n]

        mix = area("mix", 0, T * DM).rearrange("p (t c) -> p t c", t=T)
        nsaT = area("nsaT", off["mix"], 6 * SEQ).rearrange("p (s t) -> p s t", s=6)
        h_tok = area("h", off["nsaT"], T * HW).rearrange("p (t c) -> p t c", t=T)
        pair0 = off["h"]
        pairT = area("pairT", pair0, 4 * SEQ).rearrange("p (s t) -> p s t", s=4)
        prob = area("prob", off["pairT"], 3 * SEQ).rearrange("p (s t) -> p s t", s=3)
        raw = arena[:, pair0:pair0 + 6 * 515].rearrange("p (j t) -> p j t", j=6)
        conv = area("conv", off["prob"], 6 * SEQ).rearrange("p (j t) -> p j t", j=6)
        siluz = area("siluz", off["conv"], T * 256).rearrange("p (t c) -> p t c", t=T)
        assert off["siluz"] <= ARENA
        dupT = scratch[:, 0:1024].rearrange("p (s t) -> p s t", s=2)
        blk = scratch[:, 1024:1024 + 992].rearrange("p (s j c) -> p s j c", s=2, j=16)
        cpTs = scratch[:, 2048:4096].rearrange("p (t c) -> p t c", t=T)
        csb = prob[:, 0, :].rearrange("p (n c) -> p n c", c=32)
        hid = pairT[:, 3, 0:128].rearrange("p (s f c) -> p s f c", s=2, f=2)
        kcmpT = pairT[:, 3, 128:160]
        vcmp = pairT[:, 3, 160:224]
        dup = pairT[:, 0:2, :].rearrange("p s (t c) -> p s t c", c=P)
        probT = scratch[:, 0:2560].rearrange("p (b n q) -> p b n q", b=2, n=10)
        tmpo = scratch[:, 2560:2560 + 256].rearrange("p (t c) -> p t c", t=T)
        tmpl = scratch[:, 2816:2816 + 1024].rearrange("p (t c) -> p t c", t=T)
        soft = probT.rearrange("p b n q -> p b (n q)")
        attT = arena[:, off["mix"]:off["mix"] + 2560].rearrange("p (b c) -> p b c", b=2)
        g0 = off["mix"]

        def garea(n):
            nonlocal g0
            g0 += n
            return arena[:, g0 - n:g0]

        states = arena[:, g0:g0 + 2048].rearrange("p (n c) -> p n c", n=8)
        qtok = garea(1024).rearrange("p (t c) -> p t c", t=T)
        ktok = garea(1024).rearrange("p (t c) -> p t c", t=T)
        vtok = garea(1024).rearrange("p (t c) -> p t c", t=T)
        kb = garea(1024).rearrange("p (t c) -> p t c", t=T)
        u_new = kb
        kbG = garea(1024).rearrange("p (t c) -> p t c", t=T)
        qd = garea(1024).rearrange("p (t c) -> p t c", t=T)
        kd = garea(1024).rearrange("p (t c) -> p t c", t=T)
        kTb, kbTb, qTb = garea(512), garea(512), garea(512)
        sg = kTb[:, 0:256]
        qdT = garea(2048).rearrange("p (t c) -> p t c", t=T)
        intraT = garea(2048).rearrange("p (t c) -> p t c", t=T)
        wT = garea(2048).rearrange("p (t c) -> p t c", t=T)
        Dm = garea(512)
        T1 = scratch[:, 4096:5120].rearrange("p (b c) -> p b c", b=2)
        NL = scratch[:, 5120:6144].rearrange("p (b c) -> p b c", b=2)
        X = scratch[:, 6144:8192].rearrange("p (t c) -> p t c", t=T)
        assert g0 <= 19456
        XT = scratch[:, 0:2048].rearrange("p (t c) -> p t c", t=T)
        AT = scratch[:, 2048:4096].rearrange("p (t c) -> p t c", t=T)

        consts_loaded = sem("consts_loaded", 0)
        x_loaded = sem("x_loaded", 0)
        slot_loaded = [sem(f"slot{s}_loaded", 32 * LAYER_LOADS // RING) for s in range(RING)]
        lnp_loaded = sem("lnp_loaded", 3 * 32)
        params_loaded = sem("params_loaded", PARAM_DMAS * 16)
        out_stored = sem("out_stored", 0)
        down_used = sem("down_used", 2 * (DOWN_UNITS - 2))
        proj_used = sem("proj_used", len(PROJ_LOADS))
        ln_turned = sem("ln_turned", 3 * 8, 8)
        gu_ready = sem("gu_ready", 2 * FC)
        down_ready = sem("down_ready", 2 * T, 2 * T)
        bank_filled = sem("bank_filled", len(items))
        act_done = sem("act_done", ACT_STEPS)
        turned_hi = sem("turned_hi", 3 * 8, 8)
        unit_hi = sem("unit_hi", LAYER_UNITS)
        h_hi = sem("h_hi", 2 * DOWN_UNITS)
        mix_hi = sem("mix_hi", 8)
        silu_ready = sem("silu_ready", 2 * FC)
        ln_std = sem("ln_std", 3 * T)
        drained_act = sem("drained_act", seen["act"])
        conv_silu = sem("conv_silu", 1)
        gates_exp = sem("gates_exp", 1)
        cmp_exp = sem("cmp_exp", 1)
        soft_ln = sem("soft_ln", H * T)
        norm_std_ready = sem("norm_std_ready", 3)
        decays_exp = sem("decays_exp", 1)
        dve_done = sem("dve_done", DVE_STEPS)
        consts_cast = sem("consts_cast", 0)
        x_ready = sem("x_ready", 3 * T, T)
        h_ready = sem("h_ready", 2 * FC, 2)
        turned_lo = sem("turned_lo", 3 * 8, 8)
        unit_lo = sem("unit_lo", LAYER_UNITS, LAYER_UNITS)
        h_lo = sem("h_lo", 2 * DOWN_UNITS)
        ln_var = sem("ln_var", 3 * T)
        drained_dve = sem("drained_dve", seen["dve"])
        conv_done = sem("conv_done", 6)
        gates_in = sem("gates_in", 1)
        nsa_rotated = sem("nsa_rotated", 1)
        blocks_ready = sem("blocks_ready", 2)
        cmp_shifted = sem("cmp_shifted", 1)
        cmp_probs = sem("cmp_probs", 1)
        row_max = sem("row_max", UNITS * T)
        soft_ready = sem("soft_ready", H * T)
        norm_sum = sem("norm_sum", 3)
        dup_ready = sem("dup_ready", 1)
        gates_ready = sem("gates_ready", 1)
        decays_in = sem("decays_in", 1)
        gdn_ready = sem("gdn_ready", 1)
        xt0_ready = sem("xt0_ready", T)
        states_clear = sem("states_clear", 1)
        mix_ready = sem("mix_ready", 2)
        waits_taken = sem("waits_taken", 0)
        diff_rotated = sem("diff_rotated", 1)
        pool_done = sem("pool_done", POOL_STEPS)
        level_ready = sem("level_ready", LEVELS * T)

        def filled(layer, key):
            return bank_filled.at(layer, number[key] + 1)

        def drained(layer, key):
            s = drained_act if drainer[key] == "act" else drained_dve
            return s.at(layer, rank[key])

        def bank(key):
            return PS[:, number[key] % 8, :]

        block = ctx.enter_context(nc.Block())

        def slot_at(n):
            return ring[:, n % RING, :]

        def load_arrived(layer, n):
            return slot_loaded[n % RING].at(layer, 32 * (n // RING + 1))

        def proj_items(g):
            return range(3 * g, 3 * g + 3) if g < 2 else range(6 + 4 * (g - 2), 10 + 4 * (g - 2))

        def unit_views(s, u):
            if s in (0, 3):
                w = s // 3
                raw_, n = (u // 2, u % 2) if u < FC else (GU_LOADS + (u - FC) // 2, (u - FC) % 2)
                slot = slot_at(FIRST_LOAD[2 * w] + raw_)
                buf = ffn_unit[(u + w) % 2]
                if u < FC:
                    raw_ = slot.rearrange("p (k b n c) -> p k b n c", k=KD, b=2, n=2)[:, :, :, n, :]
                    return [buf[:, e, :].rearrange("p (k b c) -> p k b c", k=KD, b=2) for e in range(2)] + [raw_]
                return [buf[:, 0, :], buf[:, 1, :], slot[:, n * UNIT:(n + 1) * UNIT]]
            if s == 1:
                w = 4 * (PROJ_LOADS[u // 2][1] - PROJ_LOADS[u // 2][0])
                slot, buf = slot_at(FIRST_LOAD[1] + u // 2), proj_unit[u % 2]
            else:
                w = UNIT
                slot, buf = slot_at(FIRST_LOAD[2] - 2 + u // 2), out_unit[u]
            return [buf[:, 0, 0:w], buf[:, 1, 0:w], slot[:, (u % 2) * w:(u % 2 + 1) * w]]

        def tile_end(first, turn):
            first(0)
            first(1)
            first(2)
            turn(0)
            first(3)
            turn(1)
            turn(2)
            turn(3)

        def turn_bank(j, i, f):
            return bank(("wo", f, i)) if j == 1 else PS[:, i if f else 4 + i, :]

        @block.sync
        def _(sp):
            sp.dma_start(consts[:, :], a["consts"]).then_inc(consts_loaded.sem, 16)
            sp.dma_start(arena[:, 0:len(MASKS) * P], a["masks"]).then_inc(consts_loaded.sem, 16)
            sp.dma_start(x_tok[:, :, :], a["x"].rearrange("b (t p) d -> p (b t) d", p=P)).then_inc(x_loaded.sem, 16)

            def wait_slot_free(l, n):
                o = n - RING
                if o < 0:
                    l, o = l - 1, o + LAYER_LOADS
                if FIRST_LOAD[1] <= o < FIRST_LOAD[2]:
                    m = o - FIRST_LOAD[1]
                    if m < len(PROJ_LOADS):
                        sp.wait_ge(*unit_lo.at(l, FIRST_UNIT[1] + 2 * m + 2))
                    elif m < len(PROJ_LOADS) + 2:
                        sp.wait_ge(*filled(l, ("hid", m - len(PROJ_LOADS))))
                    else:
                        sp.wait_ge(*unit_lo.at(l, FIRST_UNIT[2] + 2 * (m - len(PROJ_LOADS) - 2) + 2))
                    sp.sem_inc(waits_taken.sem, 1)
                    return
                w = int(o >= FIRST_LOAD[2])
                m = o - FIRST_LOAD[2 * w]
                u = 2 * m + 2 if m < GU_LOADS else min(FC + 2 * (m - GU_LOADS) + 2, FFN_UNITS)
                sp.wait_ge(*unit_lo.at(l, FIRST_UNIT[3 * w] + u))

            def load_gate_up(l, w, g, s):
                gu = a["gu"][w][l].rearrange("(k p) c -> p k c", p=P)
                dst = ring[:, s, :].rearrange("p (k c) -> p k c", k=KD)
                for half in range(2):
                    sp.dma_start(dst[:, :, half * GU_W:(half + 1) * GU_W],
                                 gu[:, :, bass.ds(g * GU_W + half * DFF, GU_W)]).then_inc(slot_loaded[s].sem, 16)

            def ffn_loads(l, w):
                first = FIRST_LOAD[2 * w]
                for g in range(RING):
                    wait_slot_free(l, first + g)
                    load_gate_up(l, w, g, (first + g) % RING)
                with sp.Fori(0, 4) as it:
                    for s in range(RING):
                        sp.wait_ge(*unit_lo.at(l, it * (2 * RING) + (FIRST_UNIT[3 * w] + 2 * s + 2)))
                        load_gate_up(l, w, it * RING + (RING + s), (first + s) % RING)
                g = GU_LOADS - 1
                wait_slot_free(l, first + g)
                load_gate_up(l, w, g, (first + g) % RING)
                for idx, (f0, f1) in enumerate(DOWN_LOADS):
                    n = first + GU_LOADS + idx
                    wait_slot_free(l, n)
                    dst = ring[:, n % RING, 0:(f1 - f0) * DM].rearrange("p (f c) -> p f c", c=DM)
                    src = a["down"][w][l].rearrange("(f p) c -> p f c", p=P)[:, f0:f1, :]
                    sp.dma_start(dst, src).then_inc(slot_loaded[n % RING].sem, 32)

            def mixer_loads(l):
                n = FIRST_LOAD[1]
                for c0, c1 in PROJ_LOADS:
                    wait_slot_free(l, n)
                    dst = ring[:, n % RING, 0:KD * (c1 - c0)].rearrange("p (k c) -> p k c", k=KD)
                    sp.dma_start(dst, a["w_in"][l].rearrange("(k p) c -> p k c", p=P)[:, :, c0:c1]) \
                        .then_inc(slot_loaded[n % RING].sem, 32)
                    n += 1
                for w1 in (a["cmp_k_w1"], a["cmp_v_w1"]):
                    wait_slot_free(l, n)
                    sp.dma_start(ring[:, n % RING, :].rearrange("p (k c) -> p k c", k=16),
                                 w1[l].rearrange("(k p) c -> p k c", p=P)).then_inc(slot_loaded[n % RING].sem, 32)
                    n += 1
                for half in range(2):
                    wait_slot_free(l, n)
                    sp.dma_start(ring[:, n % RING, :].rearrange("p (k c) -> p k c", k=KD),
                                 a["w_out"][l].rearrange("(k p) c -> p k c", p=P)[:, :, half * 512:half * 512 + 512]) \
                        .then_inc(slot_loaded[n % RING].sem, 32)
                    n += 1

            with sp.Fori(0, DEPTH) as l:
                ffn_loads(l, 0)
                mixer_loads(l)
                ffn_loads(l, 1)
            for i in range(T):
                sp.wait_ge(*x_ready.at(DEPTH - 1, 2 * T + i + 1))
                sp.dma_start(out.rearrange("b (t p) d -> p (b t) d", p=P)[:, i, :], x_tok[:, i, :]) \
                    .then_inc(out_stored.sem, 16)
            sp.wait_ge(out_stored.sem, 16 * T)

        @block.tensor
        def _(pe):
            mm, tr = nc.tensor.matmul, nc.tensor.transpose
            pe.sem_inc(down_ready.sem, down_ready.start)
            pe.wait_ge(consts_loaded.sem, 32)
            pe.wait_ge(consts_cast.sem, 1)

            def turn_tile(l, j, i):
                pe.wait_ge(*x_ready.at(l, T * j + i + 1))
                for f in range(2):
                    b = turn_bank(j, i, f)
                    for c in range(4):
                        k = 4 * f + c
                        ins = tr(b[:, c * P:(c + 1) * P], x_tok[:, i, k * P:(k + 1) * P], ident)
                    ins.then_inc(ln_turned.sem, 1)

            def split_mm(b, lhs, rhs, start, stop):
                mm(b, lhsT=lhs[0], rhs=rhs[0], start=start, stop=False)
                mm(b, lhsT=lhs[0], rhs=rhs[1], start=False, stop=False)
                return mm(b, lhsT=lhs[1], rhs=rhs[0], start=False, stop=stop)

            def ffn(l, w):
                pe.wait_ge(*turned_lo.at(l, 16 * w))
                pe.sem_inc(waits_taken.sem, 1)

                def gate_up(f, par):
                    pe.wait_ge(*unit_lo.at(l, FIRST_UNIT[3 * w] + 1 + f))
                    pe.wait_ge(*h_ready.at(l, w * FC - 1 + f))
                    hi, lo, _ = unit_views(3 * w, par)
                    for kind in range(2):
                        for k in range(KD):
                            ins = split_mm(PS[:, 2 * kind + par, :], (hi[:, k, kind, :], lo[:, k, kind, :]),
                                           (xTh[:, k, :], xTl[:, k, :]), k == 0, k == KD - 1)
                    ins.then_inc(gu_ready.sem, 1)

                with pe.Fori(0, FC // 2) as it:
                    for par in range(2):
                        gate_up(it * 2 + par, par)

                def down(d, i, half, f):
                    hi, lo, _ = unit_views(3 * w, FC + d)
                    c = (f % 2) * DM + half * 512
                    return split_mm(PS[:, i if half else 4 + i, :],
                                    (hh[:, f % 4, i * P:(i + 1) * P], hl[:, f % 4, i * P:(i + 1) * P]),
                                    (hi[:, c:c + 512], lo[:, c:c + 512]), f == 0, f == FC - 1)

                for d in range(DOWN_UNITS - 2):
                    pe.wait_ge(*unit_lo.at(l, FIRST_UNIT[3 * w] + FC + d + 1))
                    pe.wait_ge(*h_lo.at(l, w * DOWN_UNITS + d + 1))
                    for half in range(2):
                        if d == 0 and half:
                            pe.wait_ge(*h_ready.at(l, w * FC + FC))
                        for f in (2 * d, 2 * d + 1):
                            for i in range(T):
                                ins = down(d, i, half, f)
                    ins.then_inc(down_used.sem, 1)
                pe.wait_ge(*unit_lo.at(l, FIRST_UNIT[3 * w] + FFN_UNITS))
                pe.wait_ge(*h_lo.at(l, (w + 1) * DOWN_UNITS))

                def last_chunks(i):
                    for half in range(2):
                        for f in range(FC - 4, FC):
                            ins = down(f // 2, i, half, f)
                    ins.then_inc(down_ready.sem, 1)

                tile_end(last_chunks, lambda i: turn_tile(l, 2 * w, i))

            def mixer(l):
                pe.wait_ge(*turned_lo.at(l, 8))
                nxt = [0]

                def fill(*key, narrow=False):
                    q = number[key]
                    assert q == nxt[0], (key, items[nxt[0]])
                    nxt[0] += 1
                    if narrow:
                        pe.sem_inc(waits_taken.sem, 1)
                    if q >= 8:
                        pe.wait_ge(*drained(l, items[q - 8][0]))
                    if narrow:
                        pe.sem_inc(waits_taken.sem, 1)
                    return PS[:, q % 8, :]

                def done(ins):
                    ins.then_inc(bank_filled.sem, 1)

                pe.wait_ge(*params_loaded.at(l, 16 * PARAM_DMAS))
                b = fill("par", narrow=True)
                done(tr(b[:, 0:PARAM_ROWS], stage[0:PARAM_ROWS, :], ident[0:PARAM_ROWS, 0:PARAM_ROWS]))
                for g in range(len(PROJ_LOADS)):
                    w = PROJ_LOADS[g][1] - PROJ_LOADS[g][0]
                    banks_ = [fill("proj", m) for m in proj_items(g)]
                    for kh in range(2):
                        pe.wait_ge(*unit_lo.at(l, FIRST_UNIT[1] + 2 * g + kh + 1))
                        hi, lo, _ = unit_views(1, 2 * g + kh)
                        wv = [e.rearrange("p (k c) -> p k c", k=4) for e in (hi, lo)]
                        for i, b in enumerate(banks_):
                            for k in range(4):
                                x_, s_ = (xTh[:, 4 * kh + k, :], xTl[:, 4 * kh + k, :]), slice(i * P, (i + 1) * P)
                                if g < 2:
                                    ins = split_mm(b, [e[:, k, s_] for e in wv], x_, kh + k == 0, kh * k == 3)
                                else:
                                    ins = split_mm(b[:, 0:w], [e[:, s_] for e in x_], [e[:, k, :] for e in wv],
                                                   kh + k == 0, kh * k == 3)
                            if kh:
                                done(ins)
                        if not kh:
                            ins.then_inc(proj_used.sem, 1)

                def turn_heads(b, src, width):
                    for i in range(T):
                        ins = tr(b[0:width, i * P:(i + 1) * P], src(i), ident)
                    return ins

                pe.wait_ge(*nsa_rotated.at(l, 1))
                for s in range(6):
                    c = (C_NQ + HD * s if s < 4 else C_NKC + 128 * (s - 3)) - GDN_W
                    b = fill("trn", s, narrow=True)
                    done(turn_heads(b, lambda i: h_tok[:, i, c:c + HD], HD))
                pe.wait_ge(*dup_ready.at(l, 1))
                for s in range(2):
                    b = fill("dup", s)
                    done(turn_heads(b, lambda i: dup[:, s, i, :], P))
                for s in range(2):
                    n = FIRST_LOAD[1] + len(PROJ_LOADS) + s
                    pe.wait_ge(*load_arrived(l, n))
                    pe.wait_ge(*blocks_ready.at(l, s + 1))
                    b = fill("hid", s)
                    wv = slot_at(n).rearrange("p (k c) -> p k c", k=16)
                    for f in range(2):
                        for k in range(16):
                            ins = mm(b[:, f * 32:f * 32 + NCMP], lhsT=wv[:, k, f * P:(f + 1) * P],
                                     rhs=blk[:, s, k, :], start=k == 0, stop=k == 15)
                    done(ins)
                pe.wait_ge(*drained(l, ("hid", 1)))
                b = fill("kcmp", narrow=True)
                for f in range(2):
                    ins = mm(b[0:HD, 0:NCMP], lhsT=w2[:, 0, f, :], rhs=hid[:, 0, f, 0:NCMP], start=f == 0, stop=f == 1)
                done(ins)
                b = fill("vcmp", narrow=True)
                for f in range(2):
                    ins = mm(b[0:NCMP, 0:HD], lhsT=hid[:, 1, f, 0:NCMP], rhs=w2[:, 1, f, :], start=f == 0, stop=f == 1)
                done(ins)
                pe.wait_ge(*drained(l, ("kcmp",)))
                b = fill("cs")
                for i in range(T):
                    for h in range(H):
                        c = (i * H + h) * 32
                        ins = mm(b[:, c:c + NCMP], lhsT=nsaT[0:HD, h, i * P:(i + 1) * P],
                                 rhs=kcmpT[0:HD, 0:NCMP], start=True, stop=True)
                done(ins)
                pe.wait_ge(*cmp_probs.at(l, 1))
                for i in range(T):
                    b = fill("cpT", i, narrow=True)
                    for h in range(H):
                        ins = tr(b[0:NCMP, h * P:(h + 1) * P], csb[:, i * H + h, 0:NCMP], ident)
                    done(ins)
                for i in range(T):
                    pe.wait_ge(*drained(l, ("cpT", i)))
                    b = fill("co", i)
                    for h in range(H):
                        ins = mm(b[:, h * HD:(h + 1) * HD], lhsT=cpTs[0:NCMP, i, h * P:(h + 1) * P],
                                 rhs=vcmp[0:NCMP, :], start=True, stop=True)
                    done(ins)

                def v_col(u):
                    if u < 2 * H:
                        return (C_NVS, C_NVW)[u % 2] - GDN_W
                    return C_DV + (u - 2 * H) // 2 * HD

                def turn_pair(u):
                    if u < UNITS:
                        h, br = divmod(u - 2 * H, 2)
                        cq, ck, w = (C_DQ1, C_DQ2)[br] + DQK * h, (C_DK1, C_DK2)[br] + DQK * h, DQK
                        s = 2 * (u % 2)
                    else:
                        h = u - UNITS
                        cq, ck, w = C_SQ + HD * h - GDN_W, C_SK + HD * h - GDN_W, HD
                    for name, c in (("trq", cq), ("trk", ck)):
                        b = fill(name, u, narrow=True)
                        done(turn_heads(b, lambda i: h_tok[:, i, c:c + w], w))

                def scores(u, i):
                    w = (i + 1) * P
                    if u < 2 * H:
                        h, br = divmod(u, 2)
                        qT, kT = nsaT[0:HD, h, :], nsaT[0:HD, 4 + br, :]
                    else:
                        s = 2 * (u % 2)
                        qT, kT = pairT[0:DQK, s, :], pairT[0:DQK, s + 1, :]
                        if i == 0:
                            pe.wait_ge(*drained(l, ("trk", u)))
                    b = fill("sc", u, i)
                    mm(b[:, 0:w], lhsT=qT[:, i * P:w], rhs=kT[:, 0:w], start=True, stop=False)
                    done(mm(b[:, i * P:w], lhsT=identb, rhs=mask("causal"), start=False, stop=True))

                def turn_probs(u, i):
                    pe.wait_ge(*drained(l, ("sc", u, i)))
                    b = fill("tp", u, i)
                    for k in range(i + 1):
                        ins = tr(b[:, k * P:(k + 1) * P], prob[:, (T * u + i) % 3, k * P:(k + 1) * P], ident)
                    done(ins)

                def attend(u):
                    pe.wait_ge(*drained(l, ("tp", u, 1)))
                    pe.wait_ge(*drained(l, ("tp", u, 3)))
                    b = fill("pv", u)
                    c = v_col(u)
                    for i in range(T):
                        for k in range(i + 1):
                            ins = mm(b[:, i * HD:(i + 1) * HD], lhsT=probT[:, u % 2, i * (i + 1) // 2 + k, :],
                                     rhs=h_tok[:, k, c:c + HD], start=k == 0, stop=k == i)
                    done(ins)

                for n in range(UNITS * T + 2):
                    u = n // T
                    if n < UNITS * T:
                        scores(u, n % T)
                        if n % T == 1 and 2 * H <= u + 1 < UNITS:
                            if u + 1 == 2 * H:
                                pe.wait_ge(*diff_rotated.at(l, 1))
                            turn_pair(u + 1)
                    if n >= 2:
                        turn_probs(*divmod(n - 2, T))
                        if (n - 2) % T == T - 1:
                            attend((n - 2) // T)

                first = [0, 512, 896, 1152]

                def log_odds(b, h, j, stop):
                    s = 2 * (h % 2)
                    w = SEQ - j * P
                    return mm(b[:, 0:w], lhsT=pairT[0:HD, s + 1, j * P:(j + 1) * P], rhs=pairT[0:HD, s, j * P:SEQ],
                              start=True, stop=stop)

                for m in range(H * T + 2):
                    if m < H * T:
                        h, j = m // T, T - 1 - m % T
                        if m % T == 0:
                            turn_pair(UNITS + h)
                            pe.wait_ge(*drained(l, ("trk", UNITS + h)))
                        b = fill("z", h, j)
                        done(log_odds(b, h, j, True))
                    if m >= 2:
                        h, j = (m - 2) // T, T - 1 - (m - 2) % T
                        w = SEQ - j * P
                        pe.wait_ge(*soft_ready.at(l, m - 1))
                        b = fill("c", h, j)
                        log_odds(b, h, j, False)
                        mm(b[:, 0:w], lhsT=const("negtri"), rhs=soft[:, h % 2, first[j]:first[j] + w],
                           start=False, stop=False)
                        for k in range(j + 1, T):
                            mm(b[:, (k - j) * P:w], lhsT=const("negone"),
                               rhs=soft[:, h % 2, first[k]:first[k] + SEQ - k * P], start=False, stop=False)
                        done(mm(b[:, 0:P], lhsT=identb, rhs=mask("sbneg"), start=False, stop=True))
                        if j == 0:
                            pe.wait_ge(*drained(l, ("c", h, 0)))
                            b = fill("sbo", h)
                            for i in range(T):
                                for k in range(i + 1):
                                    c = first[k] + (i - k) * P
                                    cv = C_SV + HD * h - GDN_W
                                    ins = mm(b[:, i * HD:(i + 1) * HD], lhsT=attT[:, h % 2, c:c + P],
                                             rhs=h_tok[:, k, cv:cv + HD], start=k == 0, stop=k == i)
                            done(ins)

                pe.wait_ge(*conv_silu.at(l, 1))
                for i in range(T):
                    for f in range(2):
                        b = fill("gtok", i, f)
                        for c in range(3):
                            ins = tr(b[:, c * P:(c + 1) * P], conv[:, 3 * f + c, i * P:(i + 1) * P], ident)
                        done(ins)
                pe.wait_ge(*gates_ready.at(l, 1))
                b = fill("G", narrow=True)
                mm(b[:, 0:16], lhsT=const("upto"), rhs=gdec, start=True, stop=True)
                mm(b[:, 16:32], lhsT=const("chunk"), rhs=gdec, start=True, stop=True)
                mm(b[0:64, 32:48], lhsT=const("chunk")[:, 0:64], rhs=gdec, start=True, stop=True)
                done(mm(b[0:64, 48:64], lhsT=const("chunk")[:, 64:128], rhs=gdec, start=True, stop=True))
                pe.wait_ge(*gdn_ready.at(l, 1))
                for i in range(T):
                    for name, src in (("kT", ktok), ("kbT", kb), ("qT", qtok), ("qdT", qd)):
                        b = fill(name, i, narrow=True)
                        for h in range(H):
                            ins = tr(b[0:HD, h * P:(h + 1) * P], src[:, i, h * HD:(h + 1) * HD], ident)
                        done(ins)
                    b = fill("D", i)
                    for h in range(H):
                        n = i * H + h
                        mm(b[:, h * P:(h + 1) * P], lhsT=gdec[:, n:n + 1].to_broadcast([P, P]), rhs=const("upto"),
                           start=True, stop=False)
                        ins = mm(b[:, h * P:(h + 1) * P], lhsT=identb, rhs=mask("gdnneg"), start=False, stop=True)
                    done(ins)
                    for name, other, need in (("KK", kbTb, "kbT"), ("KQ", qTb, "qT")):
                        pe.wait_ge(*drained(l, (need, i)))
                        pe.wait_ge(*drained(l, ("kT", i)))
                        b = fill(name, i)
                        for h in range(H):
                            ins = mm(b[:, h * P:(h + 1) * P], lhsT=kTb[0:HD, h * P:(h + 1) * P],
                                     rhs=other[0:HD, h * P:(h + 1) * P], start=True, stop=True)
                        done(ins)

                def heads(b, lhs, rhs):
                    for h in range(H):
                        s = slice(h * P, (h + 1) * P)
                        ins = mm(b[:, s], lhsT=lhs[:, s], rhs=rhs(h), start=True, stop=True)
                    return ins

                for m in range(LEVELS * T + 1):
                    if m < LEVELS * T:
                        lev, i = divmod(m, T)
                        pe.wait_ge(*level_ready.at(l, m + 1))
                        if lev == 0:
                            b = fill("X0", i)
                            done(heads(b, NL[:, m % 2, :], lambda h: ident))
                        else:
                            pe.wait_ge(*drained(l, ("X0", i) if lev == 1 else ("X", lev - 1, i)))
                            b = fill("T1", lev, i)
                            done(heads(b, NL[:, m % 2, :], lambda h: X[:, i, h * P:(h + 1) * P]))
                    if m - 1 >= T:
                        lev, i = divmod(m - 1, T)
                        t1 = T1[:, (m - 1) % 2, :]
                        pe.wait_ge(*(xt0_ready.at(l, i + 1) if lev == 1 else drained(l, ("XT", lev - 1, i))))
                        pe.wait_ge(*drained(l, ("T1", lev, i)))
                        if lev < LEVELS - 1:
                            b = fill("X", lev, i)
                            done(heads(b, XT[:, i, :], lambda h: t1[:, h * P:(h + 1) * P]))
                        b = fill("XT", lev, i)
                        done(heads(b, t1, lambda h: XT[:, i, h * P:(h + 1) * P]))
                for i in range(T):
                    pe.wait_ge(*drained(l, ("XT", LEVELS - 1, i)))
                    b = fill("wT", i, narrow=True)
                    for h in range(H):
                        ins = mm(b[0:HD, h * P:(h + 1) * P], lhsT=kbG[:, i, h * HD:(h + 1) * HD],
                                 rhs=XT[:, i, h * P:(h + 1) * P], start=True, stop=True)
                    done(ins)
                    b = fill("u", i)
                    for h in range(H):
                        ins = mm(b[:, h * HD:(h + 1) * HD], lhsT=XT[:, i, h * P:(h + 1) * P],
                                 rhs=vtok[:, i, h * HD:(h + 1) * HD], start=True, stop=True)
                    done(ins)
                pe.wait_ge(*drained(l, ("u", T - 1)))
                for n in range(2 * T):
                    i, p = divmod(n, 2)
                    rows = slice(p * CH, (p + 1) * CH)
                    if n:
                        pe.wait_ge(*drained(l, ("S", n - 1)))
                        b = fill("ws", n, narrow=True)
                        for h in range(H):
                            c = h * P + p * CH
                            ins = mm(b[rows, h * HD:(h + 1) * HD], lhsT=wT[0:HD, i, c:c + CH],
                                     rhs=states[0:HD, n, h * HD:(h + 1) * HD], start=True, stop=True)
                        done(ins)
                        pe.wait_ge(*drained(l, ("ws", n)))
                    if n < 2 * T - 1:
                        b = fill("S", n, narrow=True)
                        for h in range(H):
                            ins = mm(b[0:HD, h * HD:(h + 1) * HD], lhsT=kd[rows, i, h * HD:(h + 1) * HD],
                                     rhs=u_new[rows, i, h * HD:(h + 1) * HD], start=True, stop=True)
                        done(ins)
                    if p:
                        if n == 1:
                            pe.wait_ge(*states_clear.at(l, 1))
                        b = fill("o", i, narrow=True)
                        for h in range(H):
                            s = slice(h * HD, (h + 1) * HD)
                            for par in range(2):
                                c = h * P + par * CH
                                mm(b[par * CH:(par + 1) * CH, s], lhsT=qdT[0:HD, i, c:c + CH],
                                   rhs=states[0:HD, 2 * i + par, s], start=h == 0, stop=False, skip_group_check=True)
                            ins = mm(b[:, s], lhsT=intraT[:, i, h * P:(h + 1) * P], rhs=u_new[:, i, s],
                                     start=False, stop=h == H - 1, skip_group_check=True)
                        done(ins)
                pe.wait_ge(*mix_ready.at(l, 2))
                for i in range(T):
                    for f in range(2):
                        b = fill("mt", i, f)
                        for c in range(4):
                            k = 4 * f + c
                            ins = tr(b[:, c * P:(c + 1) * P], mix[:, i, k * P:(k + 1) * P], ident)
                        done(ins)
                pe.wait_ge(*drained(l, ("mt", T - 1, 1)))

                def out_unit_mm(b, i, u):
                    hi, lo, _ = unit_views(2, u)
                    for k in range(4):
                        kk, c = 4 * (u % 2) + k, slice(k * 512, (k + 1) * 512)
                        ins = split_mm(b, (xTh[:, kk, i * P:(i + 1) * P], xTl[:, kk, i * P:(i + 1) * P]),
                                       (hi[:, c], lo[:, c]), kk == 0, kk == KD - 1)
                    return ins

                banks_ = [fill("wo", 0, i) for i in range(T)]
                for u in range(2):
                    pe.wait_ge(*unit_lo.at(l, FIRST_UNIT[2] + u + 1))
                    for i in range(T):
                        ins = out_unit_mm(banks_[i], i, u)
                        if u:
                            done(ins)
                pe.wait_ge(*unit_lo.at(l, FIRST_UNIT[2] + OUT_UNITS))

                def last_half(i):
                    b = fill("wo", 1, i)
                    out_unit_mm(b, i, 2)
                    done(out_unit_mm(b, i, 3))

                tile_end(last_half, lambda i: turn_tile(l, 1, i))
                assert nxt[0] == len(items)

            for i in range(T):
                turn_tile(0, -1, i)
            with pe.Fori(0, DEPTH) as l:
                ffn(l, 0)
                mixer(l)
                ffn(l, 1)

        @block.scalar
        def _(act):
            f_ = nc.scalar.activation
            steps = [0]
            act.wait_ge(consts_cast.sem, 1)

            def split_hi(l, s, u, f=None):
                w = s // 3
                n = u if f is None else f
                if s in (0, 3):
                    if u < FC and f is not None:
                        n0 = FIRST_LOAD[2 * w] + u // 2
                        act.wait_ge(*slot_loaded[n0 % RING].at(l, 32 * (n0 // RING + 1) + (f - u) * 8))
                    else:
                        n0 = FIRST_LOAD[2 * w] + (u // 2 if u < FC else GU_LOADS + (u - FC) // 2)
                        act.wait_ge(*load_arrived(l, n0))
                    if u < 2 and f is None:
                        if w == 0:
                            act.wait_ge(*down_ready.at(l, 0))
                        else:
                            act.wait_ge(*filled(l, ("wo", u, T - 1)))
                    elif u - 2 < FC:
                        act.wait_ge(*gu_ready.at(l, w * FC - 1 + n))
                    else:
                        act.wait_ge(*down_used.at(l, w * (DOWN_UNITS - 2) + u - 1 - FC))
                elif s == 1:
                    act.wait_ge(*load_arrived(l, FIRST_LOAD[1] + u // 2))
                    if u < 2:
                        act.wait_ge(*h_lo.at(l, DOWN_UNITS))
                    elif u % 2:
                        act.wait_ge(*filled(l, ("proj", proj_items(u // 2 - 1)[-1])))
                    else:
                        act.wait_ge(*proj_used.at(l, u // 2))
                else:
                    act.wait_ge(*load_arrived(l, FIRST_LOAD[2] - 2 + u // 2))
                    act.wait_ge(*filled(l, ("o", T - 1) if u else ("gtok", T - 1, 1)))
                hi, _, raw_ = unit_views(s, u)
                nc.scalar.copy(hi, raw_).then_inc(unit_hi.sem, 1)

            def split_h(l, w, d):
                act.wait_ge(*h_ready.at(l, w * FC + 2 * d + 2))
                if d >= 2:
                    act.wait_ge(*down_used.at(l, w * (DOWN_UNITS - 2) + d - 1))
                elif w == 0 and d == 0:
                    act.wait_ge(*down_ready.at(l, 0))
                s = 2 * (d % 2)
                nc.scalar.copy(hh[:, s:s + 2, :], hT[:, 2 * d:2 * d + 2, :]).then_inc(h_hi.sem, 1)

            def norm_std(l, j, i):
                act.wait_ge(*ln_var.at(l, T * j + i + 1))
                f_(lnst[:, i, 14:15], lnst[:, i, 13:14], ACT.Sqrt, bias=epses[:, 0:1]).then_inc(ln_std.sem, 1)

            def turned(l, j, i):
                for f in range(2):
                    act.wait_ge(*ln_turned.at(l, 8 * j + 2 * i + f + 1))
                    nc.scalar.copy(xTh[:, 4 * f:4 * f + 4, i * P:(i + 1) * P],
                                   turn_bank(j, i, f).rearrange("p (k t) -> p k t", k=4)).then_inc(turned_hi.sem, 1)

            def finish(l, j):
                tile_end(lambda i: norm_std(l, j, i), lambda i: turned(l, j, i))

            def ffn(l, w):
                s = 3 * w

                def gate(f, par):
                    act.wait_ge(*h_ready.at(l, w * FC - 1 + f))
                    act.wait_ge(*gu_ready.at(l, w * FC + 1 + f))
                    f_(sil[:, par, :], PS[:, par, :], ACT.Silu).then_inc(silu_ready.sem, 1)

                if w == 0:
                    split_hi(l, s, 0)
                split_hi(l, s, 1)
                gate(0, 0)
                with act.Fori(0, 5) as it:
                    for e in range(4):
                        split_hi(l, s, e + 2, f=it * 4 + (e + 2))
                        if e < 3 or True:
                            gate(it * 4 + (e + 1), (e + 1) % 2)
                for d in range(2):
                    split_h(l, w, d)
                split_hi(l, s, FC)
                gate(FC - 1, (FC - 1) % 2)
                for d in range(1, DOWN_UNITS):
                    split_hi(l, s, FC + d)
                    if d >= 2:
                        split_h(l, w, d)
                if w == 0:
                    split_hi(l, 1, 0)
                    split_hi(l, 1, 1)
                finish(l, 2 * w)

            def mixer(l):
                steps[0] = 0

                def link(ins):
                    steps[0] += 1
                    ins.then_inc(act_done.sem, 1)
                    act.wait_ge(*act_done.at(l, steps[0]))

                def bank_of(*key):
                    act.wait_ge(*filled(l, key))
                    return bank(key)

                def drain_heads(dst, *key, **kw):
                    b = bank_of(*key)
                    f_(dst, b[0:dst.shape[0], 0:dst.shape[1]], ACT.Copy, **kw).then_inc(drained_act.sem, 1)

                act.wait_ge(*drained(l, ("par",)))
                for g in range(len(PROJ_LOADS)):
                    if g + 1 < len(PROJ_LOADS):
                        split_hi(l, 1, 2 * g + 2)
                        split_hi(l, 1, 2 * g + 3)
                    for m in proj_items(g):
                        if m % 2:
                            continue
                        b = bank_of("proj", m)
                        if g < 2:
                            nc.scalar.copy(raw[:, m, 3:515], b).then_inc(drained_act.sem, 1)
                        else:
                            c0, c1 = PROJ_LOADS[g]
                            d = c0 - (GDN_W if c0 >= C_GZ else 0)
                            nc.scalar.copy(h_tok[:, (m - 6) % 4, d:d + c1 - c0], b[:, 0:c1 - c0]) \
                                .then_inc(drained_act.sem, 1)
                act.wait_ge(*conv_done.at(l, 6))
                f_(conv[:, :, :], conv[:, :, :], ACT.Silu).then_inc(conv_silu.sem, 1)
                act.wait_ge(*gates_in.at(l, 1))
                z = C_GZ - GDN_W
                link(f_(siluz[:, :, :], h_tok[:, :, z:z + 256], ACT.Silu))
                link(f_(ab_e, ab_abs, ACT.Exp, scale=-1.0))
                link(f_(ab_ln, ab_e, ACT.Ln, bias=1.0))
                f_(ea, prm[:, 256:260], ACT.Exp)
                f_(lamexp, lamdot, ACT.Exp)
                cb, cg = C_GB - GDN_W, C_GATE - GDN_W
                f_(beta.rearrange("p (t h) -> p t h", t=T), h_tok[:, :, cb:cb + H], ACT.Exp, scale=-1.0)
                f_(gate.rearrange("p (t h) -> p t h", t=T), h_tok[:, :, cg:cg + 12], ACT.Exp,
                   scale=-1.0).then_inc(gates_exp.sem, 1)
                for s in range(6):
                    drain_heads(nsaT[0:HD, s, :], "trn", s)
                for s in range(2):
                    drain_heads(dupT[:, s, :], "dup", s)
                for s in range(2):
                    b = bank_of("hid", s)
                    f_(hid[:, s, :, 0:NCMP], b[:, 0:64].rearrange("p (f c) -> p f c", f=2)[:, :, 0:NCMP],
                       ACT.Silu).then_inc(drained_act.sem, 1)
                act.wait_ge(*cmp_shifted.at(l, 1))
                f_(csb[:, :, 0:NCMP], csb[:, :, 0:NCMP], ACT.Exp).then_inc(cmp_exp.sem, 1)
                for i in range(T):
                    drain_heads(cpTs[0:NCMP, i, :], "cpT", i)
                for n in range(UNITS * T + 2):
                    u, i = divmod(n, T)
                    if n < UNITS * T:
                        w = (i + 1) * P
                        b = bank_of("sc", u, i)
                        act.wait_ge(*row_max.at(l, n + 1))
                        f_(prob[:, n % 3, 0:w], b[:, 0:w], ACT.Exp, bias=nmax[:, n:n + 1],
                           accum_out=rsum[:, n:n + 1]).then_inc(drained_act.sem, 1)
                        if i == 1 and 2 * H <= u + 1 < UNITS:
                            s = 2 * ((u + 1) % 2)
                            drain_heads(pairT[0:DQK, s, :], "trq", u + 1)
                            drain_heads(pairT[0:DQK, s + 1, :], "trk", u + 1)
                    if n >= 2:
                        v, i = divmod(n - 2, T)
                        if i < 2:
                            b = bank_of("tp", v, i)
                            c = i * (i + 1) // 2
                            nc.scalar.copy(probT[:, v % 2, c:c + i + 1, :],
                                           b[:, 0:(i + 1) * P].rearrange("p (n q) -> p n q", q=P)) \
                                .then_inc(drained_act.sem, 1)
                act.wait_ge(*norm_sum.at(l, 1))
                f_(rstd[:, 0:16], ssq[:, 0:16], ACT.Sqrt, bias=epses[:, 1:2], scale=1.0 / HD).then_inc(norm_std_ready.sem, 1)
                first = [0, 512, 896, 1152]
                for m in range(H * T + 2):
                    if m < H * T:
                        h, j = m // T, T - 1 - m % T
                        if m % T == 0:
                            s = 2 * (h % 2)
                            drain_heads(pairT[0:HD, s, :], "trq", UNITS + h, scale=HD ** -0.5)
                            drain_heads(pairT[0:HD, s + 1, :], "trk", UNITS + h)
                        w = SEQ - j * P
                        t = prob[:, m % 3, 0:w]
                        if m >= 3:
                            act.wait_ge(*drained(l, ("z", (m - 3) // T, T - 1 - (m - 3) % T)))
                        b = bank_of("z", h, j)
                        link(f_(t, b[:, 0:w], ACT.Abs))
                        link(f_(t, t, ACT.Exp, scale=-1.0))
                        f_(t, t, ACT.Ln, bias=1.0).then_inc(soft_ln.sem, 1)
                    if m >= 2:
                        h, j = (m - 2) // T, T - 1 - (m - 2) % T
                        w = SEQ - j * P
                        b = bank_of("c", h, j)
                        f_(attT[:, h % 2, first[j]:first[j] + w], b[:, 0:w], ACT.Exp).then_inc(drained_act.sem, 1)
                        if j == 0:
                            b = bank_of("sbo", h)
                            c = 3 * 256 + HD * h
                            nc.scalar.copy(mix[:, :, c:c + HD],
                                           b[:, 0:256].rearrange("p (t c) -> p t c", t=T)).then_inc(drained_act.sem, 1)
                for i in range(T):
                    b = bank_of("gtok", i, 0)
                    nc.scalar.copy(qtok[:, i, :], b[:, 0:256])
                    nc.scalar.copy(ktok[:, i, 0:128], b[:, 256:384]).then_inc(drained_act.sem, 1)
                    b = bank_of("gtok", i, 1)
                    nc.scalar.copy(ktok[:, i, 128:256], b[:, 0:128])
                    nc.scalar.copy(vtok[:, i, :], b[:, 128:384]).then_inc(drained_act.sem, 1)
                act.wait_ge(*norm_sum.at(l, 2))
                f_(rstd, ssq, ACT.Sqrt, bias=epses[:, 1:2]).then_inc(norm_std_ready.sem, 1)
                act.wait_ge(*decays_in.at(l, 1))
                f_(expG, gcol[:, 0:16], ACT.Exp)
                f_(expKd, expKd, ACT.Exp)
                f_(gl[0:64, :], gcol[0:64, 32:64], ACT.Exp).then_inc(decays_exp.sem, 1)
                for i in range(T):
                    drain_heads(kTb[0:HD, :], "kT", i)
                    drain_heads(qTb[0:HD, :], "qT", i)
                    drain_heads(qdT[0:HD, i, :], "qdT", i)
                    b = bank_of("D", i)
                    if i:
                        act.wait_ge(*drained(l, ("KQ", i - 1)))
                    for h in range(H):
                        s = slice(h * P, (h + 1) * P)
                        n = i * H + h
                        ins = f_(Dm[:, s], b[:, s], ACT.Exp, bias=negG[:, n:n + 1])
                    ins.then_inc(drained_act.sem, 1)
                for m in range(T, LEVELS * T):
                    lev, i = divmod(m, T)
                    drain_heads(T1[:, m % 2, :], "T1", lev, i)
                split_hi(l, 2, 0)
                for i in range(T):
                    drain_heads(wT[0:HD, i, :], "wT", i)
                    b = bank_of("u", i)
                    nc.scalar.copy(u_new[:, i, :], b[:, 0:256]).then_inc(drained_act.sem, 1)
                for i in range(T):
                    b = bank_of("o", i)
                    nc.scalar.copy(mix[:, i, 256:512], b[:, 0:256]).then_inc(drained_act.sem, 1)
                split_hi(l, 2, 1)
                act.wait_ge(*norm_sum.at(l, 3))
                f_(rstd[:, 0:16], ssq[:, 0:16], ACT.Sqrt, bias=epses[:, 1:2], scale=1.0 / HD).then_inc(norm_std_ready.sem, 1)
                for i in range(T):
                    for f in range(2):
                        b = bank_of("mt", i, f)
                        nc.scalar.copy(xTh[:, 4 * f:4 * f + 4, i * P:(i + 1) * P],
                                       b.rearrange("p (k t) -> p k t", k=4)).then_inc(mix_hi.sem, 1)
                split_hi(l, 2, 2)
                split_hi(l, 2, 3)
                split_hi(l, 3, 0)
                finish(l, 1)
                assert steps[0] == ACT_STEPS, ("ACT_STEPS", steps[0])

            for i in range(T):
                turned(0, -1, i)
            with act.Fori(0, DEPTH) as l:
                ffn(l, 0)
                mixer(l)
                ffn(l, 1)

        @block.vector
        def _(dve):
            v = nc.vector
            tt, ts, stt = v.tensor_tensor, v.tensor_scalar, v.scalar_tensor_tensor
            steps = [0]
            dve.wait_ge(consts_loaded.sem, 32)
            v.memset(epses[:, 0:1], LN_EPS)
            v.memset(epses[:, 1:2], NORM_EPS)
            v.tensor_copy(masks[:, :], arena[:, 0:len(MASKS) * P]).then_inc(consts_cast.sem, 1)
            dve.sem_inc(h_ready.sem, h_ready.start)
            dve.wait_ge(x_loaded.sem, 16)
            dve.sem_inc(x_ready.sem, x_ready.start)
            dve.sem_inc(unit_lo.sem, unit_lo.start)

            def link(l, ins):
                steps[0] += 1
                ins.then_inc(dve_done.sem, 1)
                dve.wait_ge(*dve_done.at(l, steps[0]))

            def add_and_count(l, i, half, b, sem_=None):
                xs = x_tok[:, i, half * 512:(half + 1) * 512]
                ins = stt(out=xs, in0=xs, scalar=ALPHA, in1=b, op0=ALU.mult, op1=ALU.add)
                if sem_ is None:
                    link(l, ins)
                else:
                    ins.then_inc(sem_.sem, 1)
                    dve.wait_ge(*drained(l, ("wo", half, i)))
                link(l, v.bn_stats(lnst[:, i, 6 * half:6 * half + 6], xs))

            def normalise(l, j, i):
                dve.sem_inc(waits_taken.sem, 1)
                link(l, v.bn_aggr(lnst[:, i, 12:14], lnst[:, i, 0:12]))
                ts(lnst[:, i, 13:14], lnst[:, i, 13:14], 1.0, None, ALU.mult).then_inc(ln_var.sem, 1)
                dve.wait_ge(*ln_std.at(l, T * j + i + 1))
                link(l, v.reciprocal(lnst[:, i, 15:16], lnst[:, i, 14:15]))
                xs = x_tok[:, i, :]
                link(l, ts(xs, xs, lnst[:, i, 12:13], lnst[:, i, 15:16], ALU.subtract, ALU.mult))
                dve.wait_ge(*lnp_loaded.at(l, 32 * (j + 1)))
                link(l, tt(xs, xs, lnp[:, 0, :], ALU.mult))
                tt(xs, xs, lnp[:, 1, :], ALU.add).then_inc(x_ready.sem, 1)

            def split_lo(l, s, u, n=None):
                dve.wait_ge(*unit_hi.at(l, (u if n is None else n) + (FIRST_UNIT[s] + 1)))
                hi, lo, raw_ = unit_views(s, u)
                tt(lo, raw_, hi.bitcast(F32), ALU.subtract).then_inc(unit_lo.sem, 1)

            def turned(l, j, i):
                for f in range(2):
                    dve.wait_ge(*turned_hi.at(l, 8 * j + 2 * i + f + 1))
                    tt(xTl[:, 4 * f:4 * f + 4, i * P:(i + 1) * P], turn_bank(j, i, f).rearrange("p (k t) -> p k t", k=4),
                       xTh[:, 4 * f:4 * f + 4, i * P:(i + 1) * P].bitcast(F32), ALU.subtract).then_inc(turned_lo.sem, 1)

            def split_h(l, w, d):
                dve.wait_ge(*h_hi.at(l, w * DOWN_UNITS + d + 1))
                s = 2 * (d % 2)
                tt(hl[:, s:s + 2, :], hT[:, 2 * d:2 * d + 2, :], hh[:, s:s + 2, :].bitcast(F32),
                   ALU.subtract).then_inc(h_lo.sem, 1)

            def ffn(l, w):
                s = 3 * w

                def gated(f, par):
                    dve.wait_ge(*silu_ready.at(l, w * FC + 1 + f))
                    stt(out=hT[:, bass.ds(f, 1), :].rearrange("p f t -> p (f t)"), in0=sil[:, par, :], scalar=0.5,
                        in1=PS[:, 2 + par, :], op0=ALU.mult, op1=ALU.mult).then_inc(h_ready.sem, 1)

                if w == 0:
                    split_lo(l, s, 0)
                split_lo(l, s, 1)
                gated(0, 0)
                with dve.Fori(0, 5) as it:
                    for e in range(4):
                        split_lo(l, s, e + 2, n=it * 4 + (e + 2))
                        gated(it * 4 + (e + 1), (e + 1) % 2)
                for d in range(2):
                    split_h(l, w, d)
                split_lo(l, s, FC)
                gated(FC - 1, (FC - 1) % 2)
                for d in range(1, DOWN_UNITS):
                    split_lo(l, s, FC + d)
                    if d >= 2:
                        split_h(l, w, d)
                if w == 0:
                    split_lo(l, 1, 0)
                    split_lo(l, 1, 1)

                def tile(i):
                    dve.wait_ge(*down_ready.at(l, T * w + i + 1))
                    for half in range(2):
                        add_and_count(l, i, half, PS[:, i if half else 4 + i, :])
                    normalise(l, 2 * w, i)

                tile_end(tile, lambda i: turned(l, 2 * w, i))

            def mixer(l):
                def bank_of(*key):
                    dve.wait_ge(*filled(l, key))
                    return bank(key)

                def drain(ins):
                    ins.then_inc(drained_dve.sem, 1)

                def tiles(x_):
                    return x_.rearrange("p (t c) -> p t c", t=T)

                def over(col, n):
                    return col.unsqueeze(2).broadcast_to([col.shape[0], col.shape[1], n])

                def head_scale(dst, src, colmn):
                    for i in range(T):
                        c = over(colmn[:, i * H:(i + 1) * H], HD)
                        ins = tt(dst[:, i, :].rearrange("p (h d) -> p h d", h=H),
                                 src[:, i, :].rearrange("p (h d) -> p h d", h=H), c, ALU.mult)
                    return ins

                b = bank_of("par")
                v.memset(raw[:, :, 0:3], 0.0)
                drain(v.tensor_copy(parT[:, :], b[:, 0:PARAM_ROWS]))
                dve.wait_ge(*drained(l, ("par",)))
                for g in range(len(PROJ_LOADS)):
                    if g + 1 < len(PROJ_LOADS):
                        split_lo(l, 1, 2 * g + 2)
                        split_lo(l, 1, 2 * g + 3)
                    for m in proj_items(g):
                        if m % 2 == 0:
                            continue
                        b = bank_of("proj", m)
                        if g < 2:
                            drain(v.tensor_copy(raw[:, m, 3:515], b))
                        else:
                            c0, c1 = PROJ_LOADS[g]
                            d = c0 - (GDN_W if c0 >= C_GZ else 0)
                            drain(v.tensor_copy(h_tok[:, (m - 6) % 4, d:d + c1 - c0], b[:, 0:c1 - c0]))
                    for j in ([], [0, 1], [2, 3], [4, 5], [], [], [], [])[g]:
                        dve.wait_ge(*drained(l, ("proj", j)))
                        link(l, ts(conv[:, j, :], raw[:, j, 0:SEQ], parT[:, j:j + 1], None, ALU.mult))
                        for k in range(1, 4):
                            ins = stt(out=conv[:, j, :], in0=raw[:, j, k:k + SEQ], scalar=parT[:, 6 * k + j:6 * k + j + 1],
                                      in1=conv[:, j, :], op0=ALU.mult, op1=ALU.add)
                            if k < 3:
                                link(l, ins)
                        ins.then_inc(conv_done.sem, 1)
                dve.wait_ge(*drained(l, ("proj", 28)))
                dve.wait_ge(*drained(l, ("proj", 29)))
                ca = C_GA - GDN_W
                link(l, tt(tiles(ab_x), h_tok[:, :, ca:ca + H],
                           prm[:, 260:264].unsqueeze(1).broadcast_to([P, T, H]), ALU.add))
                link(l, stt(out=ab_abs, in0=ab_x, scalar=-1.0, in1=ab_x, op0=ALU.mult, op1=ALU.max))
                lam = rinv[:, 0:1]
                prod = prob[:, 2, 0:64]
                link(l, tt(prod, prm[:, 0:64], prm[:, 64:128], ALU.mult))
                v.tensor_reduce(lamdot, prod.rearrange("p (a d) -> p a d", a=2), AX.X, ALU.add).then_inc(gates_in.sem, 1)
                for i in range(T):
                    cq, ck = C_NQ - GDN_W, C_NKC - GDN_W
                    for src, kind, n in ((h_tok[:, i, cq:cq + 256].rearrange("p (n a d) -> p n a d", n=4, a=2), "q", 4),
                                         (h_tok[:, i, ck:ck + 384].rearrange("p (n w) -> p n w", n=3)[:, :, 0:HD]
                                          .rearrange("p n (a d) -> p n a d", a=2), "k", 3)):
                        cos = const("c" + kind)[:, i * 32:(i + 1) * 32].unsqueeze(1).unsqueeze(1)
                        sin = const("s" + kind)[:, i * 64:(i + 1) * 64].rearrange("p (a d) -> p a d", a=2).unsqueeze(1)
                        t0 = prob[:, 0, 0:64 * n].rearrange("p (n a d) -> p n a d", n=n, a=2)
                        t1 = prob[:, 1, 0:64 * n].rearrange("p (n a d) -> p n a d", n=n, a=2)
                        tt(t0, src, cos.broadcast_to([P, n, 2, 32]), ALU.mult)
                        link(l, tt(t1, src[:, :, ::-1, :], sin.broadcast_to([P, n, 2, 32]), ALU.mult))
                        ins = tt(src, t0, t1, ALU.add)
                        if i == T - 1 and kind == "k":
                            ins.then_inc(nsa_rotated.sem, 1)
                        else:
                            link(l, ins)
                dve.wait_ge(*nsa_rotated.at(l, 1))
                for s, c in ((0, C_NKC - GDN_W), (1, C_NVC - GDN_W)):
                    ins = v.tensor_copy(dup[:, s].rearrange("p t (a d) -> p t a d", a=2),
                                        h_tok[:, :, c:c + HD].unsqueeze(2).broadcast_to([P, T, 2, HD]))
                ins.then_inc(dup_ready.sem, 1)
                dve.wait_ge(*gates_exp.at(l, 1))
                for s in (beta, gate):
                    link(l, ts(s, s, 1.0, None, ALU.add))
                    link(l, v.reciprocal(s, s))
                link(l, stt(out=ab_ln, in0=ab_x, scalar=0.0, in1=ab_ln, op0=ALU.max, op1=ALU.add))
                link(l, stt(out=tiles(gdec), in0=tiles(ab_ln), scalar=-1.0,
                            in1=ea.unsqueeze(1).broadcast_to([P, T, H]), op0=ALU.mult, op1=ALU.mult))
                link(l, tt(lam, lamexp[:, 1:2], lamexp[:, 0:1], ALU.subtract))
                tt(neglam, lam, prm[:, 264:265], ALU.subtract).then_inc(gates_ready.sem, 1)
                for s in range(2):
                    dve.wait_ge(*drained(l, ("dup", s)))
                    for r in range(2):
                        rows = slice(HD * r, HD * (r + 1))
                        src = dupT[rows, s, :].rearrange("p (c q) -> p q c", q=16)
                        for e in range(2):
                            pe_ = over(parT[rows, 24 + 16 * s + 8 * e:24 + 16 * s + 8 * e + 8], NCMP)
                            ins = tt(blk[rows, s, 8 * e:8 * e + 8, :], src[:, r::2, e:e + NCMP], pe_, ALU.add)
                            if r == 0 or e == 0:
                                link(l, ins)
                    ins.then_inc(blocks_ready.sem, 1)
                b = bank_of("kcmp")
                drain(v.tensor_copy(kcmpT[0:HD, 0:NCMP], b[0:HD, 0:NCMP]))
                b = bank_of("vcmp")
                drain(v.tensor_copy(vcmp[0:NCMP, :], b[0:NCMP, 0:HD]))
                b = bank_of("cs")
                cn = csb[:, :, 0:NCMP]

                def by_tile(x_):
                    return x_.rearrange("p (t h) c -> p t h c", t=T)

                def tile_mask(name):
                    return tiles(const(name)).unsqueeze(2).broadcast_to([P, T, H, 32])[:, :, :, 0:NCMP]

                drain(tt(by_tile(cn), by_tile(b.rearrange("p (n c) -> p n c", c=32)[:, :, 0:NCMP]),
                         tile_mask("cneg"), ALU.add))
                dve.wait_ge(*drained(l, ("cs",)))
                link(l, v.tensor_reduce(cmx, cn, AX.X, ALU.max))
                tt(cn, cn, over(cmx, NCMP), ALU.subtract).then_inc(cmp_shifted.sem, 1)
                dve.wait_ge(*cmp_exp.at(l, 1))
                link(l, v.tensor_reduce(cmx, cn, AX.X, ALU.add))
                link(l, v.reciprocal(cmx, cmx))
                link(l, tt(cn, cn, over(cmx, NCMP), ALU.mult))
                tt(by_tile(cn), by_tile(cn), tile_mask("c01"), ALU.mult).then_inc(cmp_probs.sem, 1)
                gates = tiles(gate).rearrange("p t (h b) -> p t h b", b=3)
                for i in range(T):
                    b = bank_of("co", i)
                    drain(tt(mix[:, i, 512:768].rearrange("p (h d) -> p h d", h=H),
                             b[:, 0:256].rearrange("p (h d) -> p h d", h=H), over(gates[:, i, :, 0], HD), ALU.mult))
                dve.wait_ge(*drained(l, ("co", T - 1)))
                for n in range(UNITS * T + 2):
                    if n < UNITS * T:
                        u, i = divmod(n, T)
                        b = bank_of("sc", u, i)
                        v.tensor_reduce(nmax[:, n:n + 1], b[:, 0:(i + 1) * P], AX.X, ALU.max,
                                        negate=True).then_inc(row_max.sem, 1)
                    if n >= 2:
                        u, i = divmod(n - 2, T)
                        if i >= 2:
                            b = bank_of("tp", u, i)
                            c = i * (i + 1) // 2
                            drain(v.tensor_copy(probT[:, u % 2, c:c + i + 1, :],
                                                b[:, 0:(i + 1) * P].rearrange("p (n q) -> p n q", q=P)))
                        if i == T - 1:
                            b = bank_of("pv", u)
                            pv = tiles(b[:, 0:256])
                            r = rinv[:, 0:T]
                            link(l, v.reciprocal(r, rsum[:, T * u:T * u + T]))
                            if u < 2 * H:
                                h, br = divmod(u, 2)
                                c = 512 + HD * h
                                link(l, tt(r, r, gates[:, :, h, 1 + br], ALU.mult))
                            else:
                                h, br = divmod(u - 2 * H, 2)
                                c = HD * h
                                if br:
                                    link(l, ts(r, r, neglam, None, ALU.mult))
                            dst = mix[:, :, c:c + HD]
                            if u >= 2 * H and br == 0:
                                drain(tt(dst, pv, over(r, HD), ALU.mult))
                                dve.wait_ge(*drained(l, ("pv", u)))
                            else:
                                drain(tt(tmpo, pv, over(r, HD), ALU.mult))
                                dve.wait_ge(*drained(l, ("pv", u)))
                                link(l, tt(dst, dst, tmpo, ALU.add))

                def sums_of_squares(dst, src, tmp, last):
                    for i in range(T):
                        ins = tt(tmp[:, i, :], src[:, i, :], src[:, i, :], ALU.mult)
                    link(l, ins)
                    for i in range(T):
                        ins = v.tensor_reduce(dst[:, i * H:(i + 1) * H], tmp[:, i, :].rearrange("p (h d) -> p h d", h=H),
                                              AX.X, ALU.add)
                    if last:
                        ins.then_inc(norm_sum.sem, 1)
                    else:
                        link(l, ins)

                def gain(dst, g):
                    for i in range(T):
                        d = dst[:, i, :].rearrange("p (h d) -> p h d", h=H)
                        ins = tt(d, d, g.unsqueeze(1).broadcast_to([P, H, HD]), ALU.mult)
                    return ins

                dmix = mix[:, :, 0:256]
                sums_of_squares(ssq[:, 0:16], dmix, tmpl, True)
                link(l, ts(prm[:, 128:192], prm[:, 128:192], prm[:, 265:266], None, ALU.mult))
                dve.wait_ge(*norm_std_ready.at(l, 1))
                link(l, v.reciprocal(rstd[:, 0:16], rstd[:, 0:16]))
                link(l, head_scale(dmix, dmix, rstd[:, 0:16]))
                gain(dmix, prm[:, 128:192]).then_inc(mix_ready.sem, 1)
                first = [0, 512, 896, 1152]
                for m in range(H * T):
                    h, j = m // T, T - 1 - m % T
                    w = SEQ - j * P
                    dve.wait_ge(*soft_ln.at(l, m + 1))
                    b = bank_of("z", h, j)
                    drain(stt(out=soft[:, h % 2, first[j]:first[j] + w], in0=b[:, 0:w], scalar=0.0,
                              in1=prob[:, m % 3, 0:w], op0=ALU.max, op1=ALU.add))
                    dve.wait_ge(*drained(l, ("z", h, j)))
                    d = soft[:, h % 2, first[j]:first[j] + P]
                    tt(d, d, const("sb01"), ALU.mult).then_inc(soft_ready.sem, 1)
                dve.wait_ge(*drained(l, ("gtok", T - 1, 1)))
                sums_of_squares(ssq[:, 0:16], qtok, kb, False)
                sums_of_squares(ssq[:, 16:32], ktok, kd, True)
                b = bank_of("G")
                v.tensor_copy(gcol[:, 0:32], b[:, 0:32])
                drain(v.tensor_copy(gcol[0:64, 32:64], b[0:64, 32:64]))
                dve.wait_ge(*drained(l, ("G",)))
                ts(negG, gcol[:, 0:16], -1.0, None, ALU.mult)
                tt(expKd, gcol[:, 16:32], gcol[:, 0:16], ALU.subtract).then_inc(decays_in.sem, 1)
                dve.wait_ge(*norm_std_ready.at(l, 2))
                link(l, v.reciprocal(rstd, rstd))
                link(l, ts(rstd[:, 0:16], rstd[:, 0:16], HD ** -0.5, None, ALU.mult))
                head_scale(qtok, qtok, rstd[:, 0:16])
                link(l, head_scale(ktok, ktok, rstd[:, 16:32]))
                dve.wait_ge(*decays_exp.at(l, 1))
                link(l, tt(betaG, beta, expG, ALU.mult))
                head_scale(kb, ktok, beta)
                head_scale(kbG, ktok, betaG)
                head_scale(vtok, vtok, beta)
                head_scale(qd, qtok, expG)
                head_scale(kd, ktok, expKd).then_inc(gdn_ready.sem, 1)
                for i in range(T):
                    b = bank_of("kbT", i)
                    drain(v.tensor_copy(kbTb[0:HD, :], b[0:HD, :]))
                    b = bank_of("KK", i)
                    dve.wait_ge(*drained(l, ("D", i)))
                    drain(tt(AT[:, i, :], b, Dm, ALU.mult))
                    b = bank_of("KQ", i)
                    drain(tt(intraT[:, i, :], b, Dm, ALU.mult))
                eye = ident.unsqueeze(1).broadcast_to([P, H, P])

                def by_head(x_):
                    return x_.rearrange("p (h c) -> p h c", h=H)

                for m in range(LEVELS * T + 1):
                    if m < T:
                        b = bank_of("X0", m)
                        drain(tt(by_head(X[:, m, :]), by_head(b), eye, ALU.add))
                        tt(by_head(XT[:, m, :]), by_head(NL[:, m % 2, :]), eye, ALU.add).then_inc(xt0_ready.sem, 1)
                    if m - 1 >= T:
                        lev, i = divmod(m - 1, T)
                        if lev < LEVELS - 1:
                            b = bank_of("X", lev, i)
                            drain(tt(X[:, i, :], X[:, i, :], b, ALU.add))
                        b = bank_of("XT", lev, i)
                        drain(tt(XT[:, i, :], XT[:, i, :], b, ALU.add))
                v.memset(states[0:HD, 0, :], 0.0).then_inc(states_clear.sem, 1)
                split_lo(l, 2, 0)
                for n in range(2 * T):
                    i, p = divmod(n, 2)
                    rows = slice(p * CH, (p + 1) * CH)
                    if n:
                        b = bank_of("ws", n)
                        drain(tt(u_new[rows, i, :], u_new[rows, i, :], b[rows, 0:256], ALU.subtract))
                    if n < 2 * T - 1:
                        b = bank_of("S", n)
                        if n == 0:
                            drain(v.tensor_copy(states[0:HD, 1, :], b[0:HD, 0:256]))
                        else:
                            drain(tt(states[0:HD, n + 1, :], sg[0:HD, :], b[0:HD, 0:256], ALU.add))
                        dve.wait_ge(*drained(l, ("S", n)))
                        if n < 2 * T - 2:
                            i2, p2 = divmod(n + 1, 2)
                            c = p2 * 16 + i2 * H
                            link(l, tt(sg[0:HD, :].rearrange("p (h d) -> p h d", h=H),
                                       states[0:HD, n + 1, :].rearrange("p (h d) -> p h d", h=H),
                                       over(gl[0:HD, c:c + H], HD), ALU.mult))
                gmix = mix[:, :, 256:512]
                dve.wait_ge(*drained(l, ("o", T - 1)))
                sums_of_squares(ssq[:, 0:16], gmix, X[:, :, 0:256], True)
                split_lo(l, 2, 1)
                dve.wait_ge(*norm_std_ready.at(l, 3))
                link(l, v.reciprocal(rstd[:, 0:16], rstd[:, 0:16]))
                link(l, head_scale(gmix, gmix, rstd[:, 0:16]))
                link(l, gain(gmix, prm[:, 192:256]))
                tt(gmix, gmix, siluz, ALU.mult).then_inc(mix_ready.sem, 1)
                for i in range(T):
                    for f in range(2):
                        dve.wait_ge(*mix_hi.at(l, 2 * i + f + 1))
                        s = slice(i * P, (i + 1) * P)
                        drain(tt(xTl[:, 4 * f:4 * f + 4, s], bank(("mt", i, f)).rearrange("p (k t) -> p k t", k=4),
                                 xTh[:, 4 * f:4 * f + 4, s].bitcast(F32), ALU.subtract))
                split_lo(l, 2, 2)
                split_lo(l, 2, 3)
                for i in range(T):
                    add_and_count(l, i, 0, bank_of("wo", 0, i), drained_dve)
                split_lo(l, 3, 0)

                def tile(i):
                    add_and_count(l, i, 1, bank_of("wo", 1, i), drained_dve)
                    normalise(l, 1, i)

                tile_end(tile, lambda i: turned(l, 1, i))

            for i in range(T):
                turned(0, -1, i)
            with dve.Fori(0, DEPTH) as l:
                steps[0] = 0
                ffn(l, 0)
                mixer(l)
                ffn(l, 1)
                assert steps[0] == DVE_STEPS, ("DVE_STEPS", steps[0])

        @block.gpsimd
        def _(pool):
            g = nc.gpsimd
            steps = [0]
            pool.wait_ge(consts_cast.sem, 1)

            def link(l, ins):
                steps[0] += 1
                ins.then_inc(pool_done.sem, 1)
                pool.wait_ge(*pool_done.at(l, steps[0]))

            def load_norm(l, j):
                pool.sem_inc(waits_taken.sem, 1)
                for n, p_ in enumerate(a["ln"][j]):
                    g.dma_start(lnp[:, n, :], p_[bass.ds(l, 1), :].broadcast_to([P, DM])).then_inc(lnp_loaded.sem, 16)
                pool.wait_ge(*lnp_loaded.at(l, 32 * (j + 1)))

            with pool.Fori(0, DEPTH) as l:
                steps[0] = 0
                pool.wait_ge(*x_ready.at(l, 0))
                at = 0
                for name, w in (("lam_q1", 32), ("lam_q2", 32), ("lam_k1", 32), ("lam_k2", 32), ("subln", 64),
                                ("gdn_g", 64), ("a_log", 4), ("dt", 4), ("lam0", 2)):
                    g.dma_start(prm[:, at:at + w], a[name][bass.ds(l, 1), :].broadcast_to([P, w])) \
                        .then_inc(params_loaded.sem, 16)
                    at += w
                g.dma_start(stage[0:24, :], a["conv_w"][l].rearrange("k (c p) -> (k c) p", p=P)) \
                    .then_inc(params_loaded.sem, 16)
                g.dma_start(stage[24:40, :], a["pe_k"][l].rearrange("(k r) d -> k (r d)", r=2)) \
                    .then_inc(params_loaded.sem, 16)
                g.dma_start(stage[40:56, :], a["pe_v"][l].rearrange("(k r) d -> k (r d)", r=2)) \
                    .then_inc(params_loaded.sem, 16)
                for s, name in enumerate(("cmp_k_w2", "cmp_v_w2")):
                    g.dma_start(w2[:, s], a[name][l].rearrange("(f p) d -> p f d", p=P)) \
                        .then_inc(params_loaded.sem, 16)
                pool.wait_ge(*params_loaded.at(l, 16 * PARAM_DMAS))
                load_norm(l, 0)
                pool.wait_ge(*drained(l, ("proj", 28)))
                pool.wait_ge(*drained(l, ("proj", 29)))
                for i in range(T):
                    for c0, kind in ((C_DQ1, "q"), (C_DK1, "k")):
                        src = h_tok[:, i, c0:c0 + 256].rearrange("p (n a d) -> p n a d", n=8, a=2)
                        cos = const("dc" + kind)[:, i * 16:(i + 1) * 16].unsqueeze(1).unsqueeze(1)
                        sin = const("ds" + kind)[:, i * 32:(i + 1) * 32].rearrange("p (a d) -> p a d", a=2).unsqueeze(1)
                        t0 = ptmp[:, 0, :].rearrange("p (n a d) -> p n a d", n=8, a=2)
                        t1 = ptmp[:, 1, :].rearrange("p (n a d) -> p n a d", n=8, a=2)
                        g.tensor_tensor(t0, src, cos.broadcast_to([P, 8, 2, 16]), ALU.mult)
                        link(l, g.tensor_tensor(t1, src[:, :, ::-1, :], sin.broadcast_to([P, 8, 2, 16]), ALU.mult))
                        ins = g.tensor_tensor(src, t0, t1, ALU.add)
                        if i == T - 1 and kind == "k":
                            ins.then_inc(diff_rotated.sem, 1)
                        else:
                            link(l, ins)
                pool.wait_ge(*x_ready.at(l, T))
                load_norm(l, 1)
                for m in range(LEVELS * T):
                    lev, i = divmod(m, T)
                    if m < T:
                        pool.wait_ge(*drained(l, ("KK", i)))
                    if m >= 2:
                        plev, pi = divmod(m - 2, T)
                        pool.wait_ge(*filled(l, ("X0", pi) if plev == 0 else ("T1", plev, pi)))
                        if plev == 0:
                            pool.wait_ge(*xt0_ready.at(l, pi + 1))
                    g.tensor_tensor(NL[:, m % 2, :].rearrange("p (h c) -> p h c", h=H),
                                    AT[:, i, :].rearrange("p (h c) -> p h c", h=H),
                                    mask(f"lev{lev}").unsqueeze(1).broadcast_to([P, H, P]), ALU.mult) \
                        .then_inc(level_ready.sem, 1)
                pool.wait_ge(*x_ready.at(l, 2 * T))
                load_norm(l, 2)
                assert steps[0] == POOL_STEPS, ("POOL_STEPS", steps[0])


_OUT = (1, SEQ, DM)


def kernel(x, w_in, w_out, ffn1_w_gu, ffn1_w_down, ffn2_w_gu, ffn2_w_down,
           ln1_g, ln1_b, ln2_g, ln2_b, ln3_g, ln3_b,
           diff_lam_q1, diff_lam_k1, diff_lam_q2, diff_lam_k2, diff_subln_g,
           gdn_conv_w, gdn_a_log, gdn_dt_bias, gdn_norm_g,
           nsa_pe_k, nsa_pe_v, nsa_cmp_k_w1, nsa_cmp_k_w2, nsa_cmp_v_w1, nsa_cmp_v_w2):
    from concourse import bacc
    from concourse.bass_utils import run_bass_kernel_spmd

    tables, masks_, lam0 = constants()
    given = dict(x=x, w_in=w_in, w_out=w_out, gu1=ffn1_w_gu, down1=ffn1_w_down, gu2=ffn2_w_gu, down2=ffn2_w_down,
                 ln1_g=ln1_g, ln1_b=ln1_b, ln2_g=ln2_g, ln2_b=ln2_b, ln3_g=ln3_g, ln3_b=ln3_b,
                 lam_q1=diff_lam_q1, lam_k1=diff_lam_k1, lam_q2=diff_lam_q2, lam_k2=diff_lam_k2,
                 subln=diff_subln_g, conv_w=gdn_conv_w, a_log=gdn_a_log, dt=gdn_dt_bias, gdn_g=gdn_norm_g,
                 pe_k=nsa_pe_k, pe_v=nsa_pe_v, cmp_k_w1=nsa_cmp_k_w1, cmp_k_w2=nsa_cmp_k_w2,
                 cmp_v_w1=nsa_cmp_v_w1, cmp_v_w2=nsa_cmp_v_w2, consts=tables, masks=masks_, lam0=lam0)
    nc = bacc.Bacc("TRN2", target_bir_lowering=False, num_devices=1)
    arrays, aps = {}, {}
    for name, value in given.items():
        arrays[name + "_in"] = np.ascontiguousarray(value)
        aps[name] = nc.dram_tensor(name + "_in", arrays[name + "_in"].shape, F32, kind="ExternalInput").ap()
    aps["gu"] = (aps["gu1"], aps["gu2"])
    aps["down"] = (aps["down1"], aps["down2"])
    aps["ln"] = [(aps[f"ln{j}_g"], aps[f"ln{j}_b"]) for j in (1, 2, 3)]
    y = nc.dram_tensor("y_out", _OUT, F32, kind="ExternalOutput").ap()
    trunk_program(nc, aps, y)
    got = run_bass_kernel_spmd(nc, [arrays], core_ids=[0])
    return got.results[0]["y_out"]
```

```python
import math
from contextlib import ExitStack

import numpy as np
import concourse.bass as bass
from concourse import mybir

F32 = mybir.dt.float32
F32R = mybir.dt.float32r
BF16 = mybir.dt.bfloat16
ALU = mybir.AluOpType
ACT = mybir.ActivationFunctionType
AX = mybir.AxisListType

P = 128
SEQ, DM, DEPTH, DFF = 512, 1024, 2, 2816
T = SEQ // P
KD = DM // P
FC = DFF // P
H, HD, DQK = 4, 64, 32
CH = 64
NCMP = 31
ALPHA = (2 * DEPTH) ** 0.25
LN_EPS, NORM_EPS, NEG = 1e-5, 1e-6, -1e30

C_DQ1, C_DQ2, C_DK1, C_DK2, C_DV = 0, 128, 256, 384, 512
C_GQ, C_GZ, C_GA, C_GB, C_NQ = 768, 1536, 1792, 1796, 1800
C_NKC, C_NVC, C_NVS, C_NVW, C_GATE = 2056, 2120, 2248, 2376, 2440
C_SQ, C_SK, C_SV, C_END = 2452, 2708, 2964, 3220
GDN_W = 3 * H * HD
HW = C_END - GDN_W

GU_W = 256
GU_LOADS = DFF // GU_W
DOWN_LOADS = [(f, min(f + 4, FC)) for f in range(0, FC, 4)]
PROJ_COLS = [768, 1152, C_GZ, C_GZ + 422, C_GZ + 844, C_GZ + 1264, C_END]
PROJ_LOADS = list(zip(PROJ_COLS, PROJ_COLS[1:])) + [(0, 384), (384, 768)]
PROJ_LOADS = [PROJ_LOADS[2]] + PROJ_LOADS[:2] + PROJ_LOADS[3:]
BY_CHANNEL = (1, 2)
RING = 2
SLOT = KD * 2 * GU_W
FFN_LOADS = GU_LOADS + len(DOWN_LOADS)
MIX_LOADS = len(PROJ_LOADS) + 4
LAYER_LOADS = 2 * FFN_LOADS + MIX_LOADS
assert LAYER_LOADS % RING == 0
UNIT = SLOT // 2
DOWN_UNITS = FC // 2
FFN_UNITS = FC + DOWN_UNITS
PROJ_UNITS = 2 * len(PROJ_LOADS)
OUT_UNITS = 4
FIRST_UNIT = (0, FFN_UNITS, FFN_UNITS + PROJ_UNITS, FFN_UNITS + PROJ_UNITS + OUT_UNITS)
LAYER_UNITS = FIRST_UNIT[3] + FFN_UNITS
FIRST_LOAD = (0, FFN_LOADS, FFN_LOADS + MIX_LOADS)

LN_CUT = 384
SLAB = 52704
PARAM_DMAS = 14
ACT_STEPS, DVE_STEPS, POOL_STEPS = 35, 185, 27

UNITS = 2 * H + 2 * H
LEVELS = 6
PARAM_ROWS = 24 + 16 + 16


NSA_STEPS = 2 * H * T
STEPS = [(u, i) for u in range(2 * H) for i in range(T)] + \
        [(2 * H + 2 * h + br, i) for h in range(H) for i in range(T) for br in range(2)]


COMPRESSED = {0: [("kcmp",), ("vcmp",)], 2: [("cs",)], 10: [("cpT", 0), ("cpT", 1)], 11: [("co", 0)],
              12: [("cpT", 2), ("cpT", 3)], 13: [("co", 1)]}


LAG = 3


def turns_after(n):
    if n in (NSA_STEPS - 3, NSA_STEPS - 2):
        u = 2 * H + n - (NSA_STEPS - 3)
        return [(u, "q"), (u, "k"), (u, "kh")]
    h, e = divmod(n - NSA_STEPS, 2 * T)
    if n < NSA_STEPS or e not in (3, 5):
        return []
    if h < H - 1:
        u = 2 * H + 2 * (h + 1) + (e - 3) // 2
        return [(u, "q"), (u, "k"), (u, "kh")]
    return [(UNITS, "q"), (UNITS, "k"), (UNITS, "kh")] if e == 3 else []


def turned_after(n):
    s = n - LAG
    return s if 0 <= s < len(STEPS) and (s < NSA_STEPS or STEPS[s][0] % 2) else None


def attends_after(n):
    g, half = divmod(n - LAG - T, T)
    if 0 <= g < 2 * H and half < 2:
        return g, half
    h, e = divmod(n - NSA_STEPS - 2 * T, 2 * T)
    return (2 * H + h, e - LAG) if 0 <= h < H and e in (LAG, LAG + 1) else None


def mixer_items():
    q = [(("proj", m), ("act", "dve")[m % 2]) for m in range(26)]
    q.insert(T, (("par",), "dve"))
    q += [(("dup", s), "act") for s in range(2)]
    q += [(("proj", m), ("act", "dve")[m % 2]) for m in range(26, 30)]
    q += [(("hid", s), "act") for s in range(2)]
    q += [(("trn", s), ("act", "dve")[s % 2]) for s in range(8)] + [(("hidT",), "act")]

    def turn(u, kind):
        q.append((("tr", u, kind), {"q": "act", "k": "dve", "kh": "act"}[kind]))

    for n in range(len(STEPS) + LAG + 2):
        if n < len(STEPS):
            q.append((("sc", n), "act"))
            for u, kind in turns_after(n):
                turn(u, kind)
            q += [(key, "act" if key in (("cpT", 0), ("cpT", 2)) else "dve") for key in COMPRESSED.get(n, [])]
        if turned_after(n) is not None:
            s = n - LAG
            q.append((("tp", s), "dve" if s < NSA_STEPS and STEPS[s][1] == 2 else "act"))
        g, half = attends_after(n) or (0, 0)
        if half:
            q.append((("pv", g), "dve" if g < 2 * H else "act"))
    for m in range(H * T + 2):
        if m < H * T:
            q.append((("z", m // T, T - 1 - m % T), "dve"))
            if m % T == 2 and m // T + 1 < H:
                for kind in ("q", "k", "kh"):
                    turn(UNITS + m // T + 1, kind)
        if m >= 2:
            h, j = (m - 2) // T, T - 1 - (m - 2) % T
            q.append((("c", h, j), "act"))
            if j == 0:
                q.append((("sbo", h), "act"))
    q += [(("gtok", i, f), "act") for i in range(T) for f in range(2)]
    q.append((("G",), "dve"))
    for i in range(T):
        q += [(("kT", i), "act"), (("kbT", i), "dve"), (("qT", i), "act"), (("qdT", i), "act"),
              (("D", i), "act"), (("KK", i), "dve"), (("KQ", i), "dve")]
    for m in range(LEVELS * T + 1):
        if m < LEVELS * T:
            lev, i = divmod(m, T)
            q.append((("X0", i), "dve") if lev == 0 else (("T1", lev, i), "act"))
        if m - 1 >= T:
            lev, i = divmod(m - 1, T)
            if lev < LEVELS - 1:
                q.append((("X", lev, i), "dve"))
            q.append((("XT", lev, i), "dve"))
    for i in range(T):
        q += [(("wT", i), "act"), (("u", i), "act")]
    for n in range(2 * T):
        if n:
            q.append((("ws", n), "dve"))
        if n % 2 and n >= 3:
            q.append((("o", n // 2 - 1), "act"))
        if n < 2 * T - 1:
            q.append((("S", n), "dve"))
    q.append((("o", T - 1), "act"))
    q += [(("mt", i), "dve") for i in range(T)]
    q += [(("wo", f, i), "dve") for f in range(2) for i in range(T)]
    return q


def const_columns():
    widths = [("ident", 128), ("upto", 128), ("chunk", 128), ("negtri", 128), ("negone", 128),
              ("sb01", 128), ("c01", T * 32), ("cneg", T * 32),
              ("cq", T * 32), ("sq", T * 64), ("ck", T * 32), ("sk", T * 64),
              ("dcq", T * 16), ("dsq", T * 32), ("dck", T * 16), ("dsk", T * 32)]
    at, n = {}, 0
    for name, w in widths:
        at[name] = (n, n + w)
        n += w
    return at, n


MASKS = ["ident", "causal", "sbneg", "gdnneg"] + [f"lev{m}" for m in range(LEVELS)]


def constants():
    at, n = const_columns()
    c = np.zeros((P, n), np.float32)

    def put(name, a):
        c[:, at[name][0]:at[name][1]] = np.asarray(a, np.float32).reshape(P, -1)

    r = np.arange(P)[:, None]
    k = np.arange(P)[None, :]
    same = (r // CH) == (k // CH)
    put("ident", r == k)
    put("upto", (r <= k) & same)
    put("chunk", same)
    put("negtri", -(r >= k).astype(np.float32))
    put("negone", -np.ones((P, P)))
    put("sb01", r < k)
    tok = np.arange(T)[None, :, None] * P + np.arange(P)[:, None, None]
    blk = np.arange(32)[None, None, :]
    seen = (blk < NCMP) & (blk * 16 + 31 <= tok)
    put("c01", seen)
    put("cneg", np.where(seen, 0, NEG))

    def rope(dim, scale):
        inv = (np.float32(10000.0) ** (-np.arange(0, dim, 2, dtype=np.float32) / dim)).astype(np.float32)
        ang = tok.astype(np.float32) * inv[None, None, :]
        cos, sin = np.cos(ang) * scale, np.sin(ang) * scale
        return cos, np.stack([-sin, sin], 2)

    for pre, dim in (("", HD), ("d", DQK)):
        for kind, scale in (("q", np.float32(dim ** -0.5)), ("k", np.float32(1))):
            cos, sin = rope(dim, scale)
            put(pre + "c" + kind, cos)
            put(pre + "s" + kind, sin)
    masks = [r == k, np.where(k > r, NEG, 0), np.where(r < k, 0, NEG),
             np.where((k >= r) & same, 0, NEG)]
    for lev in range(LEVELS):
        b = 2 ** lev
        masks.append(-(((k // b) % 2 == 1) & ((r // b) == (k // b) - 1)).astype(np.float32))
    masks = np.stack([np.asarray(m, np.float32) for m in masks], 1).reshape(P, -1)
    lam = np.zeros((DEPTH, 2), np.float32)
    for layer in range(DEPTH):
        init = 0.8 - 0.6 * math.exp(-0.3 * layer)
        lam[layer] = (init, 1 - init)
    return c, masks, lam


class Signal:

    def __init__(self, sem, per_layer, start=0):
        self.sem, self.per_layer, self.start = sem, per_layer, start

    def at(self, layer, n):
        return self.sem, layer * self.per_layer + (n + self.start)


def trunk_program(nc, a, out):
    items = mixer_items()
    number = {key: n for n, (key, _) in enumerate(items)}
    drainer = {key: who for key, who in items}
    rank, seen = {}, {"act": 0, "dve": 0}
    for key, who in items:
        seen[who] += 1
        rank[key] = seen[who]

    ctx = ExitStack()
    with ctx:
        ctx.enter_context(nc.sbuf_tensor("slab", [P, SLAB], F32))
        slab_at = nc.sbuf_base - 4 * SLAB
        taken = [0]

        def place(name, at, shape, dt):
            return nc.alloc_sbuf_tensor_at(name, [P] + shape, dt, offset=slab_at + 4 * at)

        def sb(name, shape, dt=F32):
            words = int(np.prod(shape[1:])) // (2 if dt == BF16 else 1)
            at = taken[0]
            taken[0] += -(-words // 8) * 8
            assert taken[0] <= SLAB, (name, taken[0])
            return place(name, at, shape[1:], dt)

        def sem(name, per_layer, start=0):
            return Signal(ctx.enter_context(nc.semaphore(name)), per_layer, start)

        cat, cw = const_columns()
        consts = sb("consts", [P, cw])
        masks = sb("masks", [P, len(MASKS) * P], BF16)
        x_tok = sb("x_tok", [P, T, DM])
        xT_at = taken[0]
        xTh = sb("xTh", [P, KD, SEQ], F32R)
        xTl = sb("xTl", [P, KD, SEQ], F32R)
        scratch = place("scratch", xT_at, [2 * KD * SEQ], F32)
        ring = sb("ring", [P, RING, SLOT])
        lnp = sb("lnp", [P, 2, DM])
        small = sb("small", [P, 640])
        prm = sb("prm", [P, 272])
        w2 = sb("w2", [P, 2, 2, HD])
        stage = sb("stage", [P, P])
        parT = sb("parT", [P, PARAM_ROWS])
        ptmp = sb("ptmp", [P, 2, 256])
        epses = sb("epses", [P, 2])
        lnst = sb("lnst", [P, T, 16])
        ARENA = 24656
        arena_at = taken[0]
        arena = sb("arena", [P, ARENA])
        PS = ctx.enter_context(nc.psum_tensor("banks", [P, 8, 512], F32))

        def const(name):
            return consts[:, cat[name][0]:cat[name][1]]

        def mask(name):
            n = MASKS.index(name)
            return masks[:, n * P:(n + 1) * P]

        ident, identb = const("ident"), mask("ident")

        used = [0]

        def cols(n):
            used[0] += n
            assert used[0] <= 640
            return small[:, used[0] - n:used[0]]

        nmax, rsum = cols(64), cols(64)
        rinv = cols(16)
        cmx = cols(16)
        gate = cols(T * 12)
        ab_x, ab_abs, ab_e, ab_ln = cols(16), cols(16), cols(16), cols(16)
        ea = cols(4)
        beta, gdec = cols(16), cols(16)
        gcol = cols(64)
        negG = cols(16)
        expG, expKd, gl, betaG = cols(16), cols(16), cols(32), cols(16)
        lamdot, lamexp, neglam = cols(2), cols(2), cols(1)
        ssq = cols(32)
        rstd = cols(32)

        hT = arena[:, 0:FC * SEQ].rearrange("p (f t) -> p f t", f=FC)
        sil = arena[:, FC * SEQ:FC * SEQ + 2 * SEQ].rearrange("p (b t) -> p b t", b=2)
        hh = place("hh", arena_at + 20480, [4, SEQ], F32R)
        hl = place("hl", arena_at + 20480 + 4 * SEQ, [4, SEQ], F32R)
        ffn_unit = [place(f"ffn_unit{b}", arena_at + 12288 + b * 2 * UNIT, [2, UNIT], F32R) for b in range(2)]
        proj_unit = [place(f"proj_unit{b}", arena_at + b * 8 * 422, [2, 4 * 422], F32R) for b in range(2)]
        out_unit = [place(f"out_unit{n}", arena_at + at, [2, UNIT], F32R)
                    for n, at in enumerate((19456, 4096, 8192, 12288))]
        off = {}

        def area(name, start, n):
            off[name] = start + n
            return arena[:, start:start + n]

        dmix = area("dmix", 0, T * 256).rearrange("p (t c) -> p t c", t=T)
        gmix = area("gmix", off["dmix"], T * 256).rearrange("p (t c) -> p t c", t=T)
        outT = area("mix", off["gmix"], 4 * SEQ).rearrange("p (s t) -> p s t", s=4)
        area("nsaT", off["mix"], 6 * SEQ)
        h_tok = area("h", off["nsaT"], T * HW).rearrange("p (t c) -> p t c", t=T)
        pair0 = off["h"]
        pairT = area("pairT", pair0, 4 * SEQ).rearrange("p (s t) -> p s t", s=4)
        prob = area("prob", off["pairT"], 3 * SEQ).rearrange("p (s t) -> p s t", s=3)
        raw = arena[:, pair0:pair0 + 6 * 515].rearrange("p (j t) -> p j t", j=6)
        conv = area("conv", off["prob"], 6 * SEQ).rearrange("p (j t) -> p j t", j=6)
        siluz = area("siluz", off["conv"], T * 256).rearrange("p (t c) -> p t c", t=T)
        assert off["siluz"] <= ARENA
        nsa_r = place("nsa_r", arena_at + off["mix"], [6, SEQ], F32R)
        win_r = place("win_r", arena_at + off["dmix"], [2, SEQ], F32R)
        diff0_r = place("diff0_r", arena_at, [2, SEQ], F32R)
        pair_r = place("pair_r", arena_at + pair0, [4, SEQ], F32R)

        def stacked(u, kind):
            n = {"q": 0, "k": 1, "kh": 2}[kind]
            if u < 2 * H:
                return nsa_r[:, u // 2, :] if n == 0 else nsa_r[:, 3 + n, :] if u % 2 == 0 else win_r[:, n - 1, :]
            if u < UNITS:
                h = (u - 2 * H) // 2
                if n == 2:
                    return (diff0_r, nsa_r[:, 4:6, :], win_r, nsa_r[:, 4:6, :])[h][:, u % 2, :]
                return (pair_r, nsa_r)[h % 2][:, 2 * (u % 2) + n, :]
            return (pair_r, nsa_r)[(u - UNITS) % 2][:, n, :]

        def stack_rows(u, kind):
            w = DQK if 2 * H <= u < UNITS else HD
            return w if kind == "kh" else 2 * w

        parts = place("parts", xT_at + 4096, [T, 1024], F32R)
        dup = pairT[:, 0:2, :].rearrange("p s (t c) -> p s t c", c=P)
        dupT = prob[:, 0:2, :]
        blk = siluz.rearrange("p t c -> p (t c)")[:, 0:992].rearrange("p (s j c) -> p s j c", s=2, j=16)
        hid_tok = pairT[:, 2, :].rearrange("p (s c) -> p s c", s=2)
        hid = pairT[:, 3, 0:128].rearrange("p (s f c) -> p s f c", s=2, f=2)
        kcmpT = pairT[:, 3, 128:160]
        vcmp = pairT[:, 3, 160:224]
        csb = pairT[:, 2, :].rearrange("p (n c) -> p n c", c=32)
        cpTs = pairT[:, 0:2, :]

        def prob_of(n):
            return prob[:, n % 4, :] if n % 4 < 3 else ptmp.rearrange("p a c -> p (a c)")

        probT = scratch[:, 0:4096].rearrange("p (b k q) -> p b k q", b=2, k=T)
        tmpl = scratch[:, 2816:2816 + 1024].rearrange("p (t c) -> p t c", t=T)
        soft = scratch[:, 0:2560].rearrange("p (b n) -> p b n", b=2)
        attT = [arena[:, off["mix"] + 3 * SEQ:off["mix"] + 3 * SEQ + 1280], scratch[:, 2560:3840]]
        g0 = off["mix"]

        def garea(n):
            nonlocal g0
            g0 += n
            return arena[:, g0 - n:g0]

        states = arena[:, g0:g0 + 2048].rearrange("p (n c) -> p n c", n=8)
        qk_flat, squares_flat = arena[:, g0:g0 + 2048], arena[:, g0 + 3072:g0 + 5120]
        qtok = garea(1024).rearrange("p (t c) -> p t c", t=T)
        ktok = garea(1024).rearrange("p (t c) -> p t c", t=T)
        vtok = garea(1024).rearrange("p (t c) -> p t c", t=T)
        kb = garea(1024).rearrange("p (t c) -> p t c", t=T)
        u_new = kb
        kbG = garea(1024).rearrange("p (t c) -> p t c", t=T)
        qd = garea(1024).rearrange("p (t c) -> p t c", t=T)
        kd = garea(1024).rearrange("p (t c) -> p t c", t=T)
        kTb, kbTb, qTb = garea(512), garea(512), garea(512)
        sg = kTb[:, 0:256]
        qdT = garea(2048).rearrange("p (t c) -> p t c", t=T)
        intraT = garea(2048).rearrange("p (t c) -> p t c", t=T)
        wT = garea(2048).rearrange("p (t c) -> p t c", t=T)
        Dm = garea(512)
        T1 = scratch[:, 4096:5120].rearrange("p (b c) -> p b c", b=2)
        NL = scratch[:, 5120:6144].rearrange("p (b c) -> p b c", b=2)
        X = scratch[:, 6144:8192].rearrange("p (t c) -> p t c", t=T)
        assert g0 <= 19456
        XT = scratch[:, 0:2048].rearrange("p (t c) -> p t c", t=T)
        AT = scratch[:, 2048:4096].rearrange("p (t c) -> p t c", t=T)

        consts_loaded = sem("consts_loaded", 0)
        x_loaded = sem("x_loaded", 0)
        slot_loaded = [sem(f"slot{s}_loaded", 32 * LAYER_LOADS // RING) for s in range(RING)]
        lnp_loaded = sem("lnp_loaded", 3 * 32)
        params_loaded = sem("params_loaded", PARAM_DMAS * 16)
        out_stored = sem("out_stored", 0)
        down_used = sem("down_used", 2 * (DOWN_UNITS - 2))
        proj_used = sem("proj_used", len(PROJ_LOADS))
        ln_turned = sem("ln_turned", 3 * 8, 8)
        gu_ready = sem("gu_ready", 2 * FC)
        down_ready = sem("down_ready", 2 * T, 2 * T)
        bank_filled = sem("bank_filled", len(items))
        act_done = sem("act_done", ACT_STEPS)
        turned_hi = sem("turned_hi", 3 * 8, 8)
        unit_hi = sem("unit_hi", LAYER_UNITS)
        h_hi = sem("h_hi", 2 * DOWN_UNITS)
        mix_hi = sem("mix_hi", T)
        outT_hi = sem("outT_hi", 1)
        tok_hi_ready = sem("tok_hi_ready", 3)
        silu_ready = sem("silu_ready", 2 * FC)
        ln_std = sem("ln_std", 3 * T)
        drained_act = sem("drained_act", seen["act"])
        conv_silu = sem("conv_silu", 1)
        gates_exp = sem("gates_exp", 1)
        cmp_exp = sem("cmp_exp", 1)
        soft_ln = sem("soft_ln", H * T)
        norm_std_ready = sem("norm_std_ready", 3)
        decays_exp = sem("decays_exp", 1)
        dve_done = sem("dve_done", DVE_STEPS)
        consts_cast = sem("consts_cast", 0)
        x_ready = sem("x_ready", 3 * T, T)
        h_ready = sem("h_ready", 2 * FC, 2)
        turned_lo = sem("turned_lo", 3 * 8, 8)
        unit_lo = sem("unit_lo", LAYER_UNITS, LAYER_UNITS)
        h_lo = sem("h_lo", 2 * DOWN_UNITS)
        ln_var = sem("ln_var", 3 * T)
        drained_dve = sem("drained_dve", seen["dve"])
        conv_done = sem("conv_done", 6)
        gates_in = sem("gates_in", 1)
        nsa_rotated = sem("nsa_rotated", 1)
        blocks_ready = sem("blocks_ready", 2)
        cmp_shifted = sem("cmp_shifted", 1)
        cmp_probs = sem("cmp_probs", 1)
        row_max = sem("row_max", len(STEPS))
        probs_combined = sem("probs_combined", H * T)
        sum_inverted = sem("sum_inverted", NSA_STEPS)
        tok_lo_ready = sem("tok_lo_ready", 3)
        outT_lo = sem("outT_lo", 1)
        soft_ready = sem("soft_ready", H * T)
        norm_sum = sem("norm_sum", 3)
        dup_ready = sem("dup_ready", 1)
        gates_ready = sem("gates_ready", 1)
        decays_in = sem("decays_in", 1)
        gdn_ready = sem("gdn_ready", T)
        gdn_scaled = sem("gdn_scaled", 1)
        ln_scaled = sem("ln_scaled", 3 * T)
        xt0_ready = sem("xt0_ready", T)
        states_clear = sem("states_clear", 1)
        mix_ready = sem("mix_ready", 2)
        waits_taken = sem("waits_taken", 0)
        x_rest_ready = sem("x_rest_ready", 3 * T, T)
        diff_rotated = sem("diff_rotated", 1)
        pool_done = sem("pool_done", POOL_STEPS)
        probs_scaled = sem("probs_scaled", NSA_STEPS)
        level_ready = sem("level_ready", LEVELS * T)

        def filled(layer, key):
            return bank_filled.at(layer, number[key] + 1)

        def drained(layer, key):
            s = drained_act if drainer[key] == "act" else drained_dve
            return s.at(layer, rank[key])

        def bank(key):
            return PS[:, number[key] % 8, :]

        block = ctx.enter_context(nc.Block())

        def slot_at(n):
            return ring[:, n % RING, :]

        def load_arrived(layer, n):
            return slot_loaded[n % RING].at(layer, 32 * (n // RING + 1))

        def proj_items(g):
            sizes = [3 if e in BY_CHANNEL else T for e in range(len(PROJ_LOADS))]
            return range(sum(sizes[:g]), sum(sizes[:g + 1]))

        def unit_views(s, u):
            if s in (0, 3):
                w = s // 3
                raw_, n = (u // 2, u % 2) if u < FC else (GU_LOADS + (u - FC) // 2, (u - FC) % 2)
                slot = slot_at(FIRST_LOAD[2 * w] + raw_)
                buf = ffn_unit[(u + w) % 2]
                if u < FC:
                    raw_ = slot.rearrange("p (k b n c) -> p k b n c", k=KD, b=2, n=2)[:, :, :, n, :]
                    return [buf[:, e, :].rearrange("p (k b c) -> p k b c", k=KD, b=2) for e in range(2)] + [raw_]
                return [buf[:, 0, :], buf[:, 1, :], slot[:, n * UNIT:(n + 1) * UNIT]]
            if s == 1:
                w = 4 * (PROJ_LOADS[u // 2][1] - PROJ_LOADS[u // 2][0])
                slot, buf = slot_at(FIRST_LOAD[1] + u // 2), proj_unit[u % 2]
            else:
                w = UNIT
                slot, buf = slot_at(FIRST_LOAD[2] - 2 + u // 2), out_unit[u]
            return [buf[:, 0, 0:w], buf[:, 1, 0:w], slot[:, (u % 2) * w:(u % 2 + 1) * w]]

        def tile_end(first, turn, early=False):
            first(0)
            first(1)
            if early:
                turn(0)
            first(2)
            turn(int(early))
            first(3)
            for i in range(1 + int(early), T):
                turn(i)

        def token_parts(n):
            if n == 1:
                cq, ck = C_NQ - GDN_W, C_NKC - GDN_W
                src = [(h_tok[:, :, cq:cq + 256].rearrange("p t (n c) -> p t n c", n=4), 0, 512),
                       (h_tok[:, :, ck + 128:ck + 384].rearrange("p t (n c) -> p t n c", n=2)[:, :, :, 0:HD], 512, 768)]
            else:
                c, m = (C_DQ1, 8) if n == 2 else (C_SQ - GDN_W, 4)
                src = [(h_tok[:, :, c + at // 2:c + at // 2 + 256].rearrange("p t (n c) -> p t n c", n=m), at, at + 512)
                       for at in (0, 512)]
            found = []
            for kind, (x_, a0, a1) in enumerate(src):
                dst = parts[:, :, a0:a1].rearrange("p t (n a c) -> p t n a c", a=2, c=x_.shape[3])
                found.append((dst[:, :, :, kind, :], dst[:, :, :, 1 - kind, :], x_))
            return found

        def turn_bank(j, i, f):
            return bank(("wo", f, i)) if j == 1 else PS[:, i if f else 4 + i, :]

        @block.sync
        def _(sp):
            sp.dma_start(consts[:, :], a["consts"]).then_inc(consts_loaded.sem, 16)
            sp.dma_start(arena[:, 0:len(MASKS) * P], a["masks"]).then_inc(consts_loaded.sem, 16)
            sp.dma_start(x_tok[:, :, :], a["x"].rearrange("b (t p) d -> p (b t) d", p=P)).then_inc(x_loaded.sem, 16)

            def wait_slot_free(l, n):
                o = n - RING
                if o < 0:
                    l, o = l - 1, o + LAYER_LOADS
                if FIRST_LOAD[1] <= o < FIRST_LOAD[2]:
                    m = o - FIRST_LOAD[1]
                    if m < len(PROJ_LOADS):
                        sp.wait_ge(*unit_lo.at(l, FIRST_UNIT[1] + 2 * m + 2))
                    elif m < len(PROJ_LOADS) + 2:
                        sp.wait_ge(*filled(l, ("hid", m - len(PROJ_LOADS))))
                    else:
                        sp.wait_ge(*unit_lo.at(l, FIRST_UNIT[2] + 2 * (m - len(PROJ_LOADS) - 2) + 2))
                    sp.sem_inc(waits_taken.sem, 1)
                    return
                w = int(o >= FIRST_LOAD[2])
                m = o - FIRST_LOAD[2 * w]
                u = 2 * m + 2 if m < GU_LOADS else min(FC + 2 * (m - GU_LOADS) + 2, FFN_UNITS)
                sp.wait_ge(*unit_lo.at(l, FIRST_UNIT[3 * w] + u))

            def load_gate_up(l, w, g, s):
                gu = a["gu"][w][l].rearrange("(k p) c -> p k c", p=P)
                dst = ring[:, s, :].rearrange("p (k c) -> p k c", k=KD)
                for half in range(2):
                    sp.dma_start(dst[:, :, half * GU_W:(half + 1) * GU_W],
                                 gu[:, :, bass.ds(g * GU_W + half * DFF, GU_W)]).then_inc(slot_loaded[s].sem, 16)

            def ffn_loads(l, w):
                first = FIRST_LOAD[2 * w]
                for g in range(RING):
                    wait_slot_free(l, first + g)
                    load_gate_up(l, w, g, (first + g) % RING)
                with sp.Fori(0, 4) as it:
                    for s in range(RING):
                        sp.wait_ge(*unit_lo.at(l, it * (2 * RING) + (FIRST_UNIT[3 * w] + 2 * s + 2)))
                        load_gate_up(l, w, it * RING + (RING + s), (first + s) % RING)
                g = GU_LOADS - 1
                wait_slot_free(l, first + g)
                load_gate_up(l, w, g, (first + g) % RING)
                for idx, (f0, f1) in enumerate(DOWN_LOADS):
                    n = first + GU_LOADS + idx
                    wait_slot_free(l, n)
                    dst = ring[:, n % RING, 0:(f1 - f0) * DM].rearrange("p (f c) -> p f c", c=DM)
                    src = a["down"][w][l].rearrange("(f p) c -> p f c", p=P)[:, f0:f1, :]
                    sp.dma_start(dst, src).then_inc(slot_loaded[n % RING].sem, 32)

            def mixer_loads(l):
                n = FIRST_LOAD[1]
                for c0, c1 in PROJ_LOADS:
                    wait_slot_free(l, n)
                    dst = ring[:, n % RING, 0:KD * (c1 - c0)].rearrange("p (k c) -> p k c", k=KD)
                    sp.dma_start(dst, a["w_in"][l].rearrange("(k p) c -> p k c", p=P)[:, :, c0:c1]) \
                        .then_inc(slot_loaded[n % RING].sem, 32)
                    n += 1
                for w1 in (a["cmp_k_w1"], a["cmp_v_w1"]):
                    wait_slot_free(l, n)
                    sp.dma_start(ring[:, n % RING, :].rearrange("p (k c) -> p k c", k=16),
                                 w1[l].rearrange("(k p) c -> p k c", p=P)).then_inc(slot_loaded[n % RING].sem, 32)
                    n += 1
                for half in range(2):
                    wait_slot_free(l, n)
                    sp.dma_start(ring[:, n % RING, :].rearrange("p (k c) -> p k c", k=KD),
                                 a["w_out"][l].rearrange("(k p) c -> p k c", p=P)[:, :, half * 512:half * 512 + 512]) \
                        .then_inc(slot_loaded[n % RING].sem, 32)
                    n += 1

            with sp.Fori(0, DEPTH) as l:
                ffn_loads(l, 0)
                mixer_loads(l)
                ffn_loads(l, 1)
            for i in range(T):
                sp.wait_ge(*x_ready.at(DEPTH - 1, 2 * T + i + 1))
                sp.wait_ge(*x_rest_ready.at(DEPTH - 1, 2 * T + i + 1))
                sp.dma_start(out.rearrange("b (t p) d -> p (b t) d", p=P)[:, i, :], x_tok[:, i, :]) \
                    .then_inc(out_stored.sem, 16)
            sp.wait_ge(out_stored.sem, 16 * T)

        @block.tensor
        def _(pe):
            mm, tr = nc.tensor.matmul, nc.tensor.transpose
            pe.sem_inc(down_ready.sem, down_ready.start)
            pe.wait_ge(consts_loaded.sem, 32)
            pe.wait_ge(consts_cast.sem, 1)

            def turn_tile(l, j, i):
                pe.wait_ge(*x_ready.at(l, T * j + i + 1))
                pe.wait_ge(*x_rest_ready.at(l, T * j + i + 1))
                for f in range(2):
                    b = turn_bank(j, i, f)
                    for c in range(4):
                        k = 4 * f + c
                        ins = tr(b[:, c * P:(c + 1) * P], x_tok[:, i, k * P:(k + 1) * P], ident)
                    ins.then_inc(ln_turned.sem, 1)

            def split_mm(b, lhs, rhs, start, stop):
                mm(b, lhsT=lhs[0], rhs=rhs[0], start=start, stop=False)
                mm(b, lhsT=lhs[0], rhs=rhs[1], start=False, stop=False)
                return mm(b, lhsT=lhs[1], rhs=rhs[0], start=False, stop=stop)

            def ffn(l, w):
                pe.wait_ge(*turned_lo.at(l, 16 * w))
                pe.sem_inc(waits_taken.sem, 1)

                def gate_up(f, par):
                    pe.wait_ge(*unit_lo.at(l, FIRST_UNIT[3 * w] + 1 + f))
                    pe.wait_ge(*h_ready.at(l, w * FC - 1 + f))
                    hi, lo, _ = unit_views(3 * w, par)
                    for kind in range(2):
                        for k in range(KD):
                            ins = split_mm(PS[:, 2 * kind + par, :], (hi[:, k, kind, :], lo[:, k, kind, :]),
                                           (xTh[:, k, :], xTl[:, k, :]), k == 0, k == KD - 1)
                    ins.then_inc(gu_ready.sem, 1)

                with pe.Fori(0, FC // 2) as it:
                    for par in range(2):
                        gate_up(it * 2 + par, par)

                def down(d, i, half, f):
                    hi, lo, _ = unit_views(3 * w, FC + d)
                    c = (f % 2) * DM + half * 512
                    return split_mm(PS[:, i if half else 4 + i, :],
                                    (hh[:, f % 4, i * P:(i + 1) * P], hl[:, f % 4, i * P:(i + 1) * P]),
                                    (hi[:, c:c + 512], lo[:, c:c + 512]), f == 0, f == FC - 1)

                for d in range(DOWN_UNITS - 2):
                    pe.wait_ge(*unit_lo.at(l, FIRST_UNIT[3 * w] + FC + d + 1))
                    pe.wait_ge(*h_lo.at(l, w * DOWN_UNITS + d + 1))
                    for half in range(2):
                        if d == 0 and half:
                            pe.wait_ge(*h_ready.at(l, w * FC + FC))
                        for f in (2 * d, 2 * d + 1):
                            for i in range(T):
                                ins = down(d, i, half, f)
                    ins.then_inc(down_used.sem, 1)
                pe.wait_ge(*unit_lo.at(l, FIRST_UNIT[3 * w] + FFN_UNITS - 1))
                pe.wait_ge(*h_lo.at(l, (w + 1) * DOWN_UNITS - 1))

                def down_unit(d, i):
                    for half in range(2):
                        for f in (2 * d, 2 * d + 1):
                            ins = down(d, i, half, f)
                    return ins

                def last_chunks(i):
                    for e in {0: (0, 1, 2), 3: (3,)}.get(i, ()):
                        down_unit(DOWN_UNITS - 2, e)
                    if i == 0:
                        pe.wait_ge(*unit_lo.at(l, FIRST_UNIT[3 * w] + FFN_UNITS))
                        pe.wait_ge(*h_lo.at(l, (w + 1) * DOWN_UNITS))
                    down_unit(DOWN_UNITS - 1, i).then_inc(down_ready.sem, 1)

                if w:
                    tile_end(last_chunks, lambda i: turn_tile(l, 2, i))
                else:
                    for i in range(T):
                        last_chunks(i)
                    for i in range(2):
                        turn_tile(l, 0, i)

            def mixer(l):
                nxt = [0]

                def fill(*key, narrow=False):
                    q = number[key]
                    assert q == nxt[0], (key, items[nxt[0]])
                    nxt[0] += 1
                    if narrow:
                        pe.sem_inc(waits_taken.sem, 1)
                    if q >= 8:
                        pe.wait_ge(*drained(l, items[q - 8][0]))
                    if narrow:
                        pe.sem_inc(waits_taken.sem, 1)
                    return PS[:, q % 8, :]

                def reserve(*key):
                    q = number[key]
                    assert nxt[0] <= q < nxt[0] + 8
                    pe.sem_inc(waits_taken.sem, 1)
                    pe.wait_ge(*drained(l, items[q - 8][0]))
                    pe.sem_inc(waits_taken.sem, 1)
                    return bank(key)

                def take_turn(*key):
                    assert number[key] == nxt[0], (key, items[nxt[0]])
                    nxt[0] += 1

                def done(ins):
                    ins.then_inc(bank_filled.sem, 1)

                def turn_heads(b, src, width):
                    for i in range(T):
                        ins = tr(b[0:width, i * P:(i + 1) * P], src(i), ident)
                    return ins

                for g in range(len(PROJ_LOADS)):
                    if g == 1:
                        pe.wait_ge(*params_loaded.at(l, 16 * PARAM_DMAS))
                        b = fill("par", narrow=True)
                        done(tr(b[:, 0:PARAM_ROWS], stage[0:PARAM_ROWS, :], ident[0:PARAM_ROWS, 0:PARAM_ROWS]))
                    if g == len(PROJ_LOADS) - 1:
                        pe.wait_ge(*dup_ready.at(l, 1))
                        for s in range(2):
                            b = fill("dup", s)
                            done(turn_heads(b, lambda i: dup[:, s, i, :], P))
                    w = PROJ_LOADS[g][1] - PROJ_LOADS[g][0]
                    banks_ = [fill("proj", m) for m in proj_items(g)]

                    def half(i, kh):
                        wv = [e.rearrange("p (k c) -> p k c", k=4) for e in unit_views(1, 2 * g + kh)[:2]]
                        s_ = slice(i * P, (i + 1) * P)
                        for k in range(4):
                            x_ = (xTh[:, 4 * kh + k, :], xTl[:, 4 * kh + k, :])
                            if g in BY_CHANNEL:
                                ins = split_mm(banks_[i], [e[:, k, s_] for e in wv], x_, kh + k == 0, kh * k == 3)
                            else:
                                ins = split_mm(banks_[i][:, 0:w], [e[:, s_] for e in x_], [e[:, k, :] for e in wv],
                                               kh + k == 0, kh * k == 3)
                        return ins

                    if g == 0:
                        pe.wait_ge(*unit_lo.at(l, FIRST_UNIT[1] + 2))
                        for i in range(T):
                            pe.wait_ge(*turned_lo.at(l, 2 * i + 2))
                            ins = half(i, 0)
                            if i == T - 1:
                                ins.then_inc(proj_used.sem, 1)
                            done(half(i, 1))
                            if i + 2 < T:
                                turn_tile(l, 0, i + 2)
                        continue
                    for kh in range(2):
                        pe.wait_ge(*unit_lo.at(l, FIRST_UNIT[1] + 2 * g + kh + 1))
                        for i in range(len(banks_)):
                            ins = half(i, kh)
                            if kh:
                                done(ins)
                        if not kh:
                            ins.then_inc(proj_used.sem, 1)

                for s in range(2):
                    n = FIRST_LOAD[1] + len(PROJ_LOADS) + s
                    pe.wait_ge(*load_arrived(l, n))
                    pe.wait_ge(*blocks_ready.at(l, s + 1))
                    b = fill("hid", s, narrow=True)
                    wv = slot_at(n).rearrange("p (k c) -> p k c", k=16)
                    for k in range(16):
                        ins = mm(b[0:NCMP, 0:256], lhsT=blk[:, s, k, :], rhs=wv[:, k, :], start=k == 0, stop=k == 15)
                    done(ins)

                def turn_parts(b, at, w, kind):
                    for i in range(T):
                        s_ = slice(i * P, (i + 1) * P)
                        hi = at + (w if kind != "q" else 0)
                        if kind == "kh":
                            ins = tr(b[0:w, s_], parts[:, i, hi:hi + w].bitcast(F32), ident)
                            continue
                        ins = tr(b[0:2 * w, s_], parts[:, i, at:at + 2 * w].bitcast(F32), ident)
                    return ins

                pe.wait_ge(*tok_lo_ready.at(l, 1))
                for s in range(8):
                    b = fill("trn", s, narrow=True)
                    done(turn_parts(b, 2 * HD * s if s < 4 else 512 + 2 * HD * ((s - 4) // 2), HD,
                                    "q" if s < 4 else ("k", "kh")[s % 2]))
                pe.wait_ge(*drained(l, ("hid", 1)))
                b = fill("hidT", narrow=True)
                for s in range(2):
                    for f in range(2):
                        c = (2 * s + f) * 32
                        ins = tr(b[:, c:c + NCMP], hid_tok[0:NCMP, s, f * P:(f + 1) * P], ident[0:NCMP, 0:NCMP])
                done(ins)

                def compressed(name, j=0):
                    if name == "kcmp":
                        pe.wait_ge(*drained(l, ("hidT",)))
                        b = fill("kcmp", narrow=True)
                        for f in range(2):
                            for e in range(2):
                                ins = mm(b[HD * e:HD * e + HD, 0:NCMP], lhsT=w2[:, 0, f, :],
                                         rhs=hid[:, 0, f, 0:NCMP], start=f == 0, stop=f == 1)
                    elif name == "vcmp":
                        b = fill("vcmp", narrow=True)
                        for f in range(2):
                            ins = mm(b[0:NCMP, 0:HD], lhsT=hid[:, 1, f, 0:NCMP], rhs=w2[:, 1, f, :],
                                     start=f == 0, stop=f == 1)
                    elif name == "cs":
                        pe.wait_ge(*drained(l, ("kcmp",)))
                        b = fill("cs", narrow=True)
                        for n in range(T * H):
                            i, h = divmod(n, H)
                            ins = mm(b[:, n * 32:n * 32 + NCMP],
                                     lhsT=stacked(2 * h, "q")[:, i * P:(i + 1) * P].bitcast(F32),
                                     rhs=kcmpT[:, 0:NCMP], start=True, stop=True)
                    elif name == "cpT":
                        pe.wait_ge(*cmp_probs.at(l, 1))
                        b = fill("cpT", j, narrow=True)
                        for i in range(T):
                            ins = tr(b[0:NCMP, i * P:(i + 1) * P], csb[:, i * H + j, 0:NCMP], ident)
                    else:
                        pe.wait_ge(*drained(l, ("cpT", 2 * j)))
                        pe.sem_inc(waits_taken.sem, 1)
                        pe.wait_ge(*drained(l, ("cpT", 2 * j + 1)))
                        b = fill("co", j, narrow=True)
                        for e in range(2):
                            ins = mm(b[HD * e:HD * (e + 1), :], lhsT=vcmp[0:NCMP, :], rhs=cpTs[0:NCMP, e, :],
                                     start=True, stop=True)
                    done(ins)

                def turn(u, kind):
                    if u < UNITS:
                        h, br = divmod(u - 2 * H, 2)
                        at, w = (0 if kind == "q" else 512) + 256 * br + 2 * DQK * h, DQK
                    else:
                        at, w = (0 if kind == "q" else 512) + 2 * HD * (u - UNITS), HD
                    b = fill("tr", u, kind, narrow=True)
                    done(turn_parts(b, at, w, kind))

                def scores(n):
                    u, i = STEPS[n]
                    w = (i + 1) * P
                    if n >= NSA_STEPS and i == 0:
                        pe.wait_ge(*drained(l, ("tr", u, "k")))
                        pe.sem_inc(waits_taken.sem, 1)
                        pe.wait_ge(*drained(l, ("tr", u, "kh")))
                    b = fill("sc", n)
                    for kind in ("k", "kh"):
                        r = stack_rows(u, kind)
                        mm(b[:, 0:w], lhsT=stacked(u, "q")[0:r, i * P:w], rhs=stacked(u, kind)[0:r, 0:w],
                           start=kind == "k", stop=False)
                    done(mm(b[:, i * P:w], lhsT=identb, rhs=mask("causal"), start=False, stop=True))

                def turn_probs(n):
                    i = STEPS[n][1]
                    if n < NSA_STEPS:
                        pe.wait_ge(*probs_scaled.at(l, n + 1))
                    else:
                        pe.wait_ge(*probs_combined.at(l, (n - NSA_STEPS) // 2 + 1))
                    b = fill("tp", n)
                    for k in range(i + 1):
                        ins = tr(b[:, k * P:(k + 1) * P], prob_of(n)[:, k * P:(k + 1) * P], ident)
                    done(ins)

                def attend(g, half):
                    if g < 2 * H:
                        r = HD * (g // 2 % 2)
                        if half == 0:
                            for i in (T - 2, T - 1):
                                pe.wait_ge(*drained(l, ("tp", g * T + i)))
                            b = reserve("pv", g)
                        else:
                            b = bank(("pv", g))
                            take_turn("pv", g)
                        c = (C_NVS, C_NVW)[g % 2] - GDN_W
                        for k in (2 * half, 2 * half + 1):
                            ins = mm(b[r:r + HD, k * P:], lhsT=h_tok[:, k, c:c + HD], rhs=probT[:, g % 2, k, k * P:],
                                     start=k == 0, stop=k == T - 1)
                    else:
                        h = g - 2 * H
                        if half == 0:
                            pe.wait_ge(*drained(l, ("tp", NSA_STEPS + 2 * T * (h + 1) - 1)))
                            b = reserve("pv", g)
                        else:
                            b = bank(("pv", g))
                            take_turn("pv", g)
                        c = C_DV + HD * h
                        for i in ((0, 1, 2), (3,))[half]:
                            for k in range(i + 1):
                                ins = mm(b[:, i * HD:(i + 1) * HD], lhsT=probT[:, h % 2, k, i * P:(i + 1) * P],
                                         rhs=h_tok[:, k, c:c + HD], start=k == 0, stop=k == i)
                    if half:
                        done(ins)

                pe.wait_ge(*drained(l, ("trn", 6)))
                pe.wait_ge(*drained(l, ("trn", 7)))
                pe.sem_inc(waits_taken.sem, 1)
                for n in range(len(STEPS) + LAG + 2):
                    if n < len(STEPS):
                        scores(n)
                        for u, kind in turns_after(n):
                            if kind == "q" and (u == 2 * H or u == UNITS):
                                pe.wait_ge(*tok_lo_ready.at(l, 2 if u < UNITS else 3))
                            turn(u, kind)
                        for key in COMPRESSED.get(n, []):
                            compressed(*key)
                    if turned_after(n) is not None:
                        turn_probs(n - LAG)
                    if attends_after(n) is not None:
                        attend(*attends_after(n))

                first = [0, 512, 896, 1152]

                def log_odds(b, h, j, stop):
                    w = SEQ - j * P
                    q_, k_ = stacked(UNITS + h, "q")[:, j * P:], stacked(UNITS + h, "k")[:, j * P:(j + 1) * P]
                    mm(b[:, 0:w], lhsT=k_, rhs=q_, start=True, stop=False)
                    return mm(b[:, 0:w], lhsT=stacked(UNITS + h, "kh")[0:HD, j * P:(j + 1) * P], rhs=q_[0:HD, :],
                              start=False, stop=stop)

                for m in range(H * T + 2):
                    if m < H * T:
                        h, j = m // T, T - 1 - m % T
                        if m % T == 0:
                            pe.wait_ge(*drained(l, ("tr", UNITS + h, "k")))
                            pe.wait_ge(*drained(l, ("tr", UNITS + h, "kh")))
                        b = fill("z", h, j)
                        done(log_odds(b, h, j, True))
                        if m % T == 2 and h + 1 < H:
                            for kind in ("q", "k", "kh"):
                                turn(UNITS + h + 1, kind)
                    if m >= 2:
                        h, j = (m - 2) // T, T - 1 - (m - 2) % T
                        w = SEQ - j * P
                        pe.wait_ge(*soft_ready.at(l, m - 1))
                        b = fill("c", h, j)
                        log_odds(b, h, j, False)
                        mm(b[:, 0:w], lhsT=const("negtri"), rhs=soft[:, h % 2, first[j]:first[j] + w],
                           start=False, stop=False)
                        for k in range(j + 1, T):
                            mm(b[:, (k - j) * P:w], lhsT=const("negone"),
                               rhs=soft[:, h % 2, first[k]:first[k] + SEQ - k * P], start=False, stop=False)
                        done(mm(b[:, 0:P], lhsT=identb, rhs=mask("sbneg"), start=False, stop=True))
                        if j == 0:
                            pe.wait_ge(*drained(l, ("c", h, 0)))
                            b = fill("sbo", h, narrow=True)
                            r, cv = HD * (h % 2), C_SV + HD * h - GDN_W
                            for k in range(T):
                                ins = mm(b[r:r + HD, k * P:], lhsT=h_tok[:, k, cv:cv + HD],
                                         rhs=attT[h % 2][:, first[k]:first[k] + SEQ - k * P],
                                         start=k == 0, stop=k == T - 1)
                            done(ins)

                pe.wait_ge(*conv_silu.at(l, 1))
                for i in range(T):
                    for f in range(2):
                        b = fill("gtok", i, f)
                        for c in range(3):
                            ins = tr(b[:, c * P:(c + 1) * P], conv[:, 3 * f + c, i * P:(i + 1) * P], ident)
                        done(ins)
                pe.wait_ge(*gates_ready.at(l, 1))
                b = fill("G", narrow=True)
                mm(b[:, 0:16], lhsT=const("upto"), rhs=gdec, start=True, stop=True)
                mm(b[:, 16:32], lhsT=const("chunk"), rhs=gdec, start=True, stop=True)
                mm(b[0:64, 32:48], lhsT=const("chunk")[:, 0:64], rhs=gdec, start=True, stop=True)
                done(mm(b[0:64, 48:64], lhsT=const("chunk")[:, 64:128], rhs=gdec, start=True, stop=True))
                for i in range(T):
                    pe.wait_ge(*gdn_ready.at(l, i + 1))
                    for name, src in (("kT", ktok), ("kbT", kb), ("qT", qtok), ("qdT", qd)):
                        b = fill(name, i, narrow=True)
                        for h in range(H):
                            ins = tr(b[0:HD, h * P:(h + 1) * P], src[:, i, h * HD:(h + 1) * HD], ident)
                        done(ins)
                    b = fill("D", i)
                    for h in range(H):
                        n = i * H + h
                        mm(b[:, h * P:(h + 1) * P], lhsT=gdec[:, n:n + 1].to_broadcast([P, P]), rhs=const("upto"),
                           start=True, stop=False)
                        ins = mm(b[:, h * P:(h + 1) * P], lhsT=identb, rhs=mask("gdnneg"), start=False, stop=True)
                    done(ins)
                    for name, other, need in (("KK", kbTb, "kbT"), ("KQ", qTb, "qT")):
                        pe.wait_ge(*drained(l, (need, i)))
                        pe.wait_ge(*drained(l, ("kT", i)))
                        b = fill(name, i)
                        for h in range(H):
                            ins = mm(b[:, h * P:(h + 1) * P], lhsT=kTb[0:HD, h * P:(h + 1) * P],
                                     rhs=other[0:HD, h * P:(h + 1) * P], start=True, stop=True)
                        done(ins)

                def heads(b, lhs, rhs):
                    for h in range(H):
                        s = slice(h * P, (h + 1) * P)
                        ins = mm(b[:, s], lhsT=lhs[:, s], rhs=rhs(h), start=True, stop=True)
                    return ins

                for m in range(LEVELS * T + 1):
                    if m < LEVELS * T:
                        lev, i = divmod(m, T)
                        pe.wait_ge(*level_ready.at(l, m + 1))
                        if lev == 0:
                            b = fill("X0", i)
                            done(heads(b, NL[:, m % 2, :], lambda h: ident))
                        else:
                            pe.wait_ge(*drained(l, ("X0", i) if lev == 1 else ("X", lev - 1, i)))
                            b = fill("T1", lev, i)
                            done(heads(b, NL[:, m % 2, :], lambda h: X[:, i, h * P:(h + 1) * P]))
                    if m - 1 >= T:
                        lev, i = divmod(m - 1, T)
                        t1 = T1[:, (m - 1) % 2, :]
                        pe.wait_ge(*(xt0_ready.at(l, i + 1) if lev == 1 else drained(l, ("XT", lev - 1, i))))
                        pe.wait_ge(*drained(l, ("T1", lev, i)))
                        if lev < LEVELS - 1:
                            b = fill("X", lev, i)
                            done(heads(b, XT[:, i, :], lambda h: t1[:, h * P:(h + 1) * P]))
                        b = fill("XT", lev, i)
                        done(heads(b, t1, lambda h: XT[:, i, h * P:(h + 1) * P]))
                pe.wait_ge(*gdn_scaled.at(l, 1))
                for i in range(T):
                    pe.wait_ge(*drained(l, ("XT", LEVELS - 1, i)))
                    b = fill("wT", i, narrow=True)
                    for h in range(H):
                        ins = mm(b[0:HD, h * P:(h + 1) * P], lhsT=kbG[:, i, h * HD:(h + 1) * HD],
                                 rhs=XT[:, i, h * P:(h + 1) * P], start=True, stop=True)
                    done(ins)
                    b = fill("u", i)
                    for h in range(H):
                        ins = mm(b[:, h * HD:(h + 1) * HD], lhsT=XT[:, i, h * P:(h + 1) * P],
                                 rhs=vtok[:, i, h * HD:(h + 1) * HD], start=True, stop=True)
                    done(ins)
                pe.wait_ge(*drained(l, ("u", T - 1)))

                def outputs(i, h):
                    if h == 0:
                        reserve("o", i)
                    b, s = bank(("o", i)), slice(h * HD, (h + 1) * HD)
                    for par in range(2):
                        c = h * P + par * CH
                        mm(b[par * CH:(par + 1) * CH, s], lhsT=qdT[0:HD, i, c:c + CH],
                           rhs=states[0:HD, 2 * i + par, s], start=h == 0, stop=False, skip_group_check=True)
                    ins = mm(b[:, s], lhsT=intraT[:, i, h * P:(h + 1) * P], rhs=u_new[:, i, s],
                             start=False, stop=h == H - 1, skip_group_check=True)
                    if h == H - 1:
                        take_turn("o", i)
                        done(ins)

                for n in range(2 * T):
                    i, p = divmod(n, 2)
                    rows = slice(p * CH, (p + 1) * CH)
                    if n:
                        pe.wait_ge(*drained(l, ("S", n - 1)))
                        b = fill("ws", n, narrow=True)
                        for h in range(H):
                            c = h * P + p * CH
                            ins = mm(b[rows, h * HD:(h + 1) * HD], lhsT=wT[0:HD, i, c:c + CH],
                                     rhs=states[0:HD, n, h * HD:(h + 1) * HD], start=True, stop=True)
                        done(ins)
                        if n >= 2:
                            outputs((n - 2) // 2, 1 + 2 * (n % 2))
                        pe.wait_ge(*drained(l, ("ws", n)))
                    if n < 2 * T - 1:
                        b = fill("S", n, narrow=True)
                        for h in range(H):
                            ins = mm(b[0:HD, h * HD:(h + 1) * HD], lhsT=kd[rows, i, h * HD:(h + 1) * HD],
                                     rhs=u_new[rows, i, h * HD:(h + 1) * HD], start=True, stop=True)
                        done(ins)
                    if n == 1:
                        pe.wait_ge(*states_clear.at(l, 1))
                    if p:
                        outputs(i, 0)
                    elif n:
                        outputs(i - 1, 2)
                for h in range(1, H):
                    outputs(T - 1, h)
                pe.wait_ge(*mix_ready.at(l, 2))
                for i in range(T):
                    b = fill("mt", i)
                    for k in range(4):
                        ins = tr(b[:, k * P:(k + 1) * P], (dmix, gmix)[k // 2][:, i, (k % 2) * P:(k % 2 + 1) * P], ident)
                    done(ins)
                pe.wait_ge(*outT_lo.at(l, 1))
                pe.wait_ge(*drained(l, ("mt", T - 1)))

                def out_unit_mm(b, i, u):
                    hi, lo, _ = unit_views(2, u)
                    for k in range(4):
                        kk, c = 4 * (u % 2) + k, slice(k * 512, (k + 1) * 512)
                        ins = split_mm(b, (xTh[:, kk, i * P:(i + 1) * P], xTl[:, kk, i * P:(i + 1) * P]),
                                       (hi[:, c], lo[:, c]), kk == 0, kk == KD - 1)
                    return ins

                banks_ = [fill("wo", 0, i, narrow=True) for i in range(T)]
                for u in range(2):
                    pe.wait_ge(*unit_lo.at(l, FIRST_UNIT[2] + u + 1))
                    for i in range(T):
                        ins = out_unit_mm(banks_[i], i, u)
                        if u:
                            done(ins)
                pe.wait_ge(*unit_lo.at(l, FIRST_UNIT[2] + OUT_UNITS))

                def last_half(i):
                    b = fill("wo", 1, i)
                    out_unit_mm(b, i, 2)
                    done(out_unit_mm(b, i, 3))

                tile_end(last_half, lambda i: turn_tile(l, 1, i))
                assert nxt[0] == len(items)

            for i in range(T):
                turn_tile(0, -1, i)
            with pe.Fori(0, DEPTH) as l:
                ffn(l, 0)
                mixer(l)
                ffn(l, 1)

        @block.scalar
        def _(act):
            f_ = nc.scalar.activation
            steps = [0]
            act.wait_ge(consts_cast.sem, 1)

            def split_hi(l, s, u, f=None):
                w = s // 3
                n = u if f is None else f
                if s in (0, 3):
                    if u < FC and f is not None:
                        n0 = FIRST_LOAD[2 * w] + u // 2
                        act.wait_ge(*slot_loaded[n0 % RING].at(l, 32 * (n0 // RING + 1) + (f - u) * 8))
                    else:
                        n0 = FIRST_LOAD[2 * w] + (u // 2 if u < FC else GU_LOADS + (u - FC) // 2)
                        act.wait_ge(*load_arrived(l, n0))
                    if u < 2 and f is None:
                        if w == 0:
                            act.wait_ge(*down_ready.at(l, 0))
                        else:
                            act.wait_ge(*filled(l, ("wo", u, T - 1)))
                    elif u - 2 < FC:
                        act.wait_ge(*gu_ready.at(l, w * FC - 1 + n))
                    else:
                        act.wait_ge(*down_used.at(l, w * (DOWN_UNITS - 2) + u - 1 - FC))
                elif s == 1:
                    act.wait_ge(*load_arrived(l, FIRST_LOAD[1] + u // 2))
                    if u < 2:
                        act.wait_ge(*h_lo.at(l, DOWN_UNITS))
                    elif u % 2:
                        act.wait_ge(*filled(l, ("proj", proj_items(u // 2 - 1)[-1])))
                    else:
                        act.wait_ge(*proj_used.at(l, u // 2))
                else:
                    act.wait_ge(*load_arrived(l, FIRST_LOAD[2] - 2 + u // 2))
                    act.wait_ge(*filled(l, ("o", T - 1) if u else ("gtok", T - 1, 1)))
                hi, _, raw_ = unit_views(s, u)
                nc.scalar.copy(hi, raw_).then_inc(unit_hi.sem, 1)

            def split_h(l, w, d):
                act.wait_ge(*h_ready.at(l, w * FC + 2 * d + 2))
                if d >= 2:
                    act.wait_ge(*down_used.at(l, w * (DOWN_UNITS - 2) + d - 1))
                elif w == 0 and d == 0:
                    act.wait_ge(*down_ready.at(l, 0))
                s = 2 * (d % 2)
                nc.scalar.copy(hh[:, s:s + 2, :], hT[:, 2 * d:2 * d + 2, :]).then_inc(h_hi.sem, 1)

            def norm_std(l, j, i):
                act.wait_ge(*ln_var.at(l, T * j + i + 1))
                f_(lnst[:, i, 14:15], lnst[:, i, 13:14], ACT.Sqrt, bias=epses[:, 0:1]).then_inc(ln_std.sem, 1)

            def turned(l, j, i):
                for f in range(2):
                    act.wait_ge(*ln_turned.at(l, 8 * j + 2 * i + f + 1))
                    nc.scalar.copy(xTh[:, 4 * f:4 * f + 4, i * P:(i + 1) * P],
                                   turn_bank(j, i, f).rearrange("p (k t) -> p k t", k=4)).then_inc(turned_hi.sem, 1)

            def finish(l, j):
                tile_end(lambda i: norm_std(l, j, i), lambda i: turned(l, j, i), j == 0)

            def ffn(l, w):
                s = 3 * w

                def gate(f, par):
                    act.wait_ge(*h_ready.at(l, w * FC - 1 + f))
                    act.wait_ge(*gu_ready.at(l, w * FC + 1 + f))
                    f_(sil[:, par, :], PS[:, par, :], ACT.Silu).then_inc(silu_ready.sem, 1)

                if w == 0:
                    split_hi(l, s, 0)
                split_hi(l, s, 1)
                gate(0, 0)
                with act.Fori(0, 5) as it:
                    for e in range(4):
                        split_hi(l, s, e + 2, f=it * 4 + (e + 2))
                        gate(it * 4 + (e + 1), (e + 1) % 2)
                for d in range(2):
                    split_h(l, w, d)
                split_hi(l, s, FC)
                gate(FC - 1, (FC - 1) % 2)
                for d in range(1, DOWN_UNITS):
                    split_hi(l, s, FC + d)
                    if d >= 2:
                        split_h(l, w, d)
                if w == 0:
                    split_hi(l, 1, 0)
                    split_hi(l, 1, 1)
                finish(l, 2 * w)

            def mixer(l):
                steps[0] = 0

                def link(ins):
                    steps[0] += 1
                    ins.then_inc(act_done.sem, 1)
                    act.wait_ge(*act_done.at(l, steps[0]))

                def bank_of(*key):
                    act.wait_ge(*filled(l, key))
                    return bank(key)

                def split_tok_hi(n):
                    if n == 1:
                        act.wait_ge(*filled(l, ("proj", 29)))
                    elif n == 2:
                        act.wait_ge(*diff_rotated.at(l, 1))
                        act.wait_ge(*filled(l, ("trn", 7)))
                    elif n == 3:
                        act.wait_ge(*filled(l, ("tr", UNITS - 1, "k")))
                    for hi, _, x_ in token_parts(n):
                        ins = nc.scalar.copy(hi, x_)
                    ins.then_inc(tok_hi_ready.sem, 1)

                def drain_heads(dst, *key, **kw):
                    b = bank_of(*key)
                    f_(dst, b[0:dst.shape[0], 0:dst.shape[1]], ACT.Copy, **kw).then_inc(drained_act.sem, 1)

                for g in range(len(PROJ_LOADS)):
                    if g + 1 < len(PROJ_LOADS):
                        split_hi(l, 1, 2 * g + 2)
                        split_hi(l, 1, 2 * g + 3)
                    if g == 5:
                        act.wait_ge(*conv_done.at(l, 6))
                        f_(conv[:, :, :], conv[:, :, :], ACT.Silu).then_inc(conv_silu.sem, 1)
                    if g == 7:
                        act.wait_ge(*nsa_rotated.at(l, 1))
                        for s in range(2):
                            drain_heads(dupT[:, s, :], "dup", s)
                    if g == 1:
                        act.wait_ge(*drained(l, ("par",)))
                    for m in proj_items(g):
                        if m % 2:
                            continue
                        b = bank_of("proj", m)
                        if g in BY_CHANNEL:
                            nc.scalar.copy(raw[:, m - T, 3:515], b).then_inc(drained_act.sem, 1)
                        else:
                            c0, c1 = PROJ_LOADS[g]
                            d = c0 - (GDN_W if c0 >= C_GZ else 0)
                            nc.scalar.copy(h_tok[:, m - proj_items(g)[0], d:d + c1 - c0], b[:, 0:c1 - c0]) \
                                .then_inc(drained_act.sem, 1)
                split_tok_hi(1)
                for s in range(2):
                    b = bank_of("hid", s)
                    f_(hid_tok[0:NCMP, s, :], b[0:NCMP, 0:256], ACT.Silu).then_inc(drained_act.sem, 1)
                act.wait_ge(*gates_in.at(l, 1))
                z = C_GZ - GDN_W
                link(f_(siluz[:, :, :], h_tok[:, :, z:z + 256], ACT.Silu))
                for s in range(0, 8, 2):
                    drain_heads(stacked(2 * s, "q") if s < 4 else stacked(s // 2 - 2, "k"), "trn", s)
                b = bank_of("hidT")
                nc.scalar.copy(hid[:, :, :, 0:NCMP], b[:, 0:128].rearrange("p (s f c) -> p s f c", s=2, f=2)[:, :, :, 0:NCMP]) \
                    .then_inc(drained_act.sem, 1)
                act.sem_inc(waits_taken.sem, 1)
                act.preload_act_table_set("natural_log_exp_and_others")
                link(f_(ab_e, ab_abs, ACT.Exp, scale=-1.0))
                link(f_(ab_ln, ab_e, ACT.Ln, bias=1.0))
                f_(ea, prm[:, 256:260], ACT.Exp)
                f_(lamexp, lamdot, ACT.Exp)
                cb, cg = C_GB - GDN_W, C_GATE - GDN_W
                f_(beta.rearrange("p (t h) -> p t h", t=T), h_tok[:, :, cb:cb + H], ACT.Exp, scale=-1.0)
                f_(gate.rearrange("p (t h) -> p t h", t=T), h_tok[:, :, cg:cg + 12], ACT.Exp,
                   scale=-1.0).then_inc(gates_exp.sem, 1)
                for n in range(len(STEPS) + LAG + 2):
                    if n < len(STEPS):
                        w = (STEPS[n][1] + 1) * P
                        b = bank_of("sc", n)
                        if n >= NSA_STEPS + 4 and n % 2 == 0:
                            act.wait_ge(*probs_combined.at(l, (n - NSA_STEPS) // 2 - 1))
                        if n == 3:
                            act.wait_ge(*diff_rotated.at(l, 1))
                        act.wait_ge(*row_max.at(l, n + 1))
                        f_(prob_of(n)[:, 0:w], b[:, 0:w], ACT.Exp, bias=nmax[:, n:n + 1],
                           accum_out=rsum[:, n:n + 1]).then_inc(drained_act.sem, 1)
                        if n == NSA_STEPS // 2:
                            split_tok_hi(2)
                        if n == NSA_STEPS + 2 * T * (H - 1):
                            split_tok_hi(3)
                        for u, kind in turns_after(n):
                            if kind != "k":
                                drain_heads(stacked(u, kind)[0:stack_rows(u, kind), :], "tr", u, kind,
                                            **(dict(scale=HD ** -0.5) if u == UNITS and kind == "q" else {}))
                        if n == 3:
                            act.wait_ge(*cmp_shifted.at(l, 1))
                            f_(csb[:, :, 0:NCMP], csb[:, :, 0:NCMP], ACT.Exp).then_inc(cmp_exp.sem, 1)
                        for key in COMPRESSED.get(n, []):
                            if drainer[key] == "act":
                                drain_heads(cpTs[0:NCMP, 0, :], *key)
                    if turned_after(n) is not None and drainer[("tp", n - LAG)] == "act":
                        u, i = STEPS[n - LAG]
                        b = bank_of("tp", n - LAG)
                        nc.scalar.copy(probT[:, u % 2 if u < 2 * H else u // 2 % 2, 0:i + 1, i * P:(i + 1) * P],
                                       b[:, 0:(i + 1) * P].rearrange("p (n q) -> p n q", q=P)) \
                            .then_inc(drained_act.sem, 1)
                    g, half = attends_after(n) or (0, 0)
                    if half and g >= 2 * H:
                        b = bank_of("pv", g)
                        nc.scalar.copy(dmix[:, :, HD * (g - 2 * H):HD * (g - 2 * H + 1)],
                                       b[:, 0:256].rearrange("p (t c) -> p t c", t=T)).then_inc(drained_act.sem, 1)
                act.wait_ge(*norm_sum.at(l, 1))
                f_(rstd[:, 0:16], ssq[:, 0:16], ACT.Sqrt, bias=epses[:, 1:2], scale=1.0 / HD).then_inc(norm_std_ready.sem, 1)
                first = [0, 512, 896, 1152]
                act.preload_act_table_set("natural_log_exp_and_others")
                for m in range(H * T + 2):
                    if m < H * T:
                        h, j = m // T, T - 1 - m % T
                        w = SEQ - j * P
                        t = prob[:, m % 3, 0:w]
                        if m >= 3:
                            act.wait_ge(*drained(l, ("z", (m - 3) // T, T - 1 - (m - 3) % T)))
                        b = bank_of("z", h, j)
                        link(f_(t, b[:, 0:w], ACT.Abs))
                        link(f_(t, t, ACT.Exp, scale=-1.0))
                        f_(t, t, ACT.Ln, bias=1.0).then_inc(soft_ln.sem, 1)
                        if m % T == 2 and h + 1 < H:
                            drain_heads(stacked(UNITS + h + 1, "q"), "tr", UNITS + h + 1, "q", scale=HD ** -0.5)
                            drain_heads(stacked(UNITS + h + 1, "kh")[0:HD, :], "tr", UNITS + h + 1, "kh")
                    if m >= 2:
                        h, j = (m - 2) // T, T - 1 - (m - 2) % T
                        w = SEQ - j * P
                        b = bank_of("c", h, j)
                        f_(attT[h % 2][:, first[j]:first[j] + w], b[:, 0:w], ACT.Exp).then_inc(drained_act.sem, 1)
                        if j == 0:
                            b = bank_of("sbo", h)
                            r = slice(HD * (h % 2), HD * (h % 2) + HD)
                            nc.scalar.copy(outT[r, 2 + h // 2, :], b[r, :]).then_inc(drained_act.sem, 1)
                for i in range(T):
                    b = bank_of("gtok", i, 0)
                    nc.scalar.copy(qtok[:, i, :], b[:, 0:256])
                    nc.scalar.copy(ktok[:, i, 0:128], b[:, 256:384]).then_inc(drained_act.sem, 1)
                    b = bank_of("gtok", i, 1)
                    nc.scalar.copy(ktok[:, i, 128:256], b[:, 0:128])
                    nc.scalar.copy(vtok[:, i, :], b[:, 128:384]).then_inc(drained_act.sem, 1)
                act.wait_ge(*norm_sum.at(l, 2))
                f_(rstd, ssq, ACT.Sqrt, bias=epses[:, 1:2]).then_inc(norm_std_ready.sem, 1)
                act.wait_ge(*decays_in.at(l, 1))
                f_(expG, gcol[:, 0:16], ACT.Exp)
                f_(expKd, expKd, ACT.Exp)
                f_(gl[0:64, :], gcol[0:64, 32:64], ACT.Exp).then_inc(decays_exp.sem, 1)
                for i in range(T):
                    drain_heads(kTb[0:HD, :], "kT", i)
                    drain_heads(qTb[0:HD, :], "qT", i)
                    drain_heads(qdT[0:HD, i, :], "qdT", i)
                    b = bank_of("D", i)
                    if i:
                        act.wait_ge(*drained(l, ("KQ", i - 1)))
                    for h in range(H):
                        s = slice(h * P, (h + 1) * P)
                        n = i * H + h
                        ins = f_(Dm[:, s], b[:, s], ACT.Exp, bias=negG[:, n:n + 1])
                    ins.then_inc(drained_act.sem, 1)
                for m in range(T, LEVELS * T):
                    lev, i = divmod(m, T)
                    drain_heads(T1[:, m % 2, :], "T1", lev, i)
                split_hi(l, 2, 0)
                for i in range(T):
                    drain_heads(wT[0:HD, i, :], "wT", i)
                    b = bank_of("u", i)
                    nc.scalar.copy(u_new[:, i, :], b[:, 0:256]).then_inc(drained_act.sem, 1)
                nc.scalar.copy(xTh[:, 4:8, :], outT).then_inc(outT_hi.sem, 1)
                for i in range(T):
                    b = bank_of("o", i)
                    nc.scalar.copy(gmix[:, i, :], b[:, 0:256]).then_inc(drained_act.sem, 1)
                split_hi(l, 2, 1)
                act.wait_ge(*norm_sum.at(l, 3))
                f_(rstd[:, 0:16], ssq[:, 0:16], ACT.Sqrt, bias=epses[:, 1:2], scale=1.0 / HD).then_inc(norm_std_ready.sem, 1)
                for i in range(T):
                    b = bank_of("mt", i)
                    nc.scalar.copy(xTh[:, 0:4, i * P:(i + 1) * P],
                                   b.rearrange("p (k t) -> p k t", k=4)).then_inc(mix_hi.sem, 1)
                split_hi(l, 2, 2)
                split_hi(l, 2, 3)
                split_hi(l, 3, 0)
                finish(l, 1)
                assert steps[0] == ACT_STEPS, ("ACT_STEPS", steps[0])

            for i in range(T):
                turned(0, -1, i)
            with act.Fori(0, DEPTH) as l:
                ffn(l, 0)
                mixer(l)
                ffn(l, 1)

        @block.vector
        def _(dve):
            v = nc.vector
            tt, ts, stt = v.tensor_tensor, v.tensor_scalar, v.scalar_tensor_tensor
            steps = [0]
            dve.wait_ge(consts_loaded.sem, 32)
            v.memset(epses[:, 0:1], LN_EPS)
            v.memset(epses[:, 1:2], NORM_EPS)
            v.tensor_copy(masks[:, :], arena[:, 0:len(MASKS) * P]).then_inc(consts_cast.sem, 1)
            dve.sem_inc(h_ready.sem, h_ready.start)
            dve.wait_ge(x_loaded.sem, 16)
            dve.sem_inc(x_ready.sem, x_ready.start)
            dve.sem_inc(unit_lo.sem, unit_lo.start)

            def link(l, ins):
                steps[0] += 1
                ins.then_inc(dve_done.sem, 1)
                dve.wait_ge(*dve_done.at(l, steps[0]))

            def add_and_count(l, i, half, b, sem_=None):
                xs = x_tok[:, i, half * 512:(half + 1) * 512]
                ins = stt(out=xs, in0=xs, scalar=ALPHA, in1=b, op0=ALU.mult, op1=ALU.add)
                if sem_ is None:
                    link(l, ins)
                else:
                    ins.then_inc(sem_.sem, 1)
                    dve.wait_ge(*drained(l, ("wo", half, i)))
                link(l, v.bn_stats(lnst[:, i, 6 * half:6 * half + 6], xs))

            def normalise(l, j, i):
                dve.sem_inc(waits_taken.sem, 1)
                link(l, v.bn_aggr(lnst[:, i, 12:14], lnst[:, i, 0:12]))
                ts(lnst[:, i, 13:14], lnst[:, i, 13:14], 1.0, None, ALU.mult).then_inc(ln_var.sem, 1)
                dve.wait_ge(*ln_std.at(l, T * j + i + 1))
                link(l, v.reciprocal(lnst[:, i, 15:16], lnst[:, i, 14:15]))
                xs = x_tok[:, i, :]
                ts(xs, xs, lnst[:, i, 12:13], lnst[:, i, 15:16], ALU.subtract, ALU.mult).then_inc(ln_scaled.sem, 1)
                dve.wait_ge(*ln_scaled.at(l, T * j + i + 1))
                dve.wait_ge(*lnp_loaded.at(l, 32 * (j + 1)))
                xs = x_tok[:, i, 0:LN_CUT]
                link(l, tt(xs, xs, lnp[:, 0, 0:LN_CUT], ALU.mult))
                tt(xs, xs, lnp[:, 1, 0:LN_CUT], ALU.add).then_inc(x_ready.sem, 1)

            def split_lo(l, s, u, n=None):
                dve.wait_ge(*unit_hi.at(l, (u if n is None else n) + (FIRST_UNIT[s] + 1)))
                hi, lo, raw_ = unit_views(s, u)
                tt(lo, raw_, hi.bitcast(F32), ALU.subtract).then_inc(unit_lo.sem, 1)

            def turned(l, j, i):
                for f in range(2):
                    dve.wait_ge(*turned_hi.at(l, 8 * j + 2 * i + f + 1))
                    tt(xTl[:, 4 * f:4 * f + 4, i * P:(i + 1) * P], turn_bank(j, i, f).rearrange("p (k t) -> p k t", k=4),
                       xTh[:, 4 * f:4 * f + 4, i * P:(i + 1) * P].bitcast(F32), ALU.subtract).then_inc(turned_lo.sem, 1)

            def split_h(l, w, d):
                dve.wait_ge(*h_hi.at(l, w * DOWN_UNITS + d + 1))
                s = 2 * (d % 2)
                tt(hl[:, s:s + 2, :], hT[:, 2 * d:2 * d + 2, :], hh[:, s:s + 2, :].bitcast(F32),
                   ALU.subtract).then_inc(h_lo.sem, 1)

            def ffn(l, w):
                s = 3 * w

                def gated(f, par):
                    dve.wait_ge(*silu_ready.at(l, w * FC + 1 + f))
                    stt(out=hT[:, bass.ds(f, 1), :].rearrange("p f t -> p (f t)"), in0=sil[:, par, :], scalar=0.5,
                        in1=PS[:, 2 + par, :], op0=ALU.mult, op1=ALU.mult).then_inc(h_ready.sem, 1)

                if w == 0:
                    split_lo(l, s, 0)
                split_lo(l, s, 1)
                gated(0, 0)
                with dve.Fori(0, 5) as it:
                    for e in range(4):
                        split_lo(l, s, e + 2, n=it * 4 + (e + 2))
                        gated(it * 4 + (e + 1), (e + 1) % 2)
                for d in range(2):
                    split_h(l, w, d)
                split_lo(l, s, FC)
                gated(FC - 1, (FC - 1) % 2)
                for d in range(1, DOWN_UNITS):
                    split_lo(l, s, FC + d)
                    if d >= 2:
                        split_h(l, w, d)
                if w == 0:
                    split_lo(l, 1, 0)
                    split_lo(l, 1, 1)

                def tile(i):
                    dve.wait_ge(*down_ready.at(l, T * w + i + 1))
                    for half in range(2):
                        add_and_count(l, i, half, PS[:, i if half else 4 + i, :])
                    normalise(l, 2 * w, i)

                tile_end(tile, lambda i: turned(l, 2 * w, i), w == 0)

            def mixer(l):
                def bank_of(*key):
                    dve.wait_ge(*filled(l, key))
                    return bank(key)

                def drain(ins):
                    ins.then_inc(drained_dve.sem, 1)

                def tiles(x_):
                    return x_.rearrange("p (t c) -> p t c", t=T)

                def over(col, n):
                    return col.unsqueeze(2).broadcast_to([col.shape[0], col.shape[1], n])

                def head_scale(dst, src, colmn):
                    for i in range(T):
                        c = over(colmn[:, i * H:(i + 1) * H], HD)
                        ins = tt(dst[:, i, :].rearrange("p (h d) -> p h d", h=H),
                                 src[:, i, :].rearrange("p (h d) -> p h d", h=H), c, ALU.mult)
                    return ins

                def rotate(part, n, c):
                    for i in range(T):
                        src = h_tok[:, i, c:c + (256 if part == "q" else 384)].rearrange("p (n w) -> p n w", n=n)
                        src = src[:, :, 0:HD].rearrange("p n (a d) -> p n a d", a=2)
                        cos = const("c" + part)[:, i * 32:(i + 1) * 32].unsqueeze(1).unsqueeze(1)
                        sin = const("s" + part)[:, i * 64:(i + 1) * 64].rearrange("p (a d) -> p a d", a=2).unsqueeze(1)
                        t0 = prob[:, 0, 0:64 * n].rearrange("p (n a d) -> p n a d", n=n, a=2)
                        t1 = prob[:, 1, 0:64 * n].rearrange("p (n a d) -> p n a d", n=n, a=2)
                        tt(t0, src, cos.broadcast_to([P, n, 2, 32]), ALU.mult)
                        link(l, tt(t1, src[:, :, ::-1, :], sin.broadcast_to([P, n, 2, 32]), ALU.mult))
                        ins = tt(src, t0, t1, ALU.add)
                        if part == "q" and i == T - 1:
                            ins.then_inc(nsa_rotated.sem, 1)
                        else:
                            link(l, ins)

                def compression_blocks():
                    for s in range(2):
                        dve.wait_ge(*drained(l, ("dup", s)))
                        for r in range(2):
                            rows = slice(HD * r, HD * (r + 1))
                            src = dupT[rows, s, :].rearrange("p (c q) -> p q c", q=16)
                            for e in range(2):
                                pe_ = over(parT[rows, 24 + 16 * s + 8 * e:24 + 16 * s + 8 * e + 8], NCMP)
                                ins = tt(blk[rows, s, 8 * e:8 * e + 8, :], src[:, r::2, e:e + NCMP], pe_, ALU.add)
                                if r == 0 or e == 0:
                                    link(l, ins)
                        ins.then_inc(blocks_ready.sem, 1)

                for g in range(len(PROJ_LOADS)):
                    if g == 1:
                        b = bank_of("par")
                        v.memset(raw[:, :, 0:3], 0.0)
                        drain(v.tensor_copy(parT[:, :], b[:, 0:PARAM_ROWS]))
                        dve.wait_ge(*drained(l, ("par",)))
                    if g == 7:
                        compression_blocks()
                    if g + 1 < len(PROJ_LOADS):
                        split_lo(l, 1, 2 * g + 2)
                        split_lo(l, 1, 2 * g + 3)
                    for m in proj_items(g):
                        if m % 2 == 0:
                            continue
                        b = bank_of("proj", m)
                        if g in BY_CHANNEL:
                            drain(v.tensor_copy(raw[:, m - T, 3:515], b))
                        else:
                            c0, c1 = PROJ_LOADS[g]
                            d = c0 - (GDN_W if c0 >= C_GZ else 0)
                            drain(v.tensor_copy(h_tok[:, m - proj_items(g)[0], d:d + c1 - c0], b[:, 0:c1 - c0]))
                    for j in ([], [], [0, 1], [2, 3], [4, 5], [], [], [])[g]:
                        dve.wait_ge(*drained(l, ("proj", T + j)))
                        link(l, ts(conv[:, j, :], raw[:, j, 0:SEQ], parT[:, j:j + 1], None, ALU.mult))
                        for k in range(1, 4):
                            ins = stt(out=conv[:, j, :], in0=raw[:, j, k:k + SEQ], scalar=parT[:, 6 * k + j:6 * k + j + 1],
                                      in1=conv[:, j, :], op0=ALU.mult, op1=ALU.add)
                            if k < 3:
                                link(l, ins)
                        ins.then_inc(conv_done.sem, 1)
                    if g == 5:
                        dve.wait_ge(*drained(l, ("proj", 16)))
                        dve.wait_ge(*drained(l, ("proj", 17)))
                        dve.wait_ge(*conv_done.at(l, 6))
                        rotate("k", 3, C_NKC - GDN_W)
                        for s, c in ((0, C_NKC - GDN_W), (1, C_NVC - GDN_W)):
                            ins = v.tensor_copy(dup[:, s].rearrange("p t (a d) -> p t a d", a=2),
                                                h_tok[:, :, c:c + HD].unsqueeze(2).broadcast_to([P, T, 2, HD]))
                        ins.then_inc(dup_ready.sem, 1)
                        rotate("q", 4, C_NQ - GDN_W)
                dve.wait_ge(*drained(l, ("proj", 28)))
                dve.wait_ge(*drained(l, ("proj", 29)))
                ca = C_GA - GDN_W
                link(l, tt(tiles(ab_x), h_tok[:, :, ca:ca + H],
                           prm[:, 260:264].unsqueeze(1).broadcast_to([P, T, H]), ALU.add))
                link(l, stt(out=ab_abs, in0=ab_x, scalar=-1.0, in1=ab_x, op0=ALU.mult, op1=ALU.max))
                lam = rinv[:, 0:1]
                prod = prob[:, 2, 0:64]
                link(l, tt(prod, prm[:, 0:64], prm[:, 64:128], ALU.mult))
                v.tensor_reduce(lamdot, prod.rearrange("p (a d) -> p a d", a=2), AX.X, ALU.add).then_inc(gates_in.sem, 1)

                def split_tok_lo(n):
                    dve.wait_ge(*tok_hi_ready.at(l, n))
                    for hi, lo, x_ in token_parts(n):
                        ins = tt(lo, x_, hi.bitcast(F32), ALU.subtract)
                    ins.then_inc(tok_lo_ready.sem, 1)

                def drain_copy(dst, *key):
                    b = bank_of(*key)
                    drain(v.tensor_copy(dst, b[0:dst.shape[0], 0:dst.shape[1]]))

                split_tok_lo(1)
                for s in range(1, 8, 2):
                    drain_copy(stacked(2 * s, "q") if s < 4 else stacked(s // 2 - 2, "kh")[0:HD, :], "trn", s)
                dve.wait_ge(*gates_exp.at(l, 1))
                for s in (beta, gate):
                    link(l, ts(s, s, 1.0, None, ALU.add))
                    link(l, v.reciprocal(s, s))
                link(l, stt(out=ab_ln, in0=ab_x, scalar=0.0, in1=ab_ln, op0=ALU.max, op1=ALU.add))
                link(l, stt(out=tiles(gdec), in0=tiles(ab_ln), scalar=-1.0,
                            in1=ea.unsqueeze(1).broadcast_to([P, T, H]), op0=ALU.mult, op1=ALU.mult))
                link(l, tt(lam, lamexp[:, 1:2], lamexp[:, 0:1], ALU.subtract))
                tt(neglam, lam, prm[:, 264:265], ALU.subtract).then_inc(gates_ready.sem, 1)
                link(l, v.memset(outT[:, 0:2, :], 0.0))
                gates = tiles(gate).rearrange("p t (h b) -> p t h b", b=3)
                cn = csb[:, :, 0:NCMP]

                def by_tile(x_):
                    return x_.rearrange("p (t h) c -> p t h c", t=T)

                def tile_mask(name):
                    return tiles(const(name)).unsqueeze(2).broadcast_to([P, T, H, 32])[:, :, :, 0:NCMP]

                def compressed(name, j=0):
                    if name == "kcmp":
                        drain_copy(kcmpT[:, 0:NCMP], "kcmp")
                    elif name == "vcmp":
                        drain_copy(vcmp[0:NCMP, :], "vcmp")
                    elif name == "cs":
                        b = bank_of("cs")
                        drain(tt(by_tile(cn), by_tile(b.rearrange("p (n c) -> p n c", c=32)[:, :, 0:NCMP]),
                                 tile_mask("cneg"), ALU.add))
                        dve.wait_ge(*drained(l, ("cs",)))
                        link(l, v.tensor_reduce(cmx, cn, AX.X, ALU.max))
                        tt(cn, cn, over(cmx, NCMP), ALU.subtract).then_inc(cmp_shifted.sem, 1)
                    elif name == "cpT":
                        if drainer[("cpT", j)] == "dve":
                            drain_copy(cpTs[0:NCMP, 1, :], "cpT", j)
                    else:
                        add_out(slice(0, P), j, "co", j)

                def add_out(rows, j, *key):
                    b = bank_of(*key)
                    if added:
                        dve.wait_ge(*drained(l, added[0]))
                    added[:] = [key]
                    drain(tt(outT[rows, j, :], outT[rows, j, :], b[rows, :], ALU.add))

                added = []

                def compressed_probs(e):
                    if e == 0:
                        dve.wait_ge(*cmp_exp.at(l, 1))
                        link(l, v.tensor_reduce(cmx, cn, AX.X, ALU.add))
                    elif e == 1:
                        link(l, v.reciprocal(cmx, cmx))
                    elif e == 2:
                        link(l, tt(cn, cn, over(cmx, NCMP), ALU.mult))
                    elif e == 3:
                        link(l, tt(by_tile(cn), by_tile(cn), tile_mask("c01"), ALU.mult))
                    else:
                        tt(by_tile(cn), by_tile(cn), gates[:, :, :, 0].unsqueeze(3).broadcast_to([P, T, H, NCMP]),
                           ALU.mult).then_inc(cmp_probs.sem, 1)

                def scale_probs(n):
                    u, i = STEPS[n]
                    if n >= NSA_STEPS and u % 2 == 0:
                        return
                    p_ = prob_of(n)[:, 0:(i + 1) * P]
                    dve.wait_ge(*drained(l, ("sc", n)))
                    if n < NSA_STEPS:
                        v.reciprocal(rsum[:, n:n + 1], rsum[:, n:n + 1]).then_inc(sum_inverted.sem, 1)
                        return
                    link(l, v.reciprocal(rsum[:, n - 1:n + 1], rsum[:, n - 1:n + 1]))
                    link(l, ts(p_, p_, rsum[:, n:n + 1], neglam, ALU.mult, ALU.mult))
                    stt(out=p_, in0=prob_of(n - 1)[:, 0:(i + 1) * P], scalar=rsum[:, n - 1:n], in1=p_,
                        op0=ALU.mult, op1=ALU.add).then_inc(probs_combined.sem, 1)

                for n in range(len(STEPS) + LAG + 2):
                    if n < len(STEPS):
                        b = bank_of("sc", n)
                        v.tensor_reduce(nmax[:, n:n + 1], b[:, 0:(STEPS[n][1] + 1) * P], AX.X, ALU.max,
                                        negate=True).then_inc(row_max.sem, 1)
                        if n == NSA_STEPS // 2:
                            split_tok_lo(2)
                        if n == NSA_STEPS + 2 * T * (H - 1):
                            split_tok_lo(3)
                        for u, kind in turns_after(n):
                            if kind == "k":
                                drain_copy(stacked(u, kind)[0:stack_rows(u, kind), :], "tr", u, kind)
                        if n in range(4, 9):
                            compressed_probs(n - 4)
                        for key in COMPRESSED.get(n, []):
                            compressed(*key)
                    if 1 <= n <= len(STEPS):
                        scale_probs(n - 1)
                    if turned_after(n) is not None and drainer[("tp", n - LAG)] == "dve":
                        u, i = STEPS[n - LAG]
                        b = bank_of("tp", n - LAG)
                        drain(v.tensor_copy(probT[:, u % 2, 0:i + 1, i * P:(i + 1) * P],
                                            b[:, 0:(i + 1) * P].rearrange("p (n q) -> p n q", q=P)))
                    g, half = attends_after(n) or (0, 0)
                    if half and g < 2 * H:
                        r = HD * (g // 2 % 2)
                        add_out(slice(r, r + HD), g // 4, "pv", g)

                def sums_of_squares(dst, src, tmp, last):
                    for i in range(T):
                        ins = tt(tmp[:, i, :], src[:, i, :], src[:, i, :], ALU.mult)
                    link(l, ins)
                    for i in range(T):
                        ins = v.tensor_reduce(dst[:, i * H:(i + 1) * H], tmp[:, i, :].rearrange("p (h d) -> p h d", h=H),
                                              AX.X, ALU.add)
                    if last:
                        ins.then_inc(norm_sum.sem, 1)
                    else:
                        link(l, ins)

                def gain(dst, g):
                    for i in range(T):
                        d = dst[:, i, :].rearrange("p (h d) -> p h d", h=H)
                        ins = tt(d, d, g.unsqueeze(1).broadcast_to([P, H, HD]), ALU.mult)
                    return ins

                dve.wait_ge(*drained(l, ("pv", 3 * H - 1)))
                sums_of_squares(ssq[:, 0:16], dmix, tmpl, True)
                link(l, ts(prm[:, 128:192], prm[:, 128:192], prm[:, 265:266], None, ALU.mult))
                dve.wait_ge(*norm_std_ready.at(l, 1))
                link(l, v.reciprocal(rstd[:, 0:16], rstd[:, 0:16]))
                link(l, head_scale(dmix, dmix, rstd[:, 0:16]))
                gain(dmix, prm[:, 128:192]).then_inc(mix_ready.sem, 1)
                first = [0, 512, 896, 1152]
                for m in range(H * T):
                    h, j = m // T, T - 1 - m % T
                    w = SEQ - j * P
                    dve.wait_ge(*soft_ln.at(l, m + 1))
                    b = bank_of("z", h, j)
                    drain(stt(out=soft[:, h % 2, first[j]:first[j] + w], in0=b[:, 0:w], scalar=0.0,
                              in1=prob[:, m % 3, 0:w], op0=ALU.max, op1=ALU.add))
                    dve.wait_ge(*drained(l, ("z", h, j)))
                    d = soft[:, h % 2, first[j]:first[j] + P]
                    tt(d, d, const("sb01"), ALU.mult).then_inc(soft_ready.sem, 1)
                    if m % T == 2 and h + 1 < H:
                        drain_copy(stacked(UNITS + h + 1, "k"), "tr", UNITS + h + 1, "k")
                dve.wait_ge(*drained(l, ("gtok", T - 1, 1)))
                qk, squares = (x_.rearrange("p (n c) -> p n c", c=HD) for x_ in (qk_flat, squares_flat))
                link(l, tt(squares, qk, qk, ALU.mult))
                v.tensor_reduce(ssq, squares, AX.X, ALU.add).then_inc(norm_sum.sem, 1)
                b = bank_of("G")
                v.tensor_copy(gcol[:, 0:32], b[:, 0:32])
                drain(v.tensor_copy(gcol[0:64, 32:64], b[0:64, 32:64]))
                dve.wait_ge(*drained(l, ("G",)))
                ts(negG, gcol[:, 0:16], -1.0, None, ALU.mult)
                tt(expKd, gcol[:, 16:32], gcol[:, 0:16], ALU.subtract).then_inc(decays_in.sem, 1)
                dve.wait_ge(*norm_std_ready.at(l, 2))
                link(l, v.reciprocal(rstd, rstd))
                link(l, ts(rstd[:, 0:16], rstd[:, 0:16], HD ** -0.5, None, ALU.mult))
                dve.wait_ge(*decays_exp.at(l, 1))
                link(l, tt(betaG, beta, expG, ALU.mult))

                def scale_tile(dst, src, colmn, i):
                    return tt(dst[:, i, :].rearrange("p (h d) -> p h d", h=H),
                              src[:, i, :].rearrange("p (h d) -> p h d", h=H), over(colmn[:, i * H:(i + 1) * H], HD), ALU.mult)

                for i in range(T):
                    scale_tile(qtok, qtok, rstd[:, 0:16], i)
                    link(l, scale_tile(ktok, ktok, rstd[:, 16:32], i))
                    scale_tile(kb, ktok, beta, i)
                    scale_tile(qd, qtok, expG, i).then_inc(gdn_ready.sem, 1)
                for i in range(T):
                    b = bank_of("kbT", i)
                    drain(v.tensor_copy(kbTb[0:HD, :], b[0:HD, :]))
                    scale_tile(kbG, ktok, betaG, i)
                    scale_tile(vtok, vtok, beta, i)
                    ins = scale_tile(kd, ktok, expKd, i)
                    if i == T - 1:
                        ins.then_inc(gdn_scaled.sem, 1)
                    b = bank_of("KK", i)
                    dve.wait_ge(*drained(l, ("D", i)))
                    drain(tt(AT[:, i, :], b, Dm, ALU.mult))
                    b = bank_of("KQ", i)
                    drain(tt(intraT[:, i, :], b, Dm, ALU.mult))
                eye = ident.unsqueeze(1).broadcast_to([P, H, P])

                def by_head(x_):
                    return x_.rearrange("p (h c) -> p h c", h=H)

                for m in range(LEVELS * T + 1):
                    if m < T:
                        b = bank_of("X0", m)
                        drain(tt(by_head(X[:, m, :]), by_head(b), eye, ALU.add))
                        tt(by_head(XT[:, m, :]), by_head(NL[:, m % 2, :]), eye, ALU.add).then_inc(xt0_ready.sem, 1)
                    if m - 1 >= T:
                        lev, i = divmod(m - 1, T)
                        if lev < LEVELS - 1:
                            b = bank_of("X", lev, i)
                            drain(tt(X[:, i, :], X[:, i, :], b, ALU.add))
                        b = bank_of("XT", lev, i)
                        drain(tt(XT[:, i, :], XT[:, i, :], b, ALU.add))
                v.memset(states[0:HD, 0, :], 0.0).then_inc(states_clear.sem, 1)
                split_lo(l, 2, 0)
                for n in range(2 * T):
                    i, p = divmod(n, 2)
                    rows = slice(p * CH, (p + 1) * CH)
                    if n:
                        b = bank_of("ws", n)
                        drain(tt(u_new[rows, i, :], u_new[rows, i, :], b[rows, 0:256], ALU.subtract))
                    if n < 2 * T - 1:
                        b = bank_of("S", n)
                        if n == 0:
                            drain(v.tensor_copy(states[0:HD, 1, :], b[0:HD, 0:256]))
                        else:
                            drain(tt(states[0:HD, n + 1, :], sg[0:HD, :], b[0:HD, 0:256], ALU.add))
                        dve.wait_ge(*drained(l, ("S", n)))
                        if n < 2 * T - 2:
                            i2, p2 = divmod(n + 1, 2)
                            c = p2 * 16 + i2 * H
                            link(l, tt(sg[0:HD, :].rearrange("p (h d) -> p h d", h=H),
                                       states[0:HD, n + 1, :].rearrange("p (h d) -> p h d", h=H),
                                       over(gl[0:HD, c:c + H], HD), ALU.mult))
                    if n == 2:
                        dve.wait_ge(*outT_hi.at(l, 1))
                        tt(xTl[:, 4:8, :], outT, xTh[:, 4:8, :].bitcast(F32), ALU.subtract).then_inc(outT_lo.sem, 1)
                dve.wait_ge(*drained(l, ("o", T - 1)))
                sums_of_squares(ssq[:, 0:16], gmix, tiles(scratch[:, 4096:5120]), True)
                split_lo(l, 2, 1)
                dve.wait_ge(*norm_std_ready.at(l, 3))
                link(l, v.reciprocal(rstd[:, 0:16], rstd[:, 0:16]))
                link(l, head_scale(gmix, gmix, rstd[:, 0:16]))
                link(l, gain(gmix, prm[:, 192:256]))
                tt(gmix, gmix, siluz, ALU.mult).then_inc(mix_ready.sem, 1)
                for i in range(T):
                    dve.wait_ge(*mix_hi.at(l, i + 1))
                    s = slice(i * P, (i + 1) * P)
                    drain(tt(xTl[:, 0:4, s], bank(("mt", i)).rearrange("p (k t) -> p k t", k=4),
                             xTh[:, 0:4, s].bitcast(F32), ALU.subtract))
                split_lo(l, 2, 2)
                split_lo(l, 2, 3)
                for i in range(T):
                    add_and_count(l, i, 0, bank_of("wo", 0, i), drained_dve)
                split_lo(l, 3, 0)

                def tile(i):
                    add_and_count(l, i, 1, bank_of("wo", 1, i), drained_dve)
                    normalise(l, 1, i)

                tile_end(tile, lambda i: turned(l, 1, i))

            for i in range(T):
                turned(0, -1, i)
            with dve.Fori(0, DEPTH) as l:
                steps[0] = 0
                ffn(l, 0)
                mixer(l)
                ffn(l, 1)
                assert steps[0] == DVE_STEPS, ("DVE_STEPS", steps[0])

        @block.gpsimd
        def _(pool):
            g = nc.gpsimd
            steps = [0]
            pool.wait_ge(consts_cast.sem, 1)

            def link(l, ins):
                steps[0] += 1
                ins.then_inc(pool_done.sem, 1)
                pool.wait_ge(*pool_done.at(l, steps[0]))

            def load_norm(l, j):
                pool.sem_inc(waits_taken.sem, 1)
                for n, p_ in enumerate(a["ln"][j]):
                    g.dma_start(lnp[:, n, :], p_[bass.ds(l, 1), :].broadcast_to([P, DM])).then_inc(lnp_loaded.sem, 16)
                pool.wait_ge(*lnp_loaded.at(l, 32 * (j + 1)))

            def gain_rest(l, j):
                for i in range(T):
                    pool.wait_ge(*ln_scaled.at(l, T * j + i + 1))
                    xs = x_tok[:, i, LN_CUT:]
                    link(l, g.tensor_tensor(xs, xs, lnp[:, 0, LN_CUT:], ALU.mult))
                    g.tensor_tensor(xs, xs, lnp[:, 1, LN_CUT:], ALU.add).then_inc(x_rest_ready.sem, 1)
                pool.wait_ge(*x_rest_ready.at(l, T * (j + 1)))
                pool.wait_ge(*x_ready.at(l, T * (j + 1)))

            pool.sem_inc(x_rest_ready.sem, x_rest_ready.start)
            with pool.Fori(0, DEPTH) as l:
                steps[0] = 0
                pool.wait_ge(*x_ready.at(l, 0))
                at = 0
                for name, w in (("lam_q1", 32), ("lam_q2", 32), ("lam_k1", 32), ("lam_k2", 32), ("subln", 64),
                                ("gdn_g", 64), ("a_log", 4), ("dt", 4), ("lam0", 2)):
                    g.dma_start(prm[:, at:at + w], a[name][bass.ds(l, 1), :].broadcast_to([P, w])) \
                        .then_inc(params_loaded.sem, 16)
                    at += w
                g.dma_start(stage[0:24, :], a["conv_w"][l].rearrange("k (c p) -> (k c) p", p=P)) \
                    .then_inc(params_loaded.sem, 16)
                g.dma_start(stage[24:40, :], a["pe_k"][l].rearrange("(k r) d -> k (r d)", r=2)) \
                    .then_inc(params_loaded.sem, 16)
                g.dma_start(stage[40:56, :], a["pe_v"][l].rearrange("(k r) d -> k (r d)", r=2)) \
                    .then_inc(params_loaded.sem, 16)
                for s, name in enumerate(("cmp_k_w2", "cmp_v_w2")):
                    g.dma_start(w2[:, s], a[name][l].rearrange("(f p) d -> p f d", p=P)) \
                        .then_inc(params_loaded.sem, 16)
                pool.wait_ge(*params_loaded.at(l, 16 * PARAM_DMAS))
                load_norm(l, 0)
                gain_rest(l, 0)
                pool.wait_ge(*drained(l, ("proj", 28)))
                pool.wait_ge(*drained(l, ("proj", 29)))
                for i in range(T):
                    for c0, kind in ((C_DQ1, "q"), (C_DK1, "k")):
                        src = h_tok[:, i, c0:c0 + 256].rearrange("p (n a d) -> p n a d", n=8, a=2)
                        cos = const("dc" + kind)[:, i * 16:(i + 1) * 16].unsqueeze(1).unsqueeze(1)
                        sin = const("ds" + kind)[:, i * 32:(i + 1) * 32].rearrange("p (a d) -> p a d", a=2).unsqueeze(1)
                        t0 = ptmp[:, 0, :].rearrange("p (n a d) -> p n a d", n=8, a=2)
                        t1 = ptmp[:, 1, :].rearrange("p (n a d) -> p n a d", n=8, a=2)
                        g.tensor_tensor(t0, src, cos.broadcast_to([P, 8, 2, 16]), ALU.mult)
                        link(l, g.tensor_tensor(t1, src[:, :, ::-1, :], sin.broadcast_to([P, 8, 2, 16]), ALU.mult))
                        ins = g.tensor_tensor(src, t0, t1, ALU.add)
                        if i == T - 1 and kind == "k":
                            ins.then_inc(diff_rotated.sem, 1)
                        else:
                            link(l, ins)
                load_norm(l, 1)
                pool.wait_ge(*gates_ready.at(l, 1))
                for n in range(NSA_STEPS):
                    u, i = STEPS[n]
                    pool.wait_ge(*sum_inverted.at(l, n + 1))
                    p_, c = prob_of(n)[:, 0:(i + 1) * P], 12 * i + 3 * (u // 2) + 1 + u % 2
                    pool.sem_inc(waits_taken.sem, 1)
                    g.tensor_scalar(p_, p_, rsum[:, n:n + 1], gate[:, c:c + 1], ALU.mult, ALU.mult) \
                        .then_inc(probs_scaled.sem, 1)
                for m in range(LEVELS * T):
                    lev, i = divmod(m, T)
                    if m < T:
                        pool.wait_ge(*drained(l, ("KK", i)))
                    if m >= 2:
                        plev, pi = divmod(m - 2, T)
                        pool.wait_ge(*filled(l, ("X0", pi) if plev == 0 else ("T1", plev, pi)))
                        if plev == 0:
                            pool.wait_ge(*xt0_ready.at(l, pi + 1))
                    g.tensor_tensor(NL[:, m % 2, :].rearrange("p (h c) -> p h c", h=H),
                                    AT[:, i, :].rearrange("p (h c) -> p h c", h=H),
                                    mask(f"lev{lev}").unsqueeze(1).broadcast_to([P, H, P]), ALU.mult) \
                        .then_inc(level_ready.sem, 1)
                gain_rest(l, 1)
                load_norm(l, 2)
                gain_rest(l, 2)
                assert steps[0] == POOL_STEPS, ("POOL_STEPS", steps[0])


_OUT = (1, SEQ, DM)


def kernel(x, w_in, w_out, ffn1_w_gu, ffn1_w_down, ffn2_w_gu, ffn2_w_down,
           ln1_g, ln1_b, ln2_g, ln2_b, ln3_g, ln3_b,
           diff_lam_q1, diff_lam_k1, diff_lam_q2, diff_lam_k2, diff_subln_g,
           gdn_conv_w, gdn_a_log, gdn_dt_bias, gdn_norm_g,
           nsa_pe_k, nsa_pe_v, nsa_cmp_k_w1, nsa_cmp_k_w2, nsa_cmp_v_w1, nsa_cmp_v_w2):
    from concourse import bacc
    from concourse.bass_utils import run_bass_kernel_spmd

    tables, masks_, lam0 = constants()
    given = dict(x=x, w_in=w_in, w_out=w_out, gu1=ffn1_w_gu, down1=ffn1_w_down, gu2=ffn2_w_gu, down2=ffn2_w_down,
                 ln1_g=ln1_g, ln1_b=ln1_b, ln2_g=ln2_g, ln2_b=ln2_b, ln3_g=ln3_g, ln3_b=ln3_b,
                 lam_q1=diff_lam_q1, lam_k1=diff_lam_k1, lam_q2=diff_lam_q2, lam_k2=diff_lam_k2,
                 subln=diff_subln_g, conv_w=gdn_conv_w, a_log=gdn_a_log, dt=gdn_dt_bias, gdn_g=gdn_norm_g,
                 pe_k=nsa_pe_k, pe_v=nsa_pe_v, cmp_k_w1=nsa_cmp_k_w1, cmp_k_w2=nsa_cmp_k_w2,
                 cmp_v_w1=nsa_cmp_v_w1, cmp_v_w2=nsa_cmp_v_w2, consts=tables, masks=masks_, lam0=lam0)
    nc = bacc.Bacc("TRN2", target_bir_lowering=False, num_devices=1)
    arrays, aps = {}, {}
    for name, value in given.items():
        arrays[name + "_in"] = np.ascontiguousarray(value)
        aps[name] = nc.dram_tensor(name + "_in", arrays[name + "_in"].shape, F32, kind="ExternalInput").ap()
    aps["gu"] = (aps["gu1"], aps["gu2"])
    aps["down"] = (aps["down1"], aps["down2"])
    aps["ln"] = [(aps[f"ln{j}_g"], aps[f"ln{j}_b"]) for j in (1, 2, 3)]
    y = nc.dram_tensor("y_out", _OUT, F32, kind="ExternalOutput").ap()
    trunk_program(nc, aps, y)
    got = run_bass_kernel_spmd(nc, [arrays], core_ids=[0])
    return got.results[0]["y_out"]
```
